# Optimizing a Trainium2 kernel written in Bass

```python
import jax
import jax.numpy as jnp
from jax import lax
import numpy as np

D_MODEL = 1024
BATCH = 1
SEQ = 1024
DEPTH = 1
DEC_BATCH = 8
DEC_SEQ = 8
PAST_LEN = 8192
PAGE_SIZE = 128

N_MEM = 256
MEM_HEADS = 4
MEM_DH = D_MODEL // MEM_HEADS
RET_HEADS = 4
RET_W = D_MODEL // 2
RET_DV = RET_W // RET_HEADS
RET_DK = RET_DV // 2
RET_QK = RET_HEADS * RET_DK
RET_CHUNK = 128
ROPE_BASE = 10000.0
RWKV_N = 64
RWKV_W = D_MODEL - RET_W
RWKV_HEADS = RWKV_W // RWKV_N
LORA_W = 64
LORA_A = 64
LORA_G = 128
LNX_EPS = 64e-5
N_RET_COLS = 2 * RET_QK + 2 * RET_W
N_RWKV_COLS = 3 * RWKV_W + LORA_W + LORA_A + LORA_G
N_IN_COLS = N_RET_COLS + N_RWKV_COLS
N_GROUPS = 4
EXP_PER_GROUP = 8
N_EXPERTS = N_GROUPS * EXP_PER_GROUP
TOP_K = 2
D_EXPERT = D_MODEL // 2
MOE_BLOCK = 128
EPS = 1e-6

kernel_name = 'hymba_retnet_rwkv7_hmoe_step'

def rmsnorm(x, g):
    xf = x.astype(jnp.float32)
    y = xf * lax.rsqrt(jnp.mean(xf * xf, axis=-1, keepdims=True) + EPS)
    return (y * g.astype(jnp.float32)).astype(x.dtype)

def rotary(x, pos):
    half = x.shape[-1] // 2
    inv_freq = ROPE_BASE ** (-jnp.arange(half, dtype=jnp.float32) / half)
    ang = pos.astype(jnp.float32)[:, None] * inv_freq[None, :]
    cos = jnp.cos(ang)[None, :, None, :]
    sin = jnp.sin(ang)[None, :, None, :]
    xf = x.astype(jnp.float32)
    x1, x2 = xf[..., :half], xf[..., half:]
    return jnp.concatenate([x1 * cos - x2 * sin, x2 * cos + x1 * sin], axis=-1)

def retention(q, k, v, s0):
    B, T, H, _ = q.shape
    C = RET_CHUNK if T % RET_CHUNK == 0 else T
    n = T // C
    lg = jnp.log1p(-jnp.exp2(-5.0 - jnp.arange(H, dtype=jnp.float32)))
    idx = jnp.arange(C, dtype=jnp.float32)
    diff = idx[:, None] - idx[None, :]
    mask = jnp.where(diff[None] >= 0, jnp.exp(jnp.maximum(diff, 0.0)[None] * lg[:, None, None]), 0.0)
    q_dec = jnp.exp((idx[:, None] + 1.0) * lg[None, :])
    k_dec = jnp.exp((C - 1.0 - idx)[:, None] * lg[None, :])
    c_dec = jnp.exp(C * lg)

    def to_chunks(t):
        return t.astype(jnp.float32).reshape(B, n, C, H, t.shape[-1]).transpose(1, 0, 2, 3, 4)

    def step(S, inp):
        qc, kc, vc = inp
        att = jnp.einsum('bihd,bjhd->bhij', qc, kc) * mask[None]
        o = (jnp.einsum('bhij,bjhe->bihe', att, vc)
             + jnp.einsum('bihd,bhde->bihe', qc, S) * q_dec[None, :, :, None])
        S = S * c_dec[None, :, None, None] + jnp.einsum('bjhd,bjhe->bhde', kc * k_dec[None, :, :, None], vc)
        return S, o

    S, o = lax.scan(step, s0.astype(jnp.float32), (to_chunks(q), to_chunks(k), to_chunks(v)))
    return o.transpose(1, 0, 2, 3, 4).reshape(B, T, H, -1), S

def rwkv7_scan(r, w, k, v, a, b, s0):
    def step(S, inp):
        rt, wt, kt, vt, at, bt = inp
        sa = jnp.einsum('bhvk,bhk->bhv', S, at)
        S = S * wt[:, :, None, :] + sa[..., None] * bt[:, :, None, :] + vt[..., None] * kt[:, :, None, :]
        y = jnp.einsum('bhvk,bhk->bhv', S, rt)
        return S, y

    xs = tuple(t.transpose(1, 0, 2, 3) for t in (r, w, k, v, a, b))
    S, y = lax.scan(step, s0, xs)
    return y.transpose(1, 0, 2, 3), S

def token_mixers(xn, pos, s_ret, s_rwkv, s_shift, w_in, ret_gn, rwkv_mu, rwkv_w0, rwkv_w2, rwkv_a0,
                 rwkv_a2, rwkv_g2, rwkv_k_k, rwkv_k_a, rwkv_r_k, rwkv_lnx_w, rwkv_lnx_b, w_out):
    B, T, _ = xn.shape
    f32 = jnp.float32
    proj = xn @ w_in
    ret_p, rw_p = proj[..., :N_RET_COLS], proj[..., N_RET_COLS:]
    q, k, v, gate = jnp.split(ret_p, [RET_QK, 2 * RET_QK, 2 * RET_QK + RET_W], axis=-1)
    q = rotary(q.reshape(B, T, RET_HEADS, RET_DK), pos)
    k = rotary(k.reshape(B, T, RET_HEADS, RET_DK), pos) * (RET_DK ** -0.5)
    v = v.reshape(B, T, RET_HEADS, RET_DV)
    o_ret, s_ret_new = retention(q, k, v, s_ret)
    o_ret = o_ret * lax.rsqrt(jnp.mean(o_ret * o_ret, axis=-1, keepdims=True) + EPS)
    o_ret = o_ret.reshape(B, T, RET_W) * ret_gn.astype(f32) * jax.nn.silu(gate.astype(f32))
    prev = jnp.concatenate([s_shift[:, None, :].astype(rw_p.dtype), rw_p[:, :-1]], axis=1)
    rw_s = (rw_p + (prev - rw_p) * rwkv_mu).astype(f32)
    s_shift_new = rw_p[:, -1]
    r, kr, vr, hw, ha, hg = jnp.split(
        rw_s, [RWKV_W, 2 * RWKV_W, 3 * RWKV_W, 3 * RWKV_W + LORA_W, 3 * RWKV_W + LORA_W + LORA_A], axis=-1)
    wlog = -jax.nn.softplus(-(rwkv_w0 + jnp.tanh(hw) @ rwkv_w2)) - 0.5
    decay = jnp.exp(-jnp.exp(wlog))
    a = jax.nn.sigmoid(rwkv_a0 + ha @ rwkv_a2)
    g = jax.nn.sigmoid(hg) @ rwkv_g2

    def heads(t):
        return t.reshape(B, T, RWKV_HEADS, RWKV_N)

    kk = heads(kr * rwkv_k_k)
    kk = kk / jnp.maximum(jnp.sqrt(jnp.sum(kk * kk, axis=-1, keepdims=True)), 1e-12)
    kr = kr * (1.0 + (a - 1.0) * rwkv_k_a)
    r4, k4, v4, a4 = heads(r), heads(kr), heads(vr), heads(a)
    y, s_rwkv_new = rwkv7_scan(r4, heads(decay), k4, v4, -kk, kk * a4, s_rwkv.astype(f32))
    mean = jnp.mean(y, axis=-1, keepdims=True)
    var = jnp.mean((y - mean) ** 2, axis=-1, keepdims=True)
    y = ((y - mean) * lax.rsqrt(var + LNX_EPS)).reshape(B, T, RWKV_W) * rwkv_lnx_w + rwkv_lnx_b
    bonus = jnp.sum(r4 * k4 * rwkv_r_k, axis=-1, keepdims=True) * v4
    y = (y + bonus.reshape(B, T, RWKV_W)) * g
    o = jnp.concatenate([o_ret, y], axis=-1).astype(xn.dtype) @ w_out
    return (o.astype(xn.dtype), s_ret_new.astype(s_ret.dtype), s_rwkv_new.astype(s_rwkv.dtype),
            s_shift_new.astype(s_shift.dtype))

def memory_kv(mem, g_mem_kv, w_mk, w_mv):
    B, M, _ = mem.shape
    mn = rmsnorm(mem, g_mem_kv)
    return (mn @ w_mk).reshape(B, M, MEM_HEADS, MEM_DH), (mn @ w_mv).reshape(B, M, MEM_HEADS, MEM_DH)

def memory_attn(hn, mem_k, mem_v, w_mq, w_mo):
    B, T, _ = hn.shape
    f32 = jnp.float32
    q = (hn @ w_mq).reshape(B, T, MEM_HEADS, MEM_DH)
    s = jnp.einsum('bthd,bmhd->bhtm', q.astype(f32), mem_k.astype(f32)) * (MEM_DH ** -0.5)
    p = jax.nn.softmax(s, axis=-1)
    o = jnp.einsum('bhtm,bmhd->bthd', p, mem_v.astype(f32)).reshape(B, T, MEM_HEADS * MEM_DH)
    return o.astype(hn.dtype) @ w_mo

def hier_route(xf, w_gr, b_gr, w_er, b_er):
    f32 = jnp.float32
    x32 = xf.astype(f32)
    gl = x32 @ w_gr.astype(f32) + b_gr.astype(f32)
    pg = jax.nn.softmax(gl, axis=-1)
    gsel = jnp.argmax(gl, axis=-1)
    el = (x32 @ w_er.astype(f32) + b_er.astype(f32)).reshape(-1, N_GROUPS, EXP_PER_GROUP)
    el = jnp.take_along_axis(el, gsel[:, None, None], axis=1)[:, 0]
    top_p, top_i = lax.top_k(jax.nn.softmax(el, axis=-1), TOP_K)
    pg_sel = jnp.take_along_axis(pg, gsel[:, None], axis=1)
    comb = pg_sel * top_p / jnp.sum(top_p, axis=-1, keepdims=True)
    eid = (gsel[:, None] * EXP_PER_GROUP + top_i).astype(jnp.int32)
    return eid, comb

def routed_experts(xf, eid, comb, w_e_gate, w_e_up, w_e_down):
    T, D = xf.shape
    A = T * TOP_K
    blk = MOE_BLOCK
    n_blocks = -(-(A + N_EXPERTS * (blk - 1)) // blk)
    P = n_blocks * blk
    flat_e = eid.reshape(A)
    flat_t = jnp.arange(A, dtype=jnp.int32) // TOP_K
    order = jnp.argsort(flat_e)
    se, st = flat_e[order], flat_t[order]
    counts = jnp.bincount(flat_e, length=N_EXPERTS)
    starts = jnp.cumsum(counts) - counts
    pcounts = (counts + blk - 1) // blk * blk
    pends = jnp.cumsum(pcounts)
    pstarts = pends - pcounts
    dest = pstarts[se] + jnp.arange(A, dtype=jnp.int32) - starts[se]
    buf_tok = jnp.zeros((P,), jnp.int32).at[dest].set(st)
    blk_e = jnp.minimum(jnp.searchsorted(pends, jnp.arange(n_blocks) * blk, side='right'), N_EXPERTS - 1)
    xb = xf[buf_tok].reshape(n_blocks, blk, D)

    def expert_block(args):
        xblk, e = args
        h = jax.nn.silu(xblk @ w_e_gate[e]) * (xblk @ w_e_up[e])
        return h @ w_e_down[e]

    yb = lax.map(expert_block, (xb, blk_e)).reshape(P, D)
    contrib = yb[dest] * comb.reshape(A)[order][:, None].astype(yb.dtype)
    return jax.ops.segment_sum(contrib, st, num_segments=T)

def decoder_layer(x, pos, mem_k, mem_v, s_ret, s_rwkv, s_shift, g_mix, w_in, ret_gn, rwkv_mu, rwkv_w0,
                  rwkv_w2, rwkv_a0, rwkv_a2, rwkv_g2, rwkv_k_k, rwkv_k_a, rwkv_r_k, rwkv_lnx_w, rwkv_lnx_b,
                  w_out, g_mem_q, w_mq, w_mo, g_ffn, w_gr, b_gr, w_er, b_er, w_e_gate, w_e_up, w_e_down):
    B, T, D = x.shape
    mix, s_ret_new, s_rwkv_new, s_shift_new = token_mixers(
        rmsnorm(x, g_mix), pos, s_ret, s_rwkv, s_shift, w_in, ret_gn, rwkv_mu, rwkv_w0, rwkv_w2, rwkv_a0,
        rwkv_a2, rwkv_g2, rwkv_k_k, rwkv_k_a, rwkv_r_k, rwkv_lnx_w, rwkv_lnx_b, w_out)
    h = x + mix
    h = h + memory_attn(rmsnorm(h, g_mem_q), mem_k, mem_v, w_mq, w_mo).astype(h.dtype)
    hn = rmsnorm(h, g_ffn).reshape(B * T, D)
    eid, comb = hier_route(hn, w_gr, b_gr, w_er, b_er)
    h = h + routed_experts(hn, eid, comb, w_e_gate, w_e_up, w_e_down).reshape(B, T, D).astype(h.dtype)
    return h, s_ret_new, s_rwkv_new, s_shift_new

def setup_inputs(seed: int = 0) -> dict:
    key = jax.random.key(seed)
    ks = iter(jax.random.split(key, 64))
    L, D = DEPTH, D_MODEL

    def nrm(shape, scale):
        return scale * jax.random.normal(next(ks), shape, jnp.float32)

    def gain(shape):
        return 1.0 + 0.02 * jax.random.normal(next(ks), shape, jnp.float32)

    return {
        'x_prompt': nrm((BATCH, SEQ, D), 1.0),
        'x_sample': nrm((DEC_BATCH, DEC_SEQ, D), 1.0),
        'mem_prompt': nrm((BATCH, N_MEM, D), 1.0),
        'state_ret': nrm((L, DEC_BATCH, RET_HEADS, RET_DK, RET_DV), 0.1),
        'state_rwkv': nrm((L, DEC_BATCH, RWKV_HEADS, RWKV_N, RWKV_N), 0.1),
        'state_shift': nrm((L, DEC_BATCH, N_RWKV_COLS), 1.0),
        'cache_mem_k': nrm((L, DEC_BATCH, N_MEM, MEM_HEADS, MEM_DH), 1.0),
        'cache_mem_v': nrm((L, DEC_BATCH, N_MEM, MEM_HEADS, MEM_DH), 1.0),
        'g_mix': gain((L, D)),
        'w_in': nrm((L, D, N_IN_COLS), D ** -0.5),
        'ret_gn': gain((L, RET_W)),
        'rwkv_mu': jax.random.uniform(next(ks), (L, N_RWKV_COLS), jnp.float32),
        'rwkv_w0': -1.0 + nrm((L, RWKV_W), 0.5),
        'rwkv_w2': nrm((L, LORA_W, RWKV_W), 0.5 * LORA_W ** -0.5),
        'rwkv_a0': nrm((L, RWKV_W), 0.1),
        'rwkv_a2': nrm((L, LORA_A, RWKV_W), 0.5 * LORA_A ** -0.5),
        'rwkv_g2': nrm((L, LORA_G, RWKV_W), LORA_G ** -0.5),
        'rwkv_k_k': 0.85 + nrm((L, RWKV_W), 0.02),
        'rwkv_k_a': gain((L, RWKV_W)),
        'rwkv_r_k': nrm((L, RWKV_HEADS, RWKV_N), 0.1),
        'rwkv_lnx_w': gain((L, RWKV_W)),
        'rwkv_lnx_b': nrm((L, RWKV_W), 0.02),
        'w_out': nrm((L, D, D), D ** -0.5),
        'g_mem_q': gain((L, D)),
        'g_mem_kv': gain((L, D)),
        'w_mq': nrm((L, D, MEM_HEADS * MEM_DH), D ** -0.5),
        'w_mk': nrm((L, D, MEM_HEADS * MEM_DH), D ** -0.5),
        'w_mv': nrm((L, D, MEM_HEADS * MEM_DH), D ** -0.5),
        'w_mo': nrm((L, MEM_HEADS * MEM_DH, D), D ** -0.5),
        'g_ffn': gain((L, D)),
        'w_group_router': nrm((L, D, N_GROUPS), D ** -0.5),
        'b_group_router': nrm((L, N_GROUPS), 0.01),
        'w_expert_router': nrm((L, D, N_EXPERTS), D ** -0.5),
        'b_expert_router': nrm((L, N_EXPERTS), 0.01),
        'w_e_gate': nrm((L, N_EXPERTS, D, D_EXPERT), D ** -0.5),
        'w_e_up': nrm((L, N_EXPERTS, D, D_EXPERT), D ** -0.5),
        'w_e_down': nrm((L, N_EXPERTS, D_EXPERT, D), D_EXPERT ** -0.5),
        'g_final': gain((D,)),
    }

def reference(x_prompt, x_sample, mem_prompt, state_ret, state_rwkv, state_shift, cache_mem_k, cache_mem_v,
              g_mix, w_in, ret_gn, rwkv_mu, rwkv_w0, rwkv_w2, rwkv_a0, rwkv_a2, rwkv_g2, rwkv_k_k, rwkv_k_a,
              rwkv_r_k, rwkv_lnx_w, rwkv_lnx_b, w_out, g_mem_q, g_mem_kv, w_mq, w_mk, w_mv, w_mo, g_ffn,
              w_group_router, b_group_router, w_expert_router, b_expert_router, w_e_gate, w_e_up, w_e_down,
              g_final):
    Bp, Tp, _ = x_prompt.shape
    Ts = x_sample.shape[1]
    pos_p = jnp.arange(Tp, dtype=jnp.int32)
    pos_s = PAST_LEN + jnp.arange(Ts, dtype=jnp.int32)
    hp, hs = x_prompt, x_sample
    sr_p, sw_p, ss_p, mk_p, mv_p = [], [], [], [], []
    sr_s, sw_s, ss_s = [], [], []
    for l in range(DEPTH):
        lw = (g_mix[l], w_in[l], ret_gn[l], rwkv_mu[l], rwkv_w0[l], rwkv_w2[l], rwkv_a0[l], rwkv_a2[l],
              rwkv_g2[l], rwkv_k_k[l], rwkv_k_a[l], rwkv_r_k[l], rwkv_lnx_w[l], rwkv_lnx_b[l], w_out[l],
              g_mem_q[l], w_mq[l], w_mo[l], g_ffn[l], w_group_router[l], b_group_router[l],
              w_expert_router[l], b_expert_router[l], w_e_gate[l], w_e_up[l], w_e_down[l])
        mk, mv = memory_kv(mem_prompt, g_mem_kv[l], w_mk[l], w_mv[l])
        z_ret = jnp.zeros((Bp, RET_HEADS, RET_DK, RET_DV), jnp.float32)
        z_rwkv = jnp.zeros((Bp, RWKV_HEADS, RWKV_N, RWKV_N), jnp.float32)
        z_shift = jnp.zeros((Bp, N_RWKV_COLS), x_prompt.dtype)
        hp, a1, a2, a3 = decoder_layer(hp, pos_p, mk, mv, z_ret, z_rwkv, z_shift, *lw)
        sr_p.append(a1); sw_p.append(a2); ss_p.append(a3); mk_p.append(mk); mv_p.append(mv)
        hs, b1, b2, b3 = decoder_layer(hs, pos_s, cache_mem_k[l], cache_mem_v[l], state_ret[l],
                                       state_rwkv[l], state_shift[l], *lw)
        sr_s.append(b1); sw_s.append(b2); ss_s.append(b3)
    y_prompt = rmsnorm(hp, g_final)
    y_sample = rmsnorm(hs, g_final)
    return (y_prompt, y_sample, jnp.stack(sr_p), jnp.stack(sw_p), jnp.stack(ss_p), jnp.stack(mk_p),
            jnp.stack(mv_p), jnp.stack(sr_s), jnp.stack(sw_s), jnp.stack(ss_s))


_drawn_inputs = setup_inputs


def setup_inputs(seed=0):
    import zlib

    import numpy as np

    out = dict(_drawn_inputs(seed))
    spreads = {}
    factors = {'ret_gn': 3.559,
     'rwkv_k_k': 32.029,
     'rwkv_k_a': 2.827,
     'rwkv_lnx_w': 3.569,
     'rwkv_lnx_b': 3.087,
     'g_mem_q': 6.705,
     'g_mem_kv': 2.848,
     'b_group_router': 14.365,
     'b_expert_router': 11.412,
     'g_final': 7.411,
     'g_ffn': 8.0}
    for name, (base, spread) in spreads.items():
        noise = np.random.default_rng([zlib.crc32(name.encode()), seed]).standard_normal(out[name].shape)
        drawn = base * np.exp(spread * noise) if base else spread * noise
        out[name] = jnp.asarray(drawn.astype(out[name].dtype))
    for name, factor in factors.items():
        out[name] = (out[name] * factor).astype(out[name].dtype)
    return out
```

```python
from contextlib import ExitStack

import numpy as np

import concourse.bass as bass
from concourse import mybir

ALU = mybir.AluOpType
ACT = mybir.ActivationFunctionType
AX = mybir.AxisListType
F32 = mybir.dt.float32
I32 = mybir.dt.int32
U32 = mybir.dt.uint32

P = 128
D = 1024
KC = D // P
SEQ = 1024
DB, DS = 8, 8
NS = DB * DS
NT = SEQ // P
TILES = NT + 1
ROWS = TILES * P
PAST = 8192
NMEM, MH, MDH = 256, 4, 256
RH, RDK, RDV = 4, 64, 128
RQK, RW = RH * RDK, RH * RDV
WH, WN = 8, 64
WW = WH * WN
LW, LA, LG = 64, 64, 128
NRET = 2 * RQK + 2 * RW
NRW = 3 * WW + LW + LA + LG
NIN = NRET + NRW
NG, EPG = 4, 8
NE = NG * EPG
DE = 512
EPS = 1e-6
LNX_EPS = 64e-5
CH = 64
LEVELS = 6
CAP = P
A_MAX = 2 * (SEQ + NS)
NOVER = (A_MAX - 1) // P
NBLK = NE + NOVER
NMASK = 4 + LEVELS
LEVELS_S = 3
N_CONST = 18
PER_DVE = 42
PER_AT = 6


class Steps:

    def __init__(self, eng, sem, base=0):
        self.eng, self.sem, self.base, self.n = eng, sem, base, 0

    def __call__(self, ins):
        self.n += 1
        ins.then_inc(self.sem, 1)
        self.eng.wait_ge(self.sem, self.base + self.n)


def shape_constants():
    f = np.float32
    c = {}
    c["ident"] = np.eye(P, dtype=f)
    half = RDK // 2
    inv = (10000.0 ** (-np.arange(half, dtype=f) / f(half))).astype(f)
    pos = np.concatenate([np.arange(SEQ), PAST + np.arange(NS) % DS, np.zeros(ROWS - SEQ - NS)]).astype(f)
    ang = (pos[:, None] * inv[None, :]).astype(f)
    cos, sin = np.cos(ang).astype(f), np.sin(ang).astype(f)
    lg = np.log1p(-np.exp2(-5.0 - np.arange(RH)))
    step = np.concatenate([np.arange(SEQ) % P, np.arange(ROWS - SEQ) % DS]) + 1.0
    qdec = np.exp(step[:, None] * lg[None, :])
    kdec = np.exp(-step[:, None] * lg[None, :]) * RDK ** -0.5
    dec = np.concatenate([qdec, kdec], axis=1)
    c["rope"] = np.concatenate([(dec[:, :, None] * cos[:, None, :]).reshape(ROWS, -1),
                                (dec[:, :, None] * sin[:, None, :]).reshape(ROWS, -1)], axis=1).astype(f)
    c["cdec"] = np.stack([np.broadcast_to(np.repeat(np.exp(n * lg), RDV)[None], (RDK, RW)) for n in (P, DS)], 1).astype(f)
    s, t = np.arange(P)[:, None], np.arange(P)[None, :]
    for name, ch, rc in (("mask_p", CH, P), ("mask_s", DS, DS)):
        same = s // ch == t // ch
        strict, incl = same & (s < t), same & (s <= t)
        ret = (s // rc == t // rc) & (s <= t)
        lev = []
        for l in range(LEVELS):
            b = 2 ** l
            lev.append((s // (2 * b) == t // (2 * b)) & (s // b % 2 == 0) & (t // b % 2 == 1))
        c[name] = np.stack([strict, incl, ret, s < t] + lev, 1).astype(f)
    c["chunk_p"] = (s // CH == np.arange(DB)[None]).astype(f)
    c["chunk_s"] = (s // DS == np.arange(DB)[None]).astype(f)
    bt = (np.arange(NS)[None, None, :] // DS == np.arange(DB)[None, :, None])
    c["expand_k"] = np.broadcast_to(bt, (WN, DB, NS)).reshape(WN, -1).astype(f)
    c["expand_t"] = np.broadcast_to((np.arange(NS)[:, None, None] // DS == np.arange(DB)[None, :, None]),
                                    (NS, DB, RDV)).reshape(NS, -1).astype(f)
    row = np.arange(TILES)[None, :] * P + np.arange(P)[:, None]
    c["valid"] = (row < SEQ + NS).astype(f)
    c["token"] = row.astype(np.int32)
    cnt = np.concatenate([np.arange(NE) * CAP, np.arange(NE), np.arange(NOVER), EPG - np.arange(EPG),
                          CAP * (1.0 + np.arange(8))])
    c["count"] = np.broadcast_to(cnt[None], (P, cnt.size)).astype(f)
    return {k: np.ascontiguousarray(v) for k, v in c.items()}


class Core:

    def __init__(self, nc, ctx, dram):
        self.nc, self.ctx, self.dram, self.sems = nc, ctx, dram, {}

    def sem(self, name):
        if name not in self.sems:
            self.sems[name] = self.nc.alloc_semaphore(name=name)
        return self.sems[name]

    def end_phase(self):
        self.nc.clear_and_free_semaphores(list(self.sems.values()))
        self.nc.all_engine_barrier()
        self.sems = {}


def wide_row(ap, n):
    return ap.rearrange("(a n) -> a n", a=1).broadcast_to([P, n])


def phase_project(core, PS):
    nc, d, sem = core.nc, core.dram, core.sem
    NCH = -(-NIN // 512)
    cols = [(c * 512, min(512, NIN - c * 512)) for c in range(NCH)]
    with ExitStack() as ctx:
        sb = lambda n, s, t=F32: ctx.enter_context(nc.sbuf_tensor(n, s, t))
        w = sb("pj_w", [P, KC, NIN])
        x = sb("pj_x", [P, D])
        sq = sb("pj_sq", [P, D])
        xT = sb("pj_xT", [P, KC, P])
        g = sb("pj_g", [P, KC])
        ident = sb("pj_id", [P, P])
        out = sb("pj_out", [P, NIN])
        st = sb("pj_st", [P, 4])
        expo = sb("pj_expo", [P, 1])
        x_loaded, c_loaded = sem("pj_x_loaded"), sem("pj_c_loaded")
        w_loaded = [sem(f"pj_w_loaded{c}") for c in range(NCH)]
        ms, rstd, xn, tT, tR, pr, ev = [sem("pj_" + n) for n in
            ("ms_ready", "rstd_ready", "xn_ready", "transposed", "xT_ready", "projected", "evacuated")]
        stored, chain = [sem(f"pj_stored{c}") for c in range(NCH)], sem("pj_dve")
        with nc.Block() as block:
            @block.sync
            def _(sp):
                sp.dma_start(ident[:], d["ident"][:]).then_inc(c_loaded, 16)
                with nc.allow_non_contiguous_dma(reason="a gain by channel"):
                    sp.dma_start(g[:], d["g_mix"][0].rearrange("(c p) -> p c", p=P)).then_inc(c_loaded, 16)
                sp.dma_start(x[:], d["x"][0:P, :]).then_inc(x_loaded, 16)
                sp.dma_start(d["proj"][0:1, NRET:NIN], d["zero_row"][:]).then_inc(sem("pj_zero_stored"), 16)
                wv = d["w_in"][0].rearrange("(c p) n -> p c n", p=P)
                for c, (a, n) in enumerate(cols):
                    sp.dma_start(w[:, :, a:a + n], wv[:, :, a:a + n]).then_inc(w_loaded[c], 16)
                with sp.Fori(0, TILES) as i:
                    sp.wait_ge(tT, 2 * i + 2)
                    sp.dma_start(x[:], d["x"][bass.ds(i * P + P, P), :]).then_inc(x_loaded, 16)
                    for c, (a, n) in enumerate(cols):
                        sp.wait_ge(ev, NCH * i + NCH + c + 1)
                        sp.dma_start(d["proj"][bass.ds(i * P + 1, P), a:a + n], out[:, a:a + n]).then_inc(stored[c], 16)
                for c in range(NCH):
                    sp.wait_ge(stored[c], 16 * TILES)
                sp.wait_ge(x_loaded, 16 * (TILES + 1))
                sp.wait_ge(sem("pj_zero_stored"), 16)

            @block.vector
            def _(v):
                v.wait_ge(c_loaded, 32)
                PER = 1
                with v.Fori(0, TILES) as i:
                    lk = Steps(v, chain, i * PER)
                    v.wait_ge(x_loaded, 16 * i + 16)
                    lk(v.tensor_tensor_reduce(sq[:], x[:], x[:], 1.0, 0.0, ALU.mult, ALU.add, st[:, 0:1]))
                    v.tensor_scalar(st[:, 1:2], st[:, 0:1], 1.0 / D, EPS, ALU.mult, ALU.add).then_inc(ms, 1)
                    v.wait_ge(rstd, i + 1)
                    v.tensor_scalar(x[:], x[:], st[:, 2:3], None, ALU.mult).then_inc(xn, 1)
                    v.wait_ge(pr, NCH * i)
                    for b in range(2):
                        v.wait_ge(tT, 2 * i + b + 1)
                        v.tensor_tensor(xT[:, 4 * b:4 * b + 4, :], PS[:, b, :].rearrange("p (c t) -> p c t", c=4),
                                        g[:, 4 * b:4 * b + 4].unsqueeze(2).to_broadcast([P, 4, P]), ALU.mult).then_inc(tR, 1)
                    assert lk.n == PER

            @block.gpsimd
            def _(po):
                po.memset(expo[:], -0.5).then_inc(sem("pj_expo"), 1)
                po.wait_ge(sem("pj_expo"), 1)
                with po.Fori(0, TILES) as i:
                    po.wait_ge(ms, i + 1)
                    po.tensor_tensor(st[:, 2:3], st[:, 1:2], expo[:], ALU.pow).then_inc(rstd, 1)

            @block.tensor
            def _(pe):
                pe.wait_ge(c_loaded, 32)
                with pe.Fori(0, TILES) as i:
                    pe.wait_ge(xn, i + 1)
                    pe.wait_ge(ev, NCH * i + NCH)
                    for c in range(KC):
                        ins = pe.transpose(PS[:, c // 4, c % 4 * P:(c % 4 + 1) * P], x[:, c * P:(c + 1) * P], ident[:])
                        if c % 4 == 3:
                            ins.then_inc(tT, 1)
                    pe.wait_ge(tR, 2 * i + 2)
                    for c, (a, n) in enumerate(cols):
                        pe.wait_ge(w_loaded[c], 16)
                        pe.wait_ge(ev, NCH * i + c + 1)
                        bank = 1 + c
                        for k in range(KC):
                            ins = pe.matmul(PS[:, bank, 0:n], xT[:, k, :], w[:, k, a:a + n], start=k == 0, stop=k == KC - 1)
                        ins.then_inc(pr, 1)

            @block.scalar
            def _(act):
                act.sem_inc(ev, NCH)
                with act.Fori(0, TILES) as i:
                    for c, (a, n) in enumerate(cols):
                        act.wait_ge(pr, NCH * i + c + 1)
                        act.wait_ge(stored[c], 16 * i)
                        act.copy(out[:, a:a + n], PS[:, 1 + c, 0:n]).then_inc(ev, 1)


def phase_mixers(core, PS):
    nc, d, sem = core.nc, core.dram, core.sem
    OQ, OV, OG = 0, 2 * RQK, 2 * RQK + RW
    OR = NRET
    with ExitStack() as ctx:
        sb = lambda n, s, t=F32: ctx.enter_context(nc.sbuf_tensor("mx_" + n, s, t))
        pin, prev = sb("pin", [P, NIN]), sb("prev", [P, NRW])
        rope = sb("rope", [P, 2, 2 * RH, 32])
        mu = sb("mu", [P, NRW])
        names = ["rwkv_w0", "rwkv_a0", "rwkv_k_k", "rwkv_k_a", "rwkv_r_k", "rwkv_lnx_w", "rwkv_lnx_b", "ret_gn"]
        vec = sb("vec", [P, len(names), 512])
        V_ = {n: vec[:, j, :] for j, n in enumerate(names)}
        w2, a2, g2 = sb("w2", [LW, WW]), sb("a2", [LA, WW]), sb("g2", [LG, WW])
        ident = sb("ident", [P, P])
        masks = sb("masks", [P, NMASK, P])
        chunk = sb("chunk", [P, DB])
        cdec = sb("cdec", [RDK, 2, RW])
        expk, expt = sb("expk", [WN, DB, NS]), sb("expt", [NS, DB, RDV])
        expo = sb("expo", [P, 8])
        lora = sb("lora", [P, 256])
        loT, hgT = sb("loT", [64, 2, P]), sb("hgT", [P, P])
        sg = sb("sg", [P, 2, WW])
        lw = sb("lw", [P, WW])
        pinc, pinv, pexc = sb("pinc", [P, WW]), sb("pinv", [P, WW]), sb("pexc", [P, WW])
        gate = sb("gate", [P, WW])
        t0, kk = sb("t0", [P, WW]), sb("kk", [P, WW])
        kr, arbk = sb("kr", [P, WW]), sb("arbk", [P, 4, WW])
        st = sb("st", [P, 8, 8])
        T4 = sb("T4", [WN, WH, 4, P])
        M4 = sb("M4", [P, WH, 4, P])
        AL = sb("AL", [P, 2, 4, P])
        T, TT, X = sb("T", [P, 2, 4, P]), sb("TT", [P, 2, 4, P]), sb("X", [P, 2, 4, P])
        U = sb("U", [WN, WH, WN])
        pc = sb("pc", [WN, WH, DB])
        xs, sas = sb("xs", [P, WW]), sb("sas", [P, WW])
        y, o = sb("y", [P, WW]), sb("o", [P, D])
        qk, qkt = sb("qk", [P, 2 * RH, 64]), sb("qkt", [P, 2 * RH, 32])
        qkT = sb("qkT", [RDK, 2 * RH, P])
        att = sb("att", [P, RH, P])
        S = sb("S", [RDK, RH, RDV])
        Us = sb("Us", [WN, WH, DB, WN])
        Uv = M4[0:WN].rearrange("p h a t -> p (h a t)").rearrange("p (b h k) -> p b h k", b=DB, h=WH)
        Ss = T4[:].rearrange("p h a t -> p (h a t)").rearrange("p (b h e) -> p b h e", b=DB, h=RH)
        ex_k, ex_t = sb("ex_k", [WN, 2, 2, DB, NS]), sb("ex_t", [NS, 2, DB, RDV])
        ro, rt, rg = sb("ro", [P, RW]), sb("rt", [P, RW]), sb("rg", [P, RW])

        B = lambda b, *ix: PS[:, b, :] if not ix else PS[ix[0], b, ix[1]]
        heads = lambda ap, h=WH: ap.rearrange("p (h n) -> p h n", h=h)
        over = lambda ap, n: ap.unsqueeze(2).to_broadcast([ap.shape[0], ap.shape[1], n])
        rows = [slice(0, CH), slice(CH, P)]

        loaded, c_loaded, states = sem("mx_tile_loaded"), sem("mx_consts_loaded"), sem("mx_states_loaded")
        shift_rows = sem("mx_shift_rows_loaded")
        tile_done = sem("mx_tile_done")
        chain = {e: sem("mx_own_" + e) for e in ("dve", "act", "pool")}
        S_ = lambda n: sem("mx_" + n)

        ctx2 = ExitStack()
        with ctx2, nc.Block() as block:
            @block.sync
            def _(sp):
                n = 0
                with nc.allow_non_contiguous_dma(reason="small rows, once"):
                    for dst, src in [(mu[:], wide_row(d["rwkv_mu"][0], NRW)),
                                     *[(V_[x], wide_row(d[x][0] if x != "rwkv_r_k" else d[x][0].rearrange("h n -> (h n)"), 512)) for x in names],
                                     (w2[:], d["rwkv_w2"][0]), (a2[:], d["rwkv_a2"][0]), (g2[:], d["rwkv_g2"][0]),
                                     (ident[:], d["ident"]), (masks[:], d["mask_p"]), (chunk[:], d["chunk_p"]),
                                     (cdec[:], d["cdec"]), (expk[:].rearrange("p a b -> p (a b)"), d["expand_k"]),
                                     (expt[:].rearrange("p a b -> p (a b)"), d["expand_t"])]:
                        sp.dma_start(dst, src).then_inc(c_loaded, 16)
                        n += 1
                assert n == N_CONST

                def load(at, i):
                    sp.dma_start(pin[:], d["proj"][bass.ds(at + 1, P), :]).then_inc(loaded, 16)
                    sp.dma_start(prev[:], d["proj"][bass.ds(at, P), OR:NIN]).then_inc(loaded, 16)
                    sp.dma_start(rope[:].rearrange("p a b c -> p (a b c)"), d["rope"][bass.ds(at, P), :]).then_inc(loaded, 16)

                with sp.Fori(0, NT) as i:
                    sp.wait_ge(S_("store_ready"), i)
                    load(i * P, i)
                    sp.wait_ge(S_("store_ready"), i + 1)
                    sp.dma_start(d["mixed"][bass.ds(i * P, P), :], o[:]).then_inc(tile_done, 16)
                sp.dma_start(Uv, d["state_rwkv"][0].rearrange("b h v k -> v b h k")).then_inc(states, 16)
                sp.dma_start(Ss, d["state_ret"][0].rearrange("b h k e -> k b h e")).then_inc(states, 16)
                sp.dma_start(d["out_ret_p"].rearrange("h k e -> k h e"), S[:]).then_inc(S_("states_stored"), 16)
                sp.wait_ge(S_("U_turned"), 1)
                sp.dma_start(d["out_rwkv_p"].rearrange("h v k -> v h k"), xs[0:WN, :].rearrange("p (h n) -> p h n", h=WH)).then_inc(S_("states_stored"), 16)
                sp.dma_start(masks[:], d["mask_s"]).then_inc(c_loaded, 16)
                sp.dma_start(chunk[:], d["chunk_s"]).then_inc(c_loaded, 16)
                load(SEQ, NT)
                sp.wait_ge(loaded, 48 * (NT + 1))
                sp.dma_start(prev[0:NS:DS, :], d["state_shift"][0]).then_inc(shift_rows, 16)
                sp.wait_ge(S_("Ss_ready"), RH)
                sp.dma_start(d["out_ret_s"].rearrange("b h k e -> k b h e"), Ss).then_inc(S_("Ss_stored"), 16)
                sp.wait_ge(S_("store_ready"), NT + 1)
                sp.dma_start(d["mixed"][SEQ:SEQ + P, :], o[:]).then_inc(tile_done, 16)
                sp.dma_start(d["out_shift_p"], d["proj"][SEQ:SEQ + 1, OR:NIN]).then_inc(S_("states_stored"), 16)
                sp.dma_start(d["out_shift_s"], d["proj"][SEQ + 1:SEQ + 1 + NS, OR:NIN].rearrange("(b s) n -> b s n", s=DS)[:, DS - 1, :]).then_inc(S_("states_stored"), 16)
                sp.wait_ge(S_("Ss_stored"), 16)
                sp.wait_ge(S_("Us_turned"), WH)
                sp.dma_start(d["out_rwkv_s"].rearrange("b h v k -> v b h k"), Uv).then_inc(S_("states_stored"), 16)
                sp.wait_ge(S_("states_stored"), 80)
                sp.wait_ge(tile_done, 16 * TILES)

            def dve_prepare(v, i, lk):
                r, krr, vr = (pin[:, OR + j * WW:OR + (j + 1) * WW] for j in range(3))
                lk(v.tensor_tensor(prev[:], prev[:], pin[:, OR:NIN], ALU.subtract))
                lk(v.tensor_tensor(prev[:], prev[:], mu[:], ALU.mult))
                v.tensor_tensor(pin[:, OR:NIN], pin[:, OR:NIN], prev[:], ALU.add).then_inc(S_("shifted"), 1)
                v.wait_ge(S_("shifted"), i + 1)
                qin = pin[:, OQ:OV].rearrange("p (h n) -> p h n", n=64)
                lo, hi = qin[:, :, 0:32], qin[:, :, 32:64]
                cs, sn = rope[:, 0], rope[:, 1]
                lk(v.tensor_tensor(qk[:, :, 0:32], lo, cs, ALU.mult))
                lk(v.tensor_tensor(qkt[:], hi, sn, ALU.mult))
                lk(v.tensor_tensor(qk[:, :, 0:32], qk[:, :, 0:32], qkt[:], ALU.subtract))
                lk(v.tensor_tensor(qk[:, :, 32:64], hi, cs, ALU.mult))
                lk(v.tensor_tensor(qkt[:], lo, sn, ALU.mult))
                v.tensor_tensor(qk[:, :, 32:64], qk[:, :, 32:64], qkt[:], ALU.add).then_inc(S_("qk_ready"), 1)
                lk(v.tensor_tensor(kk[:], krr, V_["rwkv_k_k"], ALU.mult))
                lk(v.tensor_tensor(t0[:], kk[:], kk[:], ALU.mult))
                lk(v.tensor_reduce(st[:, 0, :], heads(t0[:]), AX.X, ALU.add))
                v.tensor_scalar(st[:, 1, :], st[:, 0, :], 1e-24, None, ALU.max).then_inc(S_("kk_sq"), 1)
                v.wait_ge(S_("lora_act"), i + 1)
                lk(v.tensor_scalar(lora[:, 128:256], lora[:, 128:256], 1.0, None, ALU.add))
                v.reciprocal(lora[:, 128:256], lora[:, 128:256]).then_inc(S_("lora_ready"), 1)
                v.wait_ge(S_("kk_rn"), i + 1)
                lk(v.tensor_tensor(heads(kk[:]), heads(kk[:]), over(st[:, 2, :], WN), ALU.mult))
                v.wait_ge(S_("loraT"), i + 1)
                v.tensor_copy(loT[:], B(0, slice(0, 64), slice(0, 256)).rearrange("p (a b) -> p a b", a=2))
                v.tensor_copy(hgT[:], B(0, slice(0, P), slice(256, 384))).then_inc(S_("loraT_ready"), 1)
                v.wait_ge(S_("rates"), i + 1)
                v.tensor_tensor(sg[:, 0, :], B(1), V_["rwkv_w0"], ALU.add)
                v.tensor_tensor(sg[:, 1, :], B(2), V_["rwkv_a0"], ALU.add).then_inc(S_("z_ready"), 1)
                v.wait_ge(S_("z_exp"), i + 1)
                lk(v.tensor_scalar(sg[:], sg[:], 1.0, None, ALU.add))
                lk(v.reciprocal(sg[:], sg[:]))
                v.tensor_scalar(lw[:], sg[:, 0, :], -float(np.exp(-0.5)), None, ALU.mult).then_inc(S_("lw_ready"), 1)
                lk(v.scalar_tensor_tensor(t0[:], sg[:, 1, :], -1.0, V_["rwkv_k_a"], ALU.add, ALU.mult))
                lk(v.scalar_tensor_tensor(kr[:], t0[:], 1.0, krr, ALU.add, ALU.mult))
                lk(v.tensor_tensor(t0[:], r, kr[:], ALU.mult))
                lk(v.tensor_tensor(t0[:], t0[:], V_["rwkv_r_k"], ALU.mult))
                lk(v.tensor_reduce(st[:, 3, :], heads(t0[:]), AX.X, ALU.add))
                lk(v.tensor_tensor(t0[:], kk[:], sg[:, 1, :], ALU.mult))
                v.wait_ge(S_("L_read"), i + 1)
                v.tensor_tensor(pexc[:], B(4), lw[:], ALU.subtract).then_inc(S_("lx_ready"), 1)
                v.wait_ge(S_("decays"), i + 1)
                v.scalar_tensor_tensor(arbk[:, 0, :], kk[:], -1.0, pexc[:], ALU.mult, ALU.mult)
                v.tensor_tensor(arbk[:, 1, :], r, pinc[:], ALU.mult)
                v.tensor_tensor(arbk[:, 2, :], t0[:], pinv[:], ALU.mult)
                v.tensor_tensor(arbk[:, 3, :], kr[:], pinv[:], ALU.mult).then_inc(S_("arbk_ready"), 1)

            def dve_retention(v, i, lk, sample):
                v.wait_ge(S_("qkT"), i + 1)
                for j in range(2):
                    ins = v.tensor_copy(qkT[:, 4 * j:4 * j + 4, :], B(6 + j, slice(0, RDK), slice(0, 512)).rearrange("p (a b) -> p a b", a=4))
                ins.then_inc(S_("qkT_ready"), 1)
                v.wait_ge(S_("att_done"), i + 1)
                v.tensor_tensor(att[:], B(5).rearrange("p (h t) -> p h t", h=RH),
                                masks[:, 2, :].unsqueeze(1).to_broadcast([P, RH, P]), ALU.mult).then_inc(S_("att_ready"), 1)
                if sample:
                    return
                v.wait_ge(S_("ret_done"), i + 1)
                lk(v.tensor_copy(ro[:], B(6)))
                lk(v.tensor_tensor(S[:].rearrange("p h e -> p (h e)"), S[:].rearrange("p h e -> p (h e)"), B(7, slice(0, RDK), slice(0, 512)), ALU.add))
                v.tensor_tensor(S[:].rearrange("p h e -> p (h e)"), S[:].rearrange("p h e -> p (h e)"), cdec[:, 0, :], ALU.mult).then_inc(S_("S_ready"), 1)

            def dve_matrices(v, i):
                for h in range(WH):
                    v.wait_ge(S_("headT"), WH * i + h + 1)
                    if h % 2 == 0:
                        v.tensor_copy(T4[:, h, :, :], B(h % 4, slice(0, WN), slice(0, 512)).rearrange("p (a b) -> p a b", a=4)).then_inc(S_("T4_ready_dve"), 1)
                for h in range(WH):
                    v.wait_ge(S_("products"), WH * i + h + 1)
                    src = B(4 + h % 4).rearrange("p (a b) -> p a b", a=4)
                    v.tensor_tensor(M4[:, h, 0:2, :], src[:, 0:2, :], masks[:, 0:2, :], ALU.mult)
                    v.tensor_tensor(M4[:, h, 2:4, :], src[:, 2:4, :], masks[:, 0:2, :], ALU.mult).then_inc(S_("M4_ready"), 1)

            def dve_inverse(v, i, levels, lk):
                NL = levels - 1
                inv = lambda n: S_(n)
                for g in range(2):
                    v.wait_ge(S_("AL_ready"), 2 * levels_before(i) + g + 1)
                    v.tensor_tensor(TT[:, g], AL[:, g], ident[:].unsqueeze(1).to_broadcast([P, 4, P]), ALU.add).then_inc(S_("TT_first"), 1)
                for l in range(1, levels):
                    for g in range(2):
                        n = 2 * updates_before(i) + 2 * (l - 1) + g
                        if l < levels - 1:
                            v.wait_ge(S_("dT"), 2 * grown_before(i) + 2 * (l - 1) + g + 1)
                            v.tensor_tensor(T[:, g], T[:, g], B(2 + g).rearrange("p (a b) -> p a b", a=4), ALU.add).then_inc(S_("T_ready"), 1)
                        v.wait_ge(S_("dTT"), n + 1)
                        v.tensor_tensor(TT[:, g], TT[:, g], B(4 + g).rearrange("p (a b) -> p a b", a=4), ALU.add).then_inc(S_("TT_ready"), 1)

            def dve_scan(v, i, lk):
                for c in range(2):
                    v.wait_ge(S_("U_products"), 2 * i + c + 1)
                    lk(v.tensor_tensor(U[:].rearrange("p h n -> p (h n)"), U[:].rearrange("p h n -> p (h n)"), B(1, slice(0, WN), slice(0, 512)), ALU.add))
                    v.tensor_tensor(U[:], U[:], pc[:, :, c:c + 1].to_broadcast([WN, WH, WN]), ALU.mult).then_inc(S_("U_ready"), 1)

            def dve_finish(v, i, lk):
                vr = pin[:, OR + 2 * WW:OR + 3 * WW]
                lk(v.tensor_reduce(st[:, 4, :], heads(B(0)), AX.X, ALU.add))
                lk(v.tensor_scalar(st[:, 4, :], st[:, 4, :], 1.0 / WN, None, ALU.mult))
                lk(v.tensor_tensor(heads(y[:]), heads(B(0)), over(st[:, 4, :], WN), ALU.subtract))
                lk(v.tensor_tensor(t0[:], y[:], y[:], ALU.mult))
                lk(v.tensor_reduce(st[:, 5, :], heads(t0[:]), AX.X, ALU.add))
                lk(v.tensor_scalar(st[:, 6, :], st[:, 5, :], 1.0 / WN, LNX_EPS, ALU.mult, ALU.add))
                lk(v.tensor_tensor(rt[:], ro[:], ro[:], ALU.mult))
                lk(v.tensor_reduce(st[:, 5, 0:RH], heads(rt[:], RH), AX.X, ALU.add))
                v.tensor_scalar(st[:, 0, 0:RH], st[:, 5, 0:RH], 1.0 / RDV, EPS, ALU.mult, ALU.add).then_inc(S_("norms"), 1)
                v.wait_ge(S_("gate_exp"), i + 1)
                lk(v.tensor_scalar(rg[:], rg[:], 1.0, None, ALU.add))
                lk(v.reciprocal(rg[:], rg[:]))
                lk(v.tensor_tensor(rg[:], rg[:], pin[:, OG:OG + RW], ALU.mult))
                lk(v.tensor_tensor(rg[:], rg[:], V_["ret_gn"], ALU.mult))
                v.wait_ge(S_("norm_r"), i + 1)
                lk(v.tensor_tensor(heads(y[:]), heads(y[:]), over(st[:, 7, :], WN), ALU.mult))
                lk(v.tensor_tensor(y[:], y[:], V_["rwkv_lnx_w"], ALU.mult))
                lk(v.tensor_tensor(y[:], y[:], V_["rwkv_lnx_b"], ALU.add))
                lk(v.tensor_tensor(heads(t0[:]), heads(vr), over(st[:, 3, :], WN), ALU.mult))
                lk(v.tensor_tensor(y[:], y[:], t0[:], ALU.add))
                lk(v.tensor_tensor(heads(rt[:], RH), heads(ro[:], RH), over(st[:, 2, 0:RH], RDV), ALU.mult))
                v.wait_ge(tile_done, 16 * i)
                v.tensor_tensor(o[:, RW:D], y[:], gate[:], ALU.mult)
                v.tensor_tensor(o[:, 0:RW], rt[:], rg[:], ALU.mult).then_inc(S_("store_ready"), 1)

            def dve_retention_sample(v, lk):
                for h in range(RH):
                    if h >= 2:
                        v.wait_ge(S_("ret_s_done"), h - 1)
                    v.tensor_tensor(ex_k[:, h % 2, 0], qkT[:, h, 0:NS].unsqueeze(1).to_broadcast([RDK, DB, NS]), expk[:], ALU.mult)
                    v.tensor_tensor(ex_t[:, h % 2], pin[0:NS, OV + h * RDV:OV + (h + 1) * RDV].unsqueeze(1).to_broadcast([NS, DB, RDV]),
                                    expt[:], ALU.mult).then_inc(S_("ret_ex"), 1)
                    if h >= 1:
                        ret_state(v, h - 1, lk)
                ret_state(v, RH - 1, lk)
                v.tensor_copy(ro[0:NS, :], B(6, slice(0, NS), slice(0, 512))).then_inc(S_("ro_s"), 1)
                v.wait_ge(S_("ro_s"), 1)

            def ret_state(v, h, lk):
                v.wait_ge(S_("ret_s_done"), h + 1)
                for j in range(2):
                    sv = Ss[:, 4 * j:4 * j + 4, h, :]
                    lk(v.tensor_tensor(sv, sv, B(2 * (h % 2) + j, slice(0, RDK), slice(0, 512)).rearrange("p (b e) -> p b e", b=4), ALU.add))
                v.tensor_scalar(Ss[:, :, h, :], Ss[:, :, h, :], float(np.exp(DS * np.log1p(-2.0 ** (-5.0 - h)))), None, ALU.mult).then_inc(S_("Ss_ready"), 1)

            def dve_scan_sample(v, lk):
                vr = pin[:, OR + 2 * WW:OR + 3 * WW]
                for h in range(WH):
                    if h >= 2:
                        v.wait_ge(S_("scan_s_x"), h - 1)
                    for j in range(2):
                        ins = v.tensor_tensor(ex_k[:, h % 2, j], T4[:, h, j, 0:NS].unsqueeze(1).to_broadcast([WN, DB, NS]), expk[:], ALU.mult)
                    ins.then_inc(S_("scan_ex_k"), 1)
                v.wait_ge(S_("sas_ready"), 2 * NT + 1)
                for h in range(WH):
                    hs = slice(h * WN, (h + 1) * WN)
                    if h >= 2:
                        v.wait_ge(S_("scan_s_u"), h - 1)
                    v.tensor_tensor(ex_t[:, h % 2, :, 0:WN], sas[0:NS, hs].unsqueeze(1).to_broadcast([NS, DB, WN]), expt[:, :, 0:WN], ALU.mult)
                    v.tensor_tensor(ex_t[:, h % 2, :, WN:2 * WN], vr[0:NS, hs].unsqueeze(1).to_broadcast([NS, DB, WN]), expt[:, :, 0:WN],
                                    ALU.mult).then_inc(S_("scan_ex_t"), 1)
                    if h >= 1:
                        u_state(v, h - 1, lk)
                u_state(v, WH - 1, lk)

            def u_state(v, h, lk):
                v.wait_ge(S_("scan_s_u"), h + 1)
                lk(v.tensor_tensor(Us[:, h], Us[:, h], B(1 + h % 2, slice(0, WN), slice(0, 512)).rearrange("p (b n) -> p b n", b=DB), ALU.add))
                v.tensor_tensor(Us[:, h], Us[:, h], over(pc[:, h, :], WN), ALU.mult).then_inc(S_("Us_ready"), 1)

            levels_before = lambda i: i * LEVELS
            updates_before = lambda i: i * (LEVELS - 1)
            grown_before = lambda i: i * (LEVELS - 2)

            @block.vector
            def _(v):
                v.memset(U[:], 0.0)
                v.memset(sas[:], 0.0)
                v.memset(S[:], 0.0).then_inc(S_("U_ready"), 1)
                v.wait_ge(S_("U_ready"), 1)
                v.sem_inc(S_("S_ready"), 1)
                v.wait_ge(c_loaded, 16 * N_CONST)
                with v.Fori(0, NT) as i:
                    lk = Steps(v, chain["dve"], i * PER_DVE)
                    v.wait_ge(loaded, 48 * i + 48)
                    dve_prepare(v, i, lk)
                    dve_retention(v, i, lk, False)
                    dve_matrices(v, i)
                    dve_inverse(v, i, LEVELS, lk)
                    dve_scan(v, i, lk)
                    dve_finish(v, i, lk)
                    assert lk.n == PER_DVE, lk.n
                lk = Steps(v, chain["dve"], NT * PER_DVE)
                v.wait_ge(c_loaded, 16 * (N_CONST + 2))
                v.wait_ge(loaded, 48 * (NT + 1))
                v.wait_ge(shift_rows, 16)
                v.wait_ge(states, 32)
                dve_prepare(v, NT, lk)
                dve_retention(v, NT, lk, True)
                dve_retention_sample(v, lk)
                v.wait_ge(S_("Ss_stored"), 16)
                v.wait_ge(S_("state_turned"), WH)
                dve_matrices(v, NT)
                dve_inverse(v, NT, LEVELS_S, lk)
                dve_scan_sample(v, lk)
                v.wait_ge(S_("y_s_done"), 1)
                dve_finish(v, NT, lk)

            @block.gpsimd
            def _(po):
                po.memset(expo[:], -0.5).then_inc(S_("expo"), 1)
                po.wait_ge(S_("expo"), 1)
                po.wait_ge(c_loaded, 16 * N_CONST)
                def body(i, levels):
                    po.wait_ge(S_("kk_sq"), i + 1)
                    po.tensor_tensor(st[:, 2, :], st[:, 1, :], expo[:], ALU.pow).then_inc(S_("kk_rn"), 1)
                    for l in range(levels):
                        for g in range(2):
                            if l == 0:
                                po.wait_ge(S_("M4_ready"), WH * i + 4 * g + 4)
                            if l == 1:
                                po.wait_ge(S_("TT_first"), 2 * i + g + 1)
                            if l >= 2:
                                po.wait_ge(S_("X_done"), 2 * updates_before(i) + 2 * (l - 2) + g + 1)
                            po.tensor_tensor(AL[:, g], M4[:, 4 * g:4 * g + 4, 0, :],
                                             masks[:, 4 + l, :].unsqueeze(1).to_broadcast([P, 4, P]), ALU.mult).then_inc(S_("AL_ready"), 1)
                    po.wait_ge(S_("norms"), i + 1)
                    po.tensor_tensor(st[:, 7, :], st[:, 6, :], expo[:], ALU.pow)
                    po.tensor_tensor(st[:, 2, 0:RH], st[:, 0, 0:RH], expo[:, 0:RH], ALU.pow).then_inc(S_("norm_r"), 1)
                with po.Fori(0, NT) as i:
                    body(i, LEVELS)
                po.wait_ge(c_loaded, 16 * (N_CONST + 2))
                body(NT, LEVELS_S)

            def act_prepare(act, i, nch):
                act.wait_ge(S_("shifted"), i + 1)
                hw = OR + 3 * WW
                act.activation(lora[:, 0:64], pin[:, hw:hw + 64], ACT.Tanh)
                act.copy(lora[:, 64:128], pin[:, hw + 64:hw + 128])
                act.activation(lora[:, 128:256], pin[:, hw + 128:hw + 256], ACT.Exp, scale=-1.0).then_inc(S_("lora_act"), 1)
                act.wait_ge(S_("rates"), i + 1)
                act.copy(gate[:], B(3))
                act.activation(rg[:], pin[:, OG:OG + RW], ACT.Exp, scale=-1.0).then_inc(S_("gate_exp"), 1)
                act.wait_ge(S_("z_ready"), i + 1)
                act.activation(sg[:], sg[:], ACT.Exp, scale=-1.0).then_inc(S_("z_exp"), 1)
                act.wait_ge(S_("L_ready"), i + 1)
                act.activation(pinc[:], B(4), ACT.Exp)
                act.activation(pinv[:], B(4), ACT.Exp, scale=-1.0).then_inc(S_("L_read"), 1)
                act.activation(pc[:, :, 0:nch], B(5, slice(0, WN), slice(0, WH * nch)).rearrange("p (h c) -> p h c", h=WH), ACT.Exp)
                act.wait_ge(S_("lx_ready"), i + 1)
                act.activation(pexc[:], pexc[:], ACT.Exp).then_inc(S_("decays"), 1)
                if nch == DB:
                    act.wait_ge(S_("Ss_stored"), 16)
                for h in range(1, WH, 2):
                    act.wait_ge(S_("headT"), WH * i + h + 1)
                    act.copy(T4[:, h, :, :], B(h % 4, slice(0, WN), slice(0, 512)).rearrange("p (a b) -> p a b", a=4)).then_inc(S_("T4_ready_act"), 1)

            def act_inverse(act, i, levels):
                for g in range(2):
                    act.wait_ge(S_("T_first"), 2 * i + g + 1)
                    act.copy(T[:, g], B(2 + g).rearrange("p (a b) -> p a b", a=4)).then_inc(S_("T2_ready"), 1)
                for l in range(1, levels):
                    for g in range(2):
                        n = 2 * updates_before(i) + 2 * (l - 1) + g
                        act.wait_ge(S_("X_done"), n + 1)
                        act.copy(X[:, g], B(g).rearrange("p (a b) -> p a b", a=4)).then_inc(S_("X_ready"), 1)

            @block.scalar
            def _(act):
                act.wait_ge(S_("U_ready"), 1)
                with act.Fori(0, NT) as i:
                    act_prepare(act, i, 2)
                    act_inverse(act, i, LEVELS)
                    for c in range(2):
                        act.wait_ge(S_("x_done"), 2 * i + c + 1)
                        act.copy(xs[rows[c], :], PS[rows[c], 6, :]).then_inc(S_("xs_ready"), 1)
                        act.wait_ge(S_("sa_done"), 2 * i + c + 1)
                        act.copy(sas[rows[c], :], PS[rows[c], 7, :]).then_inc(S_("sas_ready"), 1)
                act.wait_ge(S_("U_turns"), 1)
                act.copy(xs[0:WN, :], B(2, slice(0, WN), slice(0, 512))).then_inc(S_("U_turned"), 1)
                for h in range(WH):
                    act.wait_ge(S_("state_turns"), h + 1)
                    act.copy(Us[:, h], B(4 + h % 4, slice(0, WN), slice(0, 512)).rearrange("p (b n) -> p b n", b=DB)).then_inc(S_("state_turned"), 1)
                act_prepare(act, NT, DB)
                act_inverse(act, NT, LEVELS_S)
                act.wait_ge(S_("states_stored"), 32)
                act.wait_ge(S_("x_done"), 2 * NT + 1)
                act.copy(xs[0:NS, :], PS[0:NS, 6, :]).then_inc(S_("xs_ready"), 1)
                act.wait_ge(S_("sa_done"), 2 * NT + 1)
                act.copy(sas[0:NS, :], PS[0:NS, 7, :]).then_inc(S_("sas_ready"), 1)
                act.wait_ge(S_("y_s_done"), 1)
                for h in range(WH):
                    act.wait_ge(S_("back_turns"), h + 1)
                    act.copy(Uv[:, :, h, :], B(3 + h % 2, slice(0, WN), slice(0, 512)).rearrange("p (b n) -> p b n", b=DB)).then_inc(S_("Us_turned"), 1)

            def pe_prepare(pe, i, nch):
                pe.wait_ge(S_("qk_ready"), i + 1)
                pe.sem_inc(S_("passed"), 1)
                for j in range(2 * RH):
                    ins = pe.transpose(B(6 + j // 4, slice(0, RDK), slice(j % 4 * P, j % 4 * P + P)), qk[:, j, :], ident[:])
                ins.then_inc(S_("qkT"), 1)
                pe.wait_ge(S_("lora_ready"), i + 1)
                pe.sem_inc(S_("passed"), 1)
                for j in range(2):
                    pe.transpose(B(0, slice(0, 64), slice(j * P, (j + 1) * P)), lora[:, 64 * j:64 * j + 64], ident[:])
                pe.transpose(B(0, slice(0, P), slice(256, 384)), lora[:, 128:256], ident[:]).then_inc(S_("loraT"), 1)
                pe.wait_ge(S_("loraT_ready"), i + 1)
                pe.matmul(B(1), loT[:, 0, :], w2[:], start=True, stop=True)
                pe.matmul(B(2), loT[:, 1, :], a2[:], start=True, stop=True)
                pe.matmul(B(3), hgT[:], g2[:], start=True, stop=True).then_inc(S_("rates"), 1)
                pe.wait_ge(S_("lw_ready"), i + 1)
                pe.matmul(B(4), masks[:, 1, :], lw[:], start=True, stop=True)
                for h in range(WH):
                    ins = pe.matmul(B(5, slice(0, WN), slice(h * nch, (h + 1) * nch)), lw[:, h * WN:(h + 1) * WN], chunk[:, 0:nch], start=True, stop=True)
                ins.then_inc(S_("L_ready"), 1)

            def pe_attention(pe, i):
                pe.wait_ge(S_("decays"), i + 1)
                pe.wait_ge(S_("qkT_ready"), i + 1)
                for h in range(RH):
                    ins = pe.matmul(B(5, slice(0, P), slice(h * P, h * P + P)), qkT[:, RH + h, :], qkT[:, h, :], start=True, stop=True)
                ins.then_inc(S_("att_done"), 1)

            def pe_retention(pe, i):
                pe.wait_ge(S_("att_ready"), i + 1)
                pe.wait_ge(S_("S_ready"), i + 1)
                for h in range(RH):
                    vh = pin[:, OV + h * RDV:OV + (h + 1) * RDV]
                    pe.matmul(B(6, slice(0, P), slice(h * P, h * P + P)), att[:, h, :], vh, start=True, stop=False)
                    pe.matmul(B(6, slice(0, P), slice(h * P, h * P + P)), qkT[:, h, :], S[:, h, :], start=False, stop=True)
                    ins = pe.matmul(B(7, slice(0, RDK), slice(h * P, h * P + P)), qk[:, RH + h, :], vh, start=True, stop=True)
                ins.then_inc(S_("ret_done"), 1)

            def pe_matrices(pe, i):
                pe.wait_ge(S_("arbk_ready"), i + 1)
                pe.sem_inc(S_("passed"), 1)
                for h in range(WH):
                    if h >= 4:
                        pe.wait_ge(S_("T4_ready_act" if h % 2 else "T4_ready_dve"), 4 * i + (h - 4) // 2 + 1)
                        pe.sem_inc(S_("passed"), 1)
                    for j in range(4):
                        ins = pe.transpose(B(h % 4, slice(0, WN), slice(j * P, j * P + P)), arbk[:, j, h * WN:(h + 1) * WN], ident[:])
                    ins.then_inc(S_("headT"), 1)
                for h in range(WH):
                    pe.wait_ge(S_("T4_ready_act" if h % 2 else "T4_ready_dve"), 4 * i + h // 2 + 1)
                    if h == 0:
                        pe.wait_ge(S_("qkT_ready"), i + 1)
                    if h >= 4:
                        pe.wait_ge(S_("M4_ready"), WH * i + h - 3)
                    ar = T4[:, h, 0:2, :]
                    pe.matmul(B(4 + h % 4, slice(0, P), slice(0, 256)), T4[:, h, 2, :], ar, start=True, stop=True)
                    pe.matmul(B(4 + h % 4, slice(0, P), slice(256, 512)), T4[:, h, 3, :], ar, start=True, stop=True).then_inc(S_("products"), 1)

            def pe_inverse(pe, i, levels):
                for g in range(2):
                    pe.wait_ge(S_("TT_first"), 2 * i + g + 1)
                    for h in range(4):
                        ins = pe.transpose(B(2 + g, slice(0, P), slice(h * P, h * P + P)), TT[:, g, h, :], ident[:])
                    ins.then_inc(S_("T_first"), 1)
                for l in range(1, levels):
                    for g in range(2):
                        n = 2 * updates_before(i) + 2 * (l - 1) + g
                        pe.wait_ge(S_("AL_ready"), 2 * levels_before(i) + 2 * l + g + 1)
                        if l == 1:
                            pe.wait_ge(S_("T2_ready"), 2 * i + g + 1)
                        else:
                            pe.wait_ge(S_("T_ready"), 2 * grown_before(i) + 2 * (l - 2) + g + 1)
                        for h in range(4):
                            ins = pe.matmul(B(g, slice(0, P), slice(h * P, h * P + P)), AL[:, g, h, :], T[:, g, h, :], start=True, stop=True)
                        ins.then_inc(S_("X_done"), 1)
                    for g in range(2):
                        n = 2 * updates_before(i) + 2 * (l - 1) + g
                        pe.wait_ge(S_("X_ready"), n + 1)
                        if l > 1:
                            pe.wait_ge(S_("TT_ready"), n - 1)
                        if l < levels - 1:
                            for h in range(4):
                                ins = pe.matmul(B(2 + g, slice(0, P), slice(h * P, h * P + P)), TT[:, g, h, :], X[:, g, h, :], start=True, stop=True)
                            ins.then_inc(S_("dT"), 1)
                        for h in range(4):
                            ins = pe.matmul(B(4 + g, slice(0, P), slice(h * P, h * P + P)), X[:, g, h, :], TT[:, g, h, :], start=True, stop=True)
                        ins.then_inc(S_("dTT"), 1)

            def pe_scan(pe, i):
                pe.wait_ge(S_("TT_ready"), 2 * updates_before(i) + 2 * (LEVELS - 1))
                pe.wait_ge(S_("M4_ready"), WH * i + WH)
                for c in range(2):
                    r = rows[c]
                    hs = [slice(h * WN, (h + 1) * WN) for h in range(WH)]
                    pe.wait_ge(S_("U_ready"), 2 * i + c + 1)
                    pe.sem_inc(S_("passed"), 1)
                    for h in range(WH):
                        vh = pin[:, OR + 2 * WW + h * WN:OR + 2 * WW + (h + 1) * WN]
                        pe.matmul(PS[r, 6, hs[h]], M4[:, h, 2, r], vh, start=True, stop=False)
                        ins = pe.matmul(PS[r, 6, hs[h]], T4[:, h, 0, r], U[:, h, :], start=False, stop=True)
                    ins.then_inc(S_("x_done"), 1)
                    pe.wait_ge(S_("xs_ready"), 2 * i + c + 1)
                    pe.sem_inc(S_("passed"), 1)
                    for h in range(WH):
                        ins = pe.matmul(PS[r, 7, hs[h]], TT[r, h // 4, h % 4, r], xs[r, hs[h]], start=True, stop=True)
                    ins.then_inc(S_("sa_done"), 1)
                    pe.wait_ge(S_("sas_ready"), 2 * i + c + 1)
                    pe.sem_inc(S_("passed"), 1)
                    for h in range(WH):
                        vh = pin[r, OR + 2 * WW + h * WN:OR + 2 * WW + (h + 1) * WN]
                        pe.matmul(PS[0:WN, 1, hs[h]], arbk[r, 2, hs[h]], sas[r, hs[h]], start=True, stop=False)
                        pe.matmul(PS[0:WN, 1, hs[h]], arbk[r, 3, hs[h]], vh, start=False, stop=True)
                        vh = pin[:, OR + 2 * WW + h * WN:OR + 2 * WW + (h + 1) * WN]
                        pe.matmul(PS[r, 0, hs[h]], T4[:, h, 1, r], U[:, h, :], start=True, stop=False)
                        pe.matmul(PS[r, 0, hs[h]], M4[:, h, 1, r], sas[:, hs[h]], start=False, stop=False)
                        ins = pe.matmul(PS[r, 0, hs[h]], M4[:, h, 3, r], vh, start=False, stop=True)
                    ins.then_inc(S_("U_products"), 1)

            def turn_back(pe, h):
                pe.wait_ge(S_("Us_ready"), h + 1)
                if h >= 2:
                    pe.wait_ge(S_("Us_turned"), h - 1)
                for b in range(DB):
                    ins = pe.transpose(B(3 + h % 2, slice(0, WN), slice(b * WN, (b + 1) * WN)), Us[:, h, b, :], ident[0:WN, 0:WN])
                ins.then_inc(S_("back_turns"), 1)

            @block.tensor
            def _(pe):
                pe.wait_ge(c_loaded, 16 * N_CONST)
                with pe.Fori(0, NT) as i:
                    pe.wait_ge(loaded, 48 * i + 48)
                    pe_prepare(pe, i, 2)
                    pe_attention(pe, i)
                    pe_retention(pe, i)
                    pe.wait_ge(S_("S_ready"), i + 2)
                    pe.sem_inc(S_("passed"), 1)
                    pe_matrices(pe, i)
                    pe_inverse(pe, i, LEVELS)
                    pe_scan(pe, i)
                pe.wait_ge(S_("U_ready"), 2 * NT + 1)
                for h in range(WH):
                    ins = pe.transpose(B(2, slice(0, WN), slice(h * WN, (h + 1) * WN)), U[:, h, :], ident[0:WN, 0:WN])
                ins.then_inc(S_("U_turns"), 1)
                pe.wait_ge(states, 32)
                for h in range(WH):
                    if h >= 4:
                        pe.wait_ge(S_("state_turned"), h - 3)
                    for b in range(DB):
                        ins = pe.transpose(B(4 + h % 4, slice(0, WN), slice(b * WN, (b + 1) * WN)), Uv[:, b, h, :], ident[0:WN, 0:WN])
                    ins.then_inc(S_("state_turns"), 1)
                pe.wait_ge(S_("U_turned"), 1)
                pe.wait_ge(S_("state_turned"), WH)
                pe.wait_ge(c_loaded, 16 * (N_CONST + 2))
                pe.wait_ge(loaded, 48 * (NT + 1))
                pe_prepare(pe, NT, DB)
                pe_attention(pe, NT)
                pe.wait_ge(S_("att_ready"), NT + 1)
                for h in range(RH):
                    pe.wait_ge(S_("ret_ex"), h + 1)
                    if h >= 2:
                        pe.wait_ge(S_("Ss_ready"), h - 1)
                    col = slice(h * P, h * P + P)
                    pe.matmul(B(6, slice(0, NS), col), att[0:NS, h, 0:NS], pin[0:NS, OV + h * RDV:OV + (h + 1) * RDV], start=True, stop=False)
                    for b in range(DB):
                        pe.matmul(B(6, slice(0, NS), col), ex_k[:, h % 2, 0, b, :], Ss[:, b, h, :], start=False, stop=b == DB - 1)
                    for j in range(2):
                        ins = pe.matmul(B(2 * (h % 2) + j, slice(0, RDK), slice(0, 512)), qk[0:NS, RH + h, :],
                                        ex_t[:, h % 2, 4 * j:4 * j + 4, :], start=True, stop=True)
                    ins.then_inc(S_("ret_s_done"), 1)
                pe.wait_ge(S_("ro_s"), 1)
                pe_matrices(pe, NT)
                pe_inverse(pe, NT, LEVELS_S)
                hs = [slice(h * WN, (h + 1) * WN) for h in range(WH)]
                vh = [pin[0:NS, OR + 2 * WW + h * WN:OR + 2 * WW + (h + 1) * WN] for h in range(WH)]
                r = slice(0, NS)
                pe.wait_ge(S_("TT_ready"), 2 * updates_before(NT) + 2 * (LEVELS_S - 1))
                for h in range(WH):
                    pe.wait_ge(S_("scan_ex_k"), h + 1)
                    pe.matmul(PS[r, 6, hs[h]], M4[r, h, 2, r], vh[h], start=True, stop=False)
                    for b in range(DB):
                        pe.matmul(PS[r, 6, hs[h]], ex_k[:, h % 2, 0, b, :], Us[:, h, b, :], start=False, stop=b == DB - 1)
                    pe.matmul(PS[r, 0, hs[h]], M4[r, h, 3, r], vh[h], start=h == 0, stop=False, skip_group_check=True)
                    for b in range(DB):
                        ins = pe.matmul(PS[r, 0, hs[h]], ex_k[:, h % 2, 1, b, :], Us[:, h, b, :], start=False, stop=False, skip_group_check=True)
                    ins.then_inc(S_("scan_s_x" if h < WH - 1 else "x_done"), 1)
                pe.wait_ge(S_("xs_ready"), 2 * NT + 1)
                for h in range(WH):
                    ins = pe.matmul(PS[r, 7, hs[h]], TT[r, h // 4, h % 4, r], xs[r, hs[h]], start=True, stop=True)
                ins.then_inc(S_("sa_done"), 1)
                pe.wait_ge(S_("sas_ready"), 2 * NT + 1)
                for h in range(WH):
                    ins = pe.matmul(PS[r, 0, hs[h]], M4[r, h, 1, r], sas[r, hs[h]], start=False, stop=True, skip_group_check=True)
                ins.then_inc(S_("y_s_done"), 1)
                for h in range(WH):
                    pe.wait_ge(S_("scan_ex_t"), h + 1)
                    if h >= 2:
                        pe.wait_ge(S_("Us_ready"), h - 1)
                    bank = 1 + h % 2
                    pe.matmul(PS[0:WN, bank, :], arbk[r, 2, hs[h]], ex_t[:, h % 2, :, 0:WN], start=True, stop=False)
                    pe.matmul(PS[0:WN, bank, :], arbk[r, 3, hs[h]], ex_t[:, h % 2, :, WN:2 * WN], start=False, stop=True).then_inc(S_("scan_s_u"), 1)
                    if h >= 1:
                        turn_back(pe, h - 1)
                turn_back(pe, WH - 1)




def phase_memory_kv(core, PS, kT, Vm):
    nc, d, sem = core.nc, core.dram, core.sem
    MT = NMEM // P
    S_ = lambda n: sem("kv_" + n)
    with ExitStack() as ctx:
        sb = lambda n, s, t=F32: ctx.enter_context(nc.sbuf_tensor("kv_" + n, s, t))
        w = sb("w", [P, 2, KC, D])
        x, sq, xT = sb("x", [P, MT, D]), sb("sq", [P, D]), sb("xT", [P, MT, KC, P])
        g, ident, st, expo, kt = sb("g", [P, KC]), sb("ident", [P, P]), sb("st", [P, 8]), sb("expo", [P, MT]), sb("k", [P, MT, D])
        with nc.Block() as block:
            @block.sync
            def _(sp):
                sp.dma_start(x[:], d["mem_prompt"][0].rearrange("(m p) n -> p m n", p=P)).then_inc(S_("small"), 16)
                sp.dma_start(ident[:], d["ident"]).then_inc(S_("small"), 16)
                with nc.allow_non_contiguous_dma(reason="a gain by channel"):
                    sp.dma_start(g[:], d["g_mem_kv"][0].rearrange("(c p) -> p c", p=P)).then_inc(S_("small"), 16)
                for j, n in enumerate(("w_mk", "w_mv")):
                    wv = d[n][0].rearrange("(c p) n -> p c n", p=P)
                    for hf in range(2):
                        sp.dma_start(w[:, j, :, hf * 512:hf * 512 + 512], wv[:, :, hf * 512:hf * 512 + 512]).then_inc(S_(f"w{j}{hf}"), 16)
                sp.wait_ge(S_("k_ready"), 4)
                sp.dma_start(d["out_mk"].rearrange("(m p) n -> p m n", p=P), kt[:]).then_inc(S_("stored"), 16)
                sp.wait_ge(S_("v_ready"), 4)
                sp.dma_start(d["out_mv"].rearrange("(m p) n -> p m n", p=P), Vm[:]).then_inc(S_("stored"), 16)
                sp.wait_ge(S_("stored"), 32)

            @block.vector
            def _(v):
                lk = Steps(v, S_("dve"))
                v.wait_ge(S_("small"), 48)
                for m in range(MT):
                    lk(v.tensor_tensor_reduce(sq[:], x[:, m], x[:, m], 1.0, 0.0, ALU.mult, ALU.add, st[:, m:m + 1]))
                v.tensor_scalar(st[:, 2:4], st[:, 0:2], 1.0 / D, EPS, ALU.mult, ALU.add).then_inc(S_("ms"), 1)
                v.wait_ge(S_("rstd"), 1)
                for m in range(MT):
                    v.tensor_scalar(x[:, m], x[:, m], st[:, 4 + m:5 + m], None, ALU.mult).then_inc(S_("xn"), 1)
                for m in range(MT):
                    for b in range(2):
                        v.wait_ge(S_("turned"), 2 * m + b + 1)
                        v.tensor_tensor(xT[:, m, 4 * b:4 * b + 4, :], PS[:, 2 * m + b, :].rearrange("p (c t) -> p c t", c=4),
                                        g[:, 4 * b:4 * b + 4].unsqueeze(2).to_broadcast([P, 4, P]), ALU.mult).then_inc(S_("xT"), 1)
                for n in range(4):
                    v.wait_ge(S_("k_turned"), n + 1)
                    v.tensor_copy(kT[:, 4 * (n % 2):4 * (n % 2) + 4, (n // 2) * P:(n // 2) * P + P],
                                  PS[:, n, :].rearrange("p (c t) -> p c t", c=4)).then_inc(S_("kT"), 1)

            @block.gpsimd
            def _(po):
                po.memset(expo[:], -0.5).then_inc(S_("expo"), 1)
                po.wait_ge(S_("expo"), 1)
                po.wait_ge(S_("ms"), 1)
                po.tensor_tensor(st[:, 4:6], st[:, 2:4], expo[:], ALU.pow).then_inc(S_("rstd"), 1)

            @block.tensor
            def _(pe):
                for m in range(MT):
                    pe.wait_ge(S_("xn"), m + 1)
                    for c in range(KC):
                        ins = pe.transpose(PS[:, 2 * m + c // 4, c % 4 * P:c % 4 * P + P], x[:, m, c * P:(c + 1) * P], ident[:])
                        if c % 4 == 3:
                            ins.then_inc(S_("turned"), 1)
                for j in range(2):
                    for hf in range(2):
                        pe.wait_ge(S_(f"w{j}{hf}"), 16)
                        for m in range(MT):
                            pe.wait_ge(S_("xT"), 2 * m + 2)
                            if j == 1:
                                pe.wait_ge(S_("k_ready"), 2 * hf + m + 1)
                            for k in range(KC):
                                ins = pe.matmul(PS[:, 4 + 2 * hf + m, :], xT[:, m, k, :], w[:, j, k, hf * 512:hf * 512 + 512], start=k == 0, stop=k == KC - 1)
                            ins.then_inc(S_("projected"), 1)
                    if j == 0:
                        pe.wait_ge(S_("k_ready"), 4)
                        pe.wait_ge(S_("xT"), 4)
                        for m in range(MT):
                            for c in range(KC):
                                ins = pe.transpose(PS[:, 2 * m + c // 4, c % 4 * P:c % 4 * P + P], kt[:, m, c * P:(c + 1) * P], ident[:])
                                if c % 4 == 3:
                                    ins.then_inc(S_("k_turned"), 1)

            @block.scalar
            def _(act):
                for j in range(2):
                    for hf in range(2):
                        for m in range(MT):
                            act.wait_ge(S_("projected"), 4 * j + 2 * hf + m + 1)
                            dst = (kt, Vm)[j][:, m, hf * 512:hf * 512 + 512]
                            act.copy(dst, PS[:, 4 + 2 * hf + m, :]).then_inc(S_("k_ready" if j == 0 else "v_ready"), 1)


def phase_attention(core, PS, kT, Vm):
    nc, d, sem = core.nc, core.dram, core.sem
    S_ = lambda n: sem("at_" + n)
    NR = NG + NE
    SC = MDH ** -0.5
    with ExitStack() as ctx:
        sb = lambda n, s, t=F32: ctx.enter_context(nc.sbuf_tensor("at_" + n, s, t))
        w = sb("w", [P, 3, KC, D])
        wr = sb("wr", [P, KC, NR])
        br, gf = sb("br", [P, NR]), sb("gf", [P, D])
        g, ident, expo = sb("g", [P, KC]), sb("ident", [P, P]), sb("expo", [P, 1])
        mt, h, q = sb("mt", [P, D]), sb("h", [P, D]), sb("q", [P, D])
        sq = sb("sq", [P, D])
        aT, qT = sb("aT", [P, KC, P]), sb("qT", [P, KC, P])
        p, lg, st = sb("p", [P, MH, NMEM]), sb("lg", [P, NR]), sb("st", [P, 24])
        kc, kcT = sb("kc", [P, 2, 2, D]), sb("kcT", [P, KC, NMEM])
        sT = sb("sT", [P, 2, 256])
        flat = lambda ap: ap.rearrange("p c t -> p (c t)")
        two = lambda b: PS[:, b:b + 2, :].rearrange("p a (c t) -> p (a c) t", t=P)

        with nc.Block() as block:
            @block.sync
            def _(sp):
                def load(at):
                    sp.dma_start(h[:], d["x"][bass.ds(at, P), :]).then_inc(S_("loaded"), 16)
                    sp.dma_start(mt[:], d["mixed"][bass.ds(at, P), :]).then_inc(S_("loaded"), 16)

                with nc.allow_non_contiguous_dma(reason="small"):
                    for dst, src in [(ident[:], d["ident"]), (g[:], d["g_mem_q"][0].rearrange("(c p) -> p c", p=P)),
                                     (wr[:, :, 0:NG], d["w_group_router"][0].rearrange("(c p) n -> p c n", p=P)),
                                     (wr[:, :, NG:NR], d["w_expert_router"][0].rearrange("(c p) n -> p c n", p=P)),
                                     (br[:, 0:NG], wide_row(d["b_group_router"][0], NG)), (br[:, NG:NR], wide_row(d["b_expert_router"][0], NE)),
                                     (gf[:], wide_row(d["g_ffn"][0], D))]:
                        sp.dma_start(dst, src).then_inc(S_("small"), 16)
                for j, n in enumerate(("w_out", "w_mq", "w_mo")):
                    sp.dma_start(w[:, j], d[n][0].rearrange("(c p) n -> p c n", p=P)).then_inc(S_(f"w{j}"), 16)

                def stores(at, i):
                    sp.wait_ge(S_("h2_ready"), i + 1)
                    sp.dma_start(d["h2"][bass.ds(at, P), :], h[:]).then_inc(S_("h2_stored"), 16)
                    sp.wait_ge(S_("hn_ready"), i + 1)
                    sp.dma_start(d["hn"][bass.ds(at, P), :], mt[:]).then_inc(S_("hn_stored"), 16)
                    sp.wait_ge(S_("lg_ready"), i + 1)
                    sp.dma_start(d["logits"][bass.ds(at, P), :], lg[:]).then_inc(S_("lg_stored"), 16)

                with sp.Fori(0, NT) as i:
                    sp.wait_ge(S_("h2_stored"), 16 * i)
                    sp.wait_ge(S_("hn_stored"), 16 * i)
                    sp.wait_ge(S_("turned3"), i)
                    load(i * P)
                    stores(i * P, i)
                sp.wait_ge(S_("h2_stored"), 16 * NT)
                sp.wait_ge(S_("hn_stored"), 16 * NT)
                load(SEQ)
                for half, name in enumerate(("cache_mem_k", "cache_mem_v")):
                    for b in range(DB):
                        if half == 0 and b >= 2:
                            sp.wait_ge(S_("kc_turned"), b - 1)
                        if half == 1 and b < 2:
                            sp.wait_ge(S_("kc_turned"), DB - 1 + b)
                        if half == 1 and b >= 2:
                            sp.wait_ge(S_("cache_used"), b - 1)
                        sp.dma_start(kc[:, b % 2], d[name][0, b].rearrange("(m p) h n -> p m (h n)", p=P)).then_inc(S_(f"cache_loaded{b % 2}"), 16)
                stores(SEQ, NT)
                for n in ("h2_stored", "hn_stored", "lg_stored"):
                    sp.wait_ge(S_(n), 16 * TILES)

            def rms(v, i, src, k, lk):
                lk(v.tensor_tensor_reduce(sq[:], src, src, 1.0, 0.0, ALU.mult, ALU.add, st[:, 0:1]))
                v.tensor_scalar(st[:, 1:2], st[:, 0:1], 1.0 / D, EPS, ALU.mult, ALU.add).then_inc(S_("ms"), 1)
                v.wait_ge(S_("rstd"), 2 * i + k + 1)

            def dve_front(v, i, lk):
                v.wait_ge(S_("turned0"), i + 1)
                v.tensor_copy(aT[:], two(0)).then_inc(S_("aT0"), 1)
                v.wait_ge(S_("proj0"), i + 1)
                lk(v.tensor_tensor(h[:], h[:], PS[:, 2:4, :].rearrange("p a n -> p (a n)"), ALU.add))
                rms(v, i, h[:], 0, lk)
                v.tensor_scalar(mt[:], h[:], st[:, 2:3], None, ALU.mult).then_inc(S_("hq"), 1)
                v.wait_ge(S_("turned1"), i + 1)
                v.tensor_tensor(aT[:], two(0), g[:].unsqueeze(2).to_broadcast([P, KC, P]), ALU.mult).then_inc(S_("aT1"), 1)
                v.wait_ge(S_("turned2"), i + 1)
                v.tensor_copy(qT[:], two(0)).then_inc(S_("qT"), 1)

            def dve_softmax(v, i, lk, n, bank):
                v.wait_ge(S_("scores"), i + 1)
                src = PS[:, bank:bank + 2, :].rearrange("p a (b m) -> p (a b) m", m=NMEM)[:, 0:n, :]
                lk(v.tensor_reduce(st[:, 4:4 + n], src, AX.X, ALU.max))
                v.tensor_scalar(st[:, 8:8 + n], st[:, 4:4 + n], -SC, None, ALU.mult).then_inc(S_("nmax"), 1)
                v.wait_ge(S_("exps"), i + 1)
                lk(v.reciprocal(st[:, 16:16 + n], st[:, 12:12 + n]))
                v.tensor_tensor(p[:, 0:n, :], p[:, 0:n, :], st[:, 16:16 + n].unsqueeze(2).to_broadcast([P, n, NMEM]), ALU.mult).then_inc(S_("p_ready"), 1)

            def dve_attn(v, i, lk):
                dve_softmax(v, i, lk, MH, 4)
                v.wait_ge(S_("pT_done"), i + 1)
                v.tensor_copy(qT[:], two(0)).then_inc(S_("pT"), 1)
                v.wait_ge(S_("oT_done"), i + 1)
                v.tensor_copy(aT[:], two(2)).then_inc(S_("oT"), 1)

            def dve_attn_sample(v, lk):
                i = NT
                for b in range(DB):
                    v.wait_ge(S_("kc_turned"), b + 1)
                    if b:
                        v.wait_ge(S_("sT_done"), b)
                    v.tensor_copy(kcT[:].rearrange("p c (m t) -> p m c t", m=2),
                                  PS[:, 0:4, :].rearrange("p (m a) (c t) -> p m (a c) t", m=2, t=P)).then_inc(S_("kcT"), 1)
                v.wait_ge(S_("sT_done"), DB)
                v.tensor_copy(sT[:].rearrange("p m n -> p (m n)"), PS[:, 4, :]).then_inc(S_("sT"), 1)
                dve_softmax(v, i, lk, 2, 6)
                v.wait_ge(S_("pT_done"), i + 1)
                v.tensor_copy(sT[:].rearrange("p m n -> p (m n)"), PS[:, 0, :]).then_inc(S_("pT"), 1)
                v.wait_ge(S_("oT_done"), i + 1)
                v.tensor_copy(aT[:, :, 0:NS], PS[:, 2, :].rearrange("p (c t) -> p c t", c=KC)).then_inc(S_("oT"), 1)

            def dve_back(v, i, lk):
                v.wait_ge(S_("proj2"), i + 1)
                v.tensor_tensor(h[:], h[:], PS[:, 4:6, :].rearrange("p a n -> p (a n)"), ALU.add).then_inc(S_("h2_ready"), 1)
                v.wait_ge(S_("h2_ready"), i + 1)
                rms(v, i, h[:], 1, lk)
                lk(v.tensor_scalar(mt[:], h[:], st[:, 2:3], None, ALU.mult))
                v.tensor_tensor(mt[:], mt[:], gf[:], ALU.mult).then_inc(S_("hn_ready"), 1)
                v.wait_ge(S_("turned3"), i + 1)
                v.tensor_copy(aT[:], two(0)).then_inc(S_("aT3"), 1)
                v.wait_ge(S_("routed"), i + 1)
                v.wait_ge(S_("lg_stored"), 16 * i)
                v.tensor_tensor(lg[:], PS[:, 6, 0:NR], br[:], ALU.add).then_inc(S_("lg_ready"), 1)

            @block.vector
            def _(v):
                v.wait_ge(S_("small"), 16 * 7)
                with v.Fori(0, NT) as i:
                    lk = Steps(v, S_("dve"), i * PER_AT)
                    v.wait_ge(S_("loaded"), 32 * i + 32)
                    dve_front(v, i, lk)
                    dve_attn(v, i, lk)
                    dve_back(v, i, lk)
                    assert lk.n == PER_AT, lk.n
                lk = Steps(v, S_("dve"), NT * PER_AT)
                v.wait_ge(S_("loaded"), 32 * TILES)
                dve_front(v, NT, lk)
                dve_attn_sample(v, lk)
                dve_back(v, NT, lk)

            @block.gpsimd
            def _(po):
                po.memset(expo[:], -0.5).then_inc(S_("expo"), 1)
                po.wait_ge(S_("expo"), 1)
                with po.Fori(0, 2 * TILES) as i:
                    po.wait_ge(S_("ms"), i + 1)
                    po.tensor_tensor(st[:, 2:3], st[:, 1:2], expo[:], ALU.pow).then_inc(S_("rstd"), 1)

            @block.scalar
            def _(act):
                def body(i, n, bank):
                    act.wait_ge(S_("proj1"), i + 1)
                    act.copy(q[:], PS[:, 2:4, :].rearrange("p a n -> p (a n)")).then_inc(S_("q_ready"), 1)
                    act.wait_ge(S_("nmax"), i + 1)
                    for j in range(n):
                        ins = act.activation(p[:, j, :], PS[:, bank + j // 2, j % 2 * NMEM:(j % 2 + 1) * NMEM], ACT.Exp,
                                             bias=st[:, 8 + j:9 + j], scale=SC, accum_out=st[:, 12 + j:13 + j])
                    ins.then_inc(S_("exps"), 1)
                with act.Fori(0, NT) as i:
                    body(i, MH, 4)
                body(NT, 2, 6)

            def turn(pe, src, bank):
                for c in range(KC):
                    ins = pe.transpose(PS[:, bank + c // 4, c % 4 * P:c % 4 * P + P], src[:, c * P:(c + 1) * P], ident[:])
                return ins

            def project(pe, j, bank, src):
                for hf in range(2):
                    for k in range(KC):
                        ins = pe.matmul(PS[:, bank + hf, :], src[:, k, :], w[:, j, k, hf * 512:hf * 512 + 512], start=k == 0, stop=k == KC - 1)
                return ins

            def pe_front(pe, i):
                pe.wait_ge(S_("aT3"), i)
                turn(pe, mt, 0).then_inc(S_("turned0"), 1)
                pe.wait_ge(S_("aT0"), i + 1)
                pe.wait_ge(S_("w0"), 16)
                project(pe, 0, 2, aT).then_inc(S_("proj0"), 1)
                pe.wait_ge(S_("hq"), i + 1)
                turn(pe, mt, 0).then_inc(S_("turned1"), 1)
                pe.wait_ge(S_("aT1"), i + 1)
                pe.wait_ge(S_("w1"), 16)
                project(pe, 1, 2, aT).then_inc(S_("proj1"), 1)
                pe.wait_ge(S_("q_ready"), i + 1)
                turn(pe, q, 0).then_inc(S_("turned2"), 1)
                pe.wait_ge(S_("qT"), i + 1)

            def pe_attn(pe, i):
                for hd in range(MH):
                    for c in range(2):
                        ins = pe.matmul(PS[:, 4 + hd // 2, hd % 2 * NMEM:(hd % 2 + 1) * NMEM], qT[:, 2 * hd + c, :], kT[:, 2 * hd + c, :],
                                        start=c == 0, stop=c == 1)
                ins.then_inc(S_("scores"), 1)
                pe.wait_ge(S_("p_ready"), i + 1)
                turn(pe, p[:].rearrange("p h m -> p (h m)"), 0).then_inc(S_("pT_done"), 1)
                pe.wait_ge(S_("pT"), i + 1)
                for cc in range(KC):
                    for m in range(2):
                        ins = pe.matmul(PS[:, 2 + cc // 4, cc % 4 * P:cc % 4 * P + P], Vm[:, m, cc * P:(cc + 1) * P], qT[:, cc // 2 * 2 + m, :],
                                        start=m == 0, stop=m == 1)
                ins.then_inc(S_("oT_done"), 1)

            def pe_attn_sample(pe):
                i = NT
                for b in range(DB):
                    pe.wait_ge(S_(f"cache_loaded{b % 2}"), 16 * (b // 2 + 1))
                    pe.wait_ge(S_("kcT"), b)
                    for m in range(2):
                        ins = turn(pe, kc[:, b % 2, m], 2 * m)
                    ins.then_inc(S_("kc_turned"), 1)
                    pe.wait_ge(S_("kcT"), b + 1)
                    for m in range(2):
                        for hd in range(MH):
                            col = m * 256 + b * 32 + hd * 8
                            for c in range(2):
                                ins = pe.matmul(PS[:, 4, col:col + 8], kcT[:, 2 * hd + c, m * P:(m + 1) * P], qT[:, 2 * hd + c, b * DS:(b + 1) * DS],
                                                start=c == 0, stop=c == 1)
                    ins.then_inc(S_("sT_done"), 1)
                pe.wait_ge(S_("sT"), 1)
                for gq in range(2):
                    for m in range(2):
                        ins = pe.transpose(PS[:, 6, gq * NMEM + m * P:gq * NMEM + (m + 1) * P], sT[:, m, gq * P:(gq + 1) * P], ident[:])
                ins.then_inc(S_("scores"), 1)
                pe.wait_ge(S_("p_ready"), i + 1)
                for gq in range(2):
                    for m in range(2):
                        ins = pe.transpose(PS[:, 0, (gq * 2 + m) * P:(gq * 2 + m + 1) * P], p[:, gq, m * P:(m + 1) * P], ident[:])
                ins.then_inc(S_("pT_done"), 1)
                pe.wait_ge(S_("pT"), i + 1)
                pT = sT[:].rearrange("p m n -> p (m n)")
                for b in range(DB):
                    pe.wait_ge(S_(f"cache_loaded{b % 2}"), 16 * (DB // 2 + b // 2 + 1))
                    for cc in range(KC):
                        for m in range(2):
                            at = (b // 4 * 2 + m) * P + b % 4 * 32 + cc // 2 * 8
                            ins = pe.matmul(PS[:, 2, cc * NS + b * DS:cc * NS + (b + 1) * DS], kc[:, b % 2, m, cc * P:(cc + 1) * P], pT[:, at:at + 8],
                                            start=m == 0, stop=m == 1)
                    ins.then_inc(S_("cache_used" if b < DB - 1 else "oT_done"), 1)

            def pe_back(pe, i):
                pe.wait_ge(S_("oT"), i + 1)
                pe.wait_ge(S_("w2"), 16)
                project(pe, 2, 4, aT).then_inc(S_("proj2"), 1)
                pe.wait_ge(S_("hn_ready"), i + 1)
                turn(pe, mt, 0).then_inc(S_("turned3"), 1)
                pe.wait_ge(S_("aT3"), i + 1)
                pe.wait_ge(S_("lg_ready"), i)
                for k in range(KC):
                    ins = pe.matmul(PS[:, 6, 0:NR], aT[:, k, :], wr[:, k, :], start=k == 0, stop=k == KC - 1)
                ins.then_inc(S_("routed"), 1)

            @block.tensor
            def _(pe):
                pe.wait_ge(S_("small"), 16 * 7)
                with pe.Fori(0, NT) as i:
                    pe.wait_ge(S_("loaded"), 32 * i + 32)
                    pe_front(pe, i)
                    pe_attn(pe, i)
                    pe_back(pe, i)
                pe.wait_ge(S_("loaded"), 32 * TILES)
                pe_front(pe, NT)
                pe_attn_sample(pe)
                pe_back(pe, NT)


def phase_route(core, PS, dest, comb, slot_tok, over_info):
    nc, d, sem = core.nc, core.dram, core.sem
    S_ = lambda n: sem("rt_" + n)
    NR = NG + NE
    NCNT = 2 * NE + NOVER + EPG + 8
    with ExitStack() as ctx:
        sb = lambda n, s, t=F32: ctx.enter_context(nc.sbuf_tensor("rt_" + n, s, t))
        L, masks, ones, cnt_c = sb("L", [P, TILES, NR]), sb("strict", [P, P]), sb("ones", [P, P]), sb("cnt", [P, NCNT])
        valid, token, zero = sb("valid", [P, TILES]), sb("token", [P, TILES], I32), sb("zero", [P, NBLK], I32)
        s = sb("s", [P, 12, TILES])
        og, tg = sb("og", [P, TILES, NG]), sb("tg", [P, TILES, NG])
        sel, el, te = sb("sel", [P, TILES, EPG, NG]), sb("el", [P, TILES, EPG]), sb("te", [P, TILES, EPG])
        o1, o2 = sb("o1", [P, TILES, EPG]), sb("o2", [P, TILES, EPG])
        O = sb("O", [P, 2, TILES, NG, EPG])
        M = sb("M", [P, TILES, NE])
        a, b = sb("a", [P, TILES, NE]), sb("b", [P, TILES, NE])
        e32 = sb("e32", [P, 8, NE])
        nbt = sb("nbt", [P, NE, 8])
        own, own2 = sb("own", [P, NOVER, NE]), sb("own2", [P, NOVER, NE])
        df, of = sb("df", [P, 2, TILES]), sb("of", [P, NOVER + 1])
        ebase, eid, ovn, desc, full = (cnt_c[:, 0:NE], cnt_c[:, NE:2 * NE], cnt_c[:, 2 * NE:2 * NE + NOVER],
                                       cnt_c[:, 2 * NE + NOVER:2 * NE + NOVER + EPG], cnt_c[:, 2 * NE + NOVER + EPG:])
        bc = lambda ap, *shape: ap.to_broadcast([P, *shape])
        with nc.Block() as block:
            @block.sync
            def _(sp):
                with nc.allow_non_contiguous_dma(reason="small"):
                    sp.dma_start(L[:], d["logits"].rearrange("(t p) n -> p t n", p=P)).then_inc(S_("in"), 16)
                for dst, src in ((masks[:], d["mask_p"][:, 3, :]), (cnt_c[:], d["count"]), (valid[:], d["valid"]), (token[:], d["token"])):
                    sp.dma_start(dst, src).then_inc(S_("in"), 16)
                sp.dma_start(d["blocks"][NE * P:NBLK * P, :], d["zero_row"][0:1, 0:D].broadcast_to([NOVER * P, D])).then_inc(S_("cleared"), 16)
                sp.wait_ge(S_("cleared"), 16)

            @block.vector
            def _(v):
                lk = Steps(v, S_("dve"))
                tt, red = v.tensor_tensor, v.tensor_reduce
                v.memset(ones[:], 1.0).then_inc(S_("ones"), 1)
                v.wait_ge(S_("in"), 80)

                def pick(dst, src, best, t, n):
                    lk(red(best, src, AX.X, ALU.max))
                    lk(tt(t, src, bc(best.unsqueeze(2), TILES, n), ALU.is_equal))
                    lk(tt(t, t, bc(desc[:, 0:n].unsqueeze(1), TILES, n), ALU.mult))
                    lk(red(s[:, 11], t, AX.X, ALU.max))
                    lk(tt(dst, t, bc(s[:, 11].unsqueeze(2), TILES, n), ALU.is_equal))

                gl = L[:, :, 0:NG]
                pick(og[:], gl, s[:, 0], tg[:], NG)
                tt(tg[:], gl, bc(s[:, 0].unsqueeze(2), TILES, NG), ALU.subtract).then_inc(S_("g_shift"), 1)
                lk(tt(sel[:], L[:, :, NG:NR].rearrange("p t (g e) -> p t e g", g=NG), bc(og[:].unsqueeze(2), TILES, EPG, NG), ALU.mult))
                lk(red(el[:], sel[:], AX.X, ALU.add))
                pick(o1[:], el[:], s[:, 1], te[:], EPG)
                lk(v.scalar_tensor_tensor(el[:], o1[:], -1e30, el[:], ALU.mult, ALU.add))
                pick(o2[:], el[:], s[:, 2], te[:], EPG)
                tt(s[:, 3], s[:, 2], s[:, 1], ALU.subtract).then_inc(S_("e_shift"), 1)
                for k, o in enumerate((o1, o2)):
                    ins = tt(O[:, k], bc(og[:].unsqueeze(3), TILES, NG, EPG), bc(o[:].unsqueeze(2), TILES, NG, EPG), ALU.mult)
                lk(ins)
                O_ = lambda k: O[:, k].rearrange("p t g e -> p t (g e)")
                lk(tt(M[:], O_(0), O_(1), ALU.add))
                tt(M[:], M[:], bc(valid[:].unsqueeze(2), TILES, NE), ALU.mult).then_inc(S_("M_ready"), 1)
                v.wait_ge(S_("exps"), 1)
                lk(red(s[:, 5], tg[:], AX.X, ALU.add))
                lk(v.tensor_scalar(s[:, 6], s[:, 4], 1.0, None, ALU.add))
                lk(tt(s[:, 6], s[:, 6], s[:, 5], ALU.mult))
                lk(v.reciprocal(comb[:, 0], s[:, 6]))
                lk(tt(comb[:, 1], comb[:, 0], s[:, 4], ALU.mult))
                v.wait_ge(S_("ranks"), 1)
                cnt, nb, c0, c1, start, corr = (e32[:, j] for j in range(6))
                lk(v.tensor_copy(cnt, PS[:, 1, 0:NE]))
                lk(v.tensor_copy(b[:].rearrange("p t e -> p (t e)"), PS[:, 0, 0:TILES * NE]))
                lk(tt(nbt[:], bc(cnt.unsqueeze(2), NE, 8), bc(full.unsqueeze(1), NE, 8), ALU.is_gt))
                lk(red(nb, nbt[:], AX.X, ALU.add))
                lk(v.tensor_copy(c0, nb))
                step = 1
                while step < NE:
                    v.tensor_copy(c1[:, 0:step], c0[:, 0:step])
                    lk(tt(c1[:, step:NE], c0[:, step:NE], c0[:, 0:NE - step], ALU.add))
                    c0, c1, step = c1, c0, 2 * step
                lk(tt(start, c0, nb, ALU.subtract))
                lk(v.tensor_scalar(corr, start, float(CAP), float(NE * CAP - CAP), ALU.mult, ALU.add))
                lk(tt(corr, corr, ebase, ALU.subtract))
                lk(v.tensor_scalar(a[:], b[:], float(CAP), None, ALU.is_ge))
                lk(tt(a[:], a[:], bc(corr.unsqueeze(1), TILES, NE), ALU.mult))
                lk(tt(a[:], a[:], b[:], ALU.add))
                lk(tt(a[:], a[:], bc(ebase.unsqueeze(1), TILES, NE), ALU.add))
                for k in range(2):
                    lk(tt(b[:], a[:], O_(k), ALU.mult))
                    lk(red(df[:, k], b[:], AX.X, ALU.add))
                v.tensor_copy(dest[:], df[:]).then_inc(S_("dest"), 1)
                lk(tt(own[:], bc(start.unsqueeze(1), NOVER, NE), bc(ovn.unsqueeze(2), NOVER, NE), ALU.is_le))
                lk(tt(own2[:], bc(c0.unsqueeze(1), NOVER, NE), bc(ovn.unsqueeze(2), NOVER, NE), ALU.is_gt))
                lk(tt(own[:], own[:], own2[:], ALU.mult))
                lk(tt(own[:], own[:], bc(eid.unsqueeze(1), NOVER, NE), ALU.mult))
                lk(red(of[:, 0:NOVER], own[:], AX.X, ALU.add))
                lk(v.tensor_copy(of[:, NOVER:NOVER + 1], c0[:, NE - 1:NE]))
                lk(v.tensor_copy(over_info[:], of[:]))

            @block.scalar
            def _(act):
                act.wait_ge(S_("g_shift"), 1)
                act.activation(tg[:], tg[:], ACT.Exp)
                act.wait_ge(S_("e_shift"), 1)
                act.activation(s[:, 4], s[:, 3], ACT.Exp).then_inc(S_("exps"), 1)

            @block.tensor
            def _(pe):
                pe.wait_ge(S_("ones"), 1)
                pe.wait_ge(S_("M_ready"), 1)
                for t in range(TILES):
                    pe.matmul(PS[:, 0, t * NE:(t + 1) * NE], masks[:], M[:, t, :], start=True, stop=t == 0)
                    for j in range(t):
                        pe.matmul(PS[:, 0, t * NE:(t + 1) * NE], ones[:], M[:, j, :], start=False, stop=j == t - 1)
                for t in range(TILES):
                    ins = pe.matmul(PS[:, 1, 0:NE], ones[:], M[:, t, :], start=t == 0, stop=t == TILES - 1)
                ins.then_inc(S_("ranks"), 1)

            @block.gpsimd
            def _(po):
                po.memset(zero[:], 0).then_inc(S_("zero"), 1)
                po.wait_ge(S_("zero"), 1)
                po.dma_start(d["slots"].rearrange("(p n) o -> p (n o)", p=P), zero[:]).then_inc(S_("slots_zero"), 16)
                po.wait_ge(S_("slots_zero"), 16)
                po.wait_ge(S_("in"), 80)
                po.wait_ge(S_("dest"), 1)
                n = 0
                for k in range(2):
                    for t in range(TILES):
                        rows = P if t < NT else NS
                        po.indirect_dma_start(d["slots"], bass.IndirectOffsetOnAxis(ap=dest[0:rows, k, t:t + 1], axis=0),
                                              token[0:rows, t:t + 1], None).then_inc(S_("scattered"), 16)
                        n += 16
                po.wait_ge(S_("scattered"), n)
                with nc.allow_non_contiguous_dma(reason="a table turned"):
                    po.dma_start(slot_tok[:], d["slots"].rearrange("(b p) o -> p (b o)", p=P)).then_inc(S_("slots_in"), 16)
                po.wait_ge(S_("slots_in"), 16)


def phase_experts(core, PS, slot_tok, over_info):
    nc, d, sem = core.nc, core.dram, core.sem
    S_ = lambda n: sem("ex_" + n)
    HC = DE // P
    with ExitStack() as ctx:
        sb = lambda n, s, t=F32: ctx.enter_context(nc.sbuf_tensor("ex_" + n, s, t))
        wg, wu = sb("wg", [P, 2, KC, DE]), sb("wu", [P, 2, KC, DE])
        wd = sb("wd", [P, 2, HC, D])
        xg, xT = sb("xg", [P, 2, D]), sb("xT", [P, 2, KC, P])
        idx = sb("idx", [P, 2], I32)
        e, h, hT, y = sb("e", [P, 2, DE]), sb("h", [P, 2, DE]), sb("hT", [P, HC, P]), sb("y", [P, 2, D])
        ident = sb("ident", [P, P])
        GATE, UP, HT, OUT = 2, 3, 4, 5

        def weights(n, name):
            return d[name][0][bass.ds(n, 1)].rearrange("a (c p) m -> p (a c) m", p=P)

        def over_blocks(eng, body):
            n_over = eng.value_load(over_info[0:1, NOVER:NOVER + 1], min_val=0, max_val=NOVER)
            with eng.Fori(0, NOVER) as j:
                with eng.If(j < n_over):
                    body(j)

        def gate_up(pe, bf):
            for bank, w in ((GATE, wg), (UP, wu)):
                for k in range(KC):
                    ins = pe.matmul(PS[:, bank, :], xT[:, bf, k, :], w[:, bf, k, :], start=k == 0, stop=k == KC - 1)
            return ins

        def down(pe, bf):
            for hf in range(2):
                for k in range(HC):
                    ins = pe.matmul(PS[:, OUT + hf, :], hT[:, k, :], wd[:, bf, k, hf * 512:hf * 512 + 512], start=k == 0, stop=k == HC - 1)
            return ins

        def turn_rows(pe, bf):
            for c in range(KC):
                ins = pe.transpose(PS[:, c // 4, c % 4 * P:c % 4 * P + P], xg[:, bf, c * P:(c + 1) * P], ident[:])
            return ins

        def turn_h(pe, bf):
            for c in range(HC):
                ins = pe.transpose(PS[:, HT, c * P:(c + 1) * P], h[:, bf, c * P:(c + 1) * P], ident[:])
            return ins

        def silu_up(v, bf, lk):
            lk(v.tensor_scalar(e[:, bf], e[:, bf], 1.0, None, ALU.add))
            lk(v.reciprocal(e[:, bf], e[:, bf]))
            lk(v.tensor_tensor(e[:, bf], e[:, bf], PS[:, GATE, :], ALU.mult))
            return v.tensor_tensor(h[:, bf], e[:, bf], PS[:, UP, :], ALU.mult)

        rows_out = lambda: PS[:, OUT:OUT + 2, :].rearrange("p a n -> p (a n)")
        rows_in = lambda: PS[:, 0:2, :].rearrange("p a (c t) -> p (a c) t", t=P)

        with nc.Block() as block:
            @block.sync
            def _(sp):
                sp.dma_start(ident[:], d["ident"]).then_inc(S_("ident"), 16)

                def load(it, bf, n):
                    sp.wait_ge(S_(f"gu_used{bf}"), it)
                    sp.dma_start(wg[:, bf], weights(n, "w_e_gate")).then_inc(S_(f"wg{bf}"), 16)
                    sp.dma_start(wu[:, bf], weights(n, "w_e_up")).then_inc(S_(f"wu{bf}"), 16)
                    sp.wait_ge(S_(f"d_used{bf}"), it)
                    sp.dma_start(wd[:, bf], weights(n, "w_e_down")).then_inc(S_(f"wd{bf}"), 16)

                with sp.Fori(0, NE // 2) as it:
                    load(it, 0, 2 * it)
                    load(it, 1, 2 * it + 1)
                sp.wait_ge(S_("gu_used0"), NE // 2)
                sp.wait_ge(S_("d_used0"), NE // 2)

                def over(j):
                    n = sp.value_load(over_info[0:1, bass.ds(j, 1)], min_val=0, max_val=NE - 1)
                    sp.wait_ge(S_("ov_d"), j)
                    for dst, name in ((wg[:, 0], "w_e_gate"), (wu[:, 0], "w_e_up"), (wd[:, 0], "w_e_down")):
                        sp.dma_start(dst, weights(n, name)).then_inc(S_("ov_w"), 16)
                over_blocks(sp, over)

            @block.gpsimd
            def _(po):
                def gather(n, bf):
                    po.tensor_copy(idx[:, bf:bf + 1], slot_tok[:, bass.ds(n, 1)]).then_inc(S_("idx"), 1)
                    po.wait_ge(S_("idx"), n + 1)
                    po.sem_inc(S_("passed"), 1)
                    po.indirect_dma_start(xg[:, bf], None, d["hn"], bass.IndirectOffsetOnAxis(ap=idx[:, bf:bf + 1], axis=0)).then_inc(S_(f"rows{bf}"), 16)

                with po.Fori(0, NE // 2) as it:
                    for bf in range(2):
                        po.wait_ge(S_(f"rows_used{bf}"), it)
                        gather(2 * it + bf, bf)
                po.wait_ge(S_("rows_used0"), NE // 2)
                po.wait_ge(S_("rows0"), 16 * (NE // 2))

                def over(j):
                    po.wait_ge(S_("ov_turned"), j)
                    po.tensor_copy(idx[:, 0:1], slot_tok[:, bass.ds(j + NE, 1)]).then_inc(S_("ov_idx"), 1)
                    po.wait_ge(S_("ov_idx"), j + 1)
                    po.sem_inc(S_("passed"), 1)
                    po.indirect_dma_start(xg[:, 0], None, d["hn"], bass.IndirectOffsetOnAxis(ap=idx[:, 0:1], axis=0)).then_inc(S_("ov_rows"), 16)
                over_blocks(po, over)

            @block.tensor
            def _(pe):
                pe.wait_ge(S_("ident"), 16)

                def T(n, it, bf):
                    pe.wait_ge(S_(f"rows{bf}"), 16 * it + 16)
                    turn_rows(pe, bf).then_inc(S_(f"rows_used{bf}"), 1)

                def GU(n, it, bf):
                    pe.wait_ge(S_("xT"), n + 1)
                    pe.wait_ge(S_(f"wg{bf}"), 16 * it + 16)
                    pe.wait_ge(S_(f"wu{bf}"), 16 * it + 16)
                    pe.wait_ge(S_("h"), n)
                    gate_up(pe, bf).then_inc(S_(f"gu_used{bf}"), 1)

                def HT_(n, bf):
                    pe.wait_ge(S_("h"), n + 1)
                    turn_h(pe, bf).then_inc(S_("h_turned"), 1)

                def DN(n, it, bf):
                    pe.wait_ge(S_("hT"), n + 1)
                    pe.wait_ge(S_(f"wd{bf}"), 16 * it + 16)
                    pe.wait_ge(S_("y"), n)
                    down(pe, bf).then_inc(S_(f"d_used{bf}"), 1)

                T(0, 0, 0)
                GU(0, 0, 0)
                T(1, 0, 1)
                with pe.Fori(0, NE // 2 - 1) as it:
                    n = 2 * it + 1
                    GU(n, it, 1)
                    HT_(n - 1, 0)
                    T(n + 1, it + 1, 0)
                    DN(n - 1, it, 0)
                    GU(n + 1, it + 1, 0)
                    HT_(n, 1)
                    T(n + 2, it + 1, 1)
                    DN(n, it, 1)
                L = NE - 1
                GU(L, NE // 2 - 1, 1)
                HT_(L - 1, 0)
                DN(L - 1, NE // 2 - 1, 0)
                HT_(L, 1)
                DN(L, NE // 2 - 1, 1)

                def over(j):
                    pe.wait_ge(S_("ov_rows"), 16 * j + 16)
                    pe.wait_ge(S_("ov_h"), j)
                    turn_rows(pe, 0).then_inc(S_("ov_turned"), 1)
                    pe.wait_ge(S_("ov_xT"), j + 1)
                    pe.wait_ge(S_("ov_w"), 48 * j + 48)
                    gate_up(pe, 0).then_inc(S_("ov_gu"), 1)
                    pe.wait_ge(S_("ov_h"), j + 1)
                    turn_h(pe, 0).then_inc(S_("ov_ht"), 1)
                    pe.wait_ge(S_("ov_hT"), j + 1)
                    pe.wait_ge(S_("ov_y"), j)
                    down(pe, 0).then_inc(S_("ov_d"), 1)
                pe.wait_ge(S_("y"), NE)
                over_blocks(pe, over)

            @block.vector
            def _(v):
                def block_h(n, it, bf, lk):
                    v.wait_ge(S_("exp"), n + 1)
                    silu_up(v, bf, lk).then_inc(S_("h"), 1)

                def block_hT(n):
                    v.wait_ge(S_("h_turned"), n + 1)
                    v.tensor_copy(hT[:].rearrange("p c t -> p (c t)"), PS[:, HT, :]).then_inc(S_("hT"), 1)

                block_h(0, 0, 0, Steps(v, S_("dve"), 0))
                with v.Fori(0, NE // 2 - 1) as it:
                    n = 2 * it + 1
                    lk = Steps(v, S_("dve"), 6 * it + 3)
                    block_hT(n - 1)
                    block_h(n, it, 1, lk)
                    v.wait_ge(S_("d_used0"), it + 1)
                    block_hT(n)
                    block_h(n + 1, it + 1, 0, lk)
                    v.wait_ge(S_("d_used1"), it + 1)
                lk = Steps(v, S_("dve"), 6 * (NE // 2 - 1) + 3)
                block_hT(NE - 2)
                block_h(NE - 1, 0, 1, lk)
                v.wait_ge(S_("d_used0"), NE // 2)
                block_hT(NE - 1)

                def over(j):
                    lk = Steps(v, S_("ov_dve"), 3 * j)
                    v.wait_ge(S_("ov_exp"), j + 1)
                    silu_up(v, 0, lk).then_inc(S_("ov_h"), 1)
                    v.wait_ge(S_("ov_ht"), j + 1)
                    v.wait_ge(S_("ov_d"), j)
                    v.tensor_copy(hT[:].rearrange("p c t -> p (c t)"), PS[:, HT, :]).then_inc(S_("ov_hT"), 1)
                over_blocks(v, over)

            @block.scalar
            def _(act):
                def X(n, it, bf):
                    act.wait_ge(S_(f"rows_used{bf}"), it + 1)
                    act.copy(xT[:, bf], rows_in()).then_inc(S_("xT"), 1)

                def E(it, bf):
                    act.wait_ge(S_(f"gu_used{bf}"), it + 1)
                    act.activation(e[:, bf], PS[:, GATE, :], ACT.Exp, scale=-1.0).then_inc(S_("exp"), 1)

                def Y(n, it, bf):
                    act.wait_ge(S_(f"d_used{bf}"), it + 1)
                    act.wait_ge(S_(f"y_stored{bf}"), 16 * it)
                    act.copy(y[:, bf], rows_out()).then_inc(S_("y"), 1)
                    act.wait_ge(S_("y"), n + 1)
                    act.dma_start(d["blocks"][bass.ds(n * P, P), :], y[:, bf]).then_inc(S_(f"y_stored{bf}"), 16)

                X(0, 0, 0)
                E(0, 0)
                X(1, 0, 1)
                with act.Fori(0, NE // 2 - 1) as it:
                    n = 2 * it + 1
                    E(it, 1)
                    X(n + 1, it + 1, 0)
                    Y(n - 1, it, 0)
                    E(it + 1, 0)
                    X(n + 2, it + 1, 1)
                    Y(n, it, 1)
                E(NE // 2 - 1, 1)
                Y(NE - 2, NE // 2 - 1, 0)
                Y(NE - 1, NE // 2 - 1, 1)
                act.wait_ge(S_("y_stored0"), 16 * (NE // 2))
                act.wait_ge(S_("y_stored1"), 16 * (NE // 2))

                def over(j):
                    act.wait_ge(S_("ov_turned"), j + 1)
                    act.copy(xT[:, 0], rows_in()).then_inc(S_("ov_xT"), 1)
                    act.wait_ge(S_("ov_gu"), j + 1)
                    act.activation(e[:, 0], PS[:, GATE, :], ACT.Exp, scale=-1.0).then_inc(S_("ov_exp"), 1)
                    act.wait_ge(S_("ov_d"), j + 1)
                    act.copy(y[:, 0], rows_out()).then_inc(S_("ov_y"), 1)
                    act.wait_ge(S_("ov_y"), j + 1)
                    act.dma_start(d["blocks"][bass.ds(j * P + NE * P, P), :], y[:, 0]).then_inc(S_("ov_stored"), 16)
                    act.wait_ge(S_("ov_stored"), 16 * j + 16)
                    act.sem_inc(S_("ov_finished"), 1)
                over_blocks(act, over)


def phase_combine(core, PS, dest, comb):
    nc, d, sem = core.nc, core.dram, core.sem
    S_ = lambda n: sem("cb_" + n)
    with ExitStack() as ctx:
        sb = lambda n, s, t=F32: ctx.enter_context(nc.sbuf_tensor("cb_" + n, s, t))
        h, y1, y2, sq, o = sb("h", [P, TILES, D]), sb("y1", [P, TILES, D]), sb("y2", [P, TILES, D]), sb("sq", [P, D]), sb("o", [P, 2, D])
        gf, expo, st = sb("gf", [P, D]), sb("expo", [P, 1]), sb("st", [P, TILES, 4])
        rows = [P if t < NT else NS for t in range(TILES)]
        with nc.Block() as block:
            @block.sync
            def _(sp):
                sp.dma_start(gf[:], wide_row(d["g_final"], D)).then_inc(S_("g"), 16)
                for t in range(TILES):
                    sp.dma_start(h[:, t], d["h2"][t * P:(t + 1) * P, :]).then_inc(S_(f"h{t}"), 16)
                for t in range(TILES):
                    sp.wait_ge(S_("out"), t + 1)
                    dst = d["y_p"][t * P:(t + 1) * P, :] if t < NT else d["y_s"]
                    sp.dma_start(dst, o[0:rows[t], t % 2]).then_inc(S_(f"stored{t % 2}"), 16)
                sp.wait_ge(S_("stored0"), 16 * 5)
                sp.wait_ge(S_("stored1"), 16 * 4)

            @block.gpsimd
            def _(po):
                po.memset(expo[:], -0.5).then_inc(S_("expo"), 1)
                po.wait_ge(S_("expo"), 1)
                for t in range(TILES):
                    for k, y in enumerate((y1, y2)):
                        po.indirect_dma_start(y[0:rows[t], t], None, d["blocks"],
                                              bass.IndirectOffsetOnAxis(ap=dest[0:rows[t], k, t:t + 1], axis=0)).then_inc(S_(f"y{t}"), 16)
                for t in range(TILES):
                    po.wait_ge(S_("ms"), t + 1)
                    po.tensor_tensor(st[:, t, 2:3], st[:, t, 1:2], expo[:], ALU.pow).then_inc(S_("rstd"), 1)

            @block.vector
            def _(v):
                lk = Steps(v, S_("dve"))
                v.wait_ge(S_("g"), 16)
                v.memset(st[:], 1.0)
                for t in range(TILES):
                    r = slice(0, rows[t])
                    v.wait_ge(S_(f"h{t}"), 16)
                    v.wait_ge(S_(f"y{t}"), 32)
                    lk(v.scalar_tensor_tensor(h[r, t], y1[r, t], comb[r, 0, t:t + 1], h[r, t], ALU.mult, ALU.add))
                    lk(v.scalar_tensor_tensor(h[r, t], y2[r, t], comb[r, 1, t:t + 1], h[r, t], ALU.mult, ALU.add))
                    lk(v.tensor_tensor_reduce(sq[r], h[r, t], h[r, t], 1.0, 0.0, ALU.mult, ALU.add, st[r, t, 0:1]))
                    v.tensor_scalar(st[r, t, 1:2], st[r, t, 0:1], 1.0 / D, EPS, ALU.mult, ALU.add).then_inc(S_("ms"), 1)
                    v.wait_ge(S_("rstd"), t + 1)
                    if t >= 2:
                        v.wait_ge(S_(f"stored{t % 2}"), 16 * (t // 2))
                    lk(v.tensor_scalar(o[r, t % 2], h[r, t], st[r, t, 2:3], None, ALU.mult))
                    v.tensor_tensor(o[r, t % 2], o[r, t % 2], gf[r], ALU.mult).then_inc(S_("out"), 1)


def build(nc, dram):
    with ExitStack() as ctx:
        core = Core(nc, ctx, dram)
        PS = ctx.enter_context(nc.psum_tensor("banks", [P, 8, 512], F32))
        phase_project(core, PS)
        core.end_phase()
        phase_mixers(core, PS)
        core.end_phase()
        with ExitStack() as mem:
            kT = mem.enter_context(nc.sbuf_tensor("mem_kT", [P, KC, NMEM], F32))
            Vm = mem.enter_context(nc.sbuf_tensor("mem_v", [P, NMEM // P, D], F32))
            phase_memory_kv(core, PS, kT, Vm)
            core.end_phase()
            phase_attention(core, PS, kT, Vm)
            core.end_phase()
        sb = lambda n, s, t: ctx.enter_context(nc.sbuf_tensor("moe_" + n, s, t))
        dest, comb = sb("dest", [P, 2, TILES], I32), sb("comb", [P, 2, TILES], F32)
        slot_tok, over_info = sb("slot_tok", [P, NBLK], I32), sb("over_info", [P, NOVER + 1], I32)
        phase_route(core, PS, dest, comb, slot_tok, over_info)
        core.end_phase()
        phase_experts(core, PS, slot_tok, over_info)
        core.end_phase()
        phase_combine(core, PS, dest, comb)


SCRATCH = {"proj": ((ROWS + 8, NIN), F32), "mixed": ((ROWS, D), F32), "h2": ((ROWS, D), F32),
           "hn": ((ROWS, D), F32), "logits": ((ROWS, NG + NE), F32),
           "slots": ((NBLK * P, 1), I32), "blocks": ((NBLK * P, D), F32)}

INPUTS = ["w_in", "g_mix"]
OUTPUTS = [
    ("y_p", (SEQ, D)), ("y_s", (NS, D)),
    ("out_ret_p", (RH, RDK, RDV)), ("out_rwkv_p", (WH, WN, WN)), ("out_shift_p", (1, NRW)),
    ("out_ret_s", (DB, RH, RDK, RDV)), ("out_rwkv_s", (DB, WH, WN, WN)), ("out_shift_s", (DB, NRW)),
    ("out_mk", (NMEM, D)), ("out_mv", (NMEM, D)),
]


def program(nc, shapes):
    dram = {n: nc.dram_tensor(n, s, t, kind="ExternalInput").ap() for n, (s, t) in shapes.items()}
    for n, (s, t) in SCRATCH.items():
        dram[n] = nc.dram_tensor(n, s, t).ap()
    for n, s in OUTPUTS:
        dram[n] = nc.dram_tensor(n, s, F32, kind="ExternalOutput").ap()
    build(nc, dram)


def arrays_of(inputs):
    a = {k: np.ascontiguousarray(v) for k, v in inputs.items() if k not in ("x_prompt", "x_sample")}
    x = np.zeros((ROWS + P, D), np.float32)
    x[:SEQ] = inputs["x_prompt"][0]
    x[SEQ:SEQ + NS] = np.asarray(inputs["x_sample"]).reshape(NS, D)
    a["x"] = x
    a["zero_row"] = np.zeros((1, NRW), np.float32)
    a.update(shape_constants())
    return a


def kernel(**inputs):
    import concourse.bacc as bacc
    from concourse.bass_utils import run_bass_kernel_spmd

    arrays = arrays_of(inputs)
    nc = bacc.Bacc("TRN2", target_bir_lowering=False, num_devices=1)
    program(nc, {n: (a.shape, mybir.dt.from_np(a.dtype)) for n, a in arrays.items()})
    r = run_bass_kernel_spmd(nc, [arrays], core_ids=[0])
    got = r.results[0]
    order = [("y_p", (1, SEQ, D)), ("y_s", (DB, DS, D)), ("out_ret_p", (1, 1, RH, RDK, RDV)), ("out_rwkv_p", (1, 1, WH, WN, WN)),
             ("out_shift_p", (1, 1, NRW)), ("out_mk", (1, 1, NMEM, MH, MDH)), ("out_mv", (1, 1, NMEM, MH, MDH)),
             ("out_ret_s", (1, DB, RH, RDK, RDV)), ("out_rwkv_s", (1, DB, WH, WN, WN)), ("out_shift_s", (1, DB, NRW))]
    return tuple(got[n].reshape(s) for n, s in order)
```

```python
from contextlib import ExitStack

import numpy as np

import concourse.bass as bass
from concourse import mybir

ALU = mybir.AluOpType
ACT = mybir.ActivationFunctionType
AX = mybir.AxisListType
F32 = mybir.dt.float32
I32 = mybir.dt.int32
U32 = mybir.dt.uint32

P = 128
D = 1024
KC = D // P
SEQ = 1024
DB, DS = 8, 8
NS = DB * DS
NT = SEQ // P
TILES = NT + 1
ROWS = TILES * P
PAST = 8192
NMEM, MH, MDH = 256, 4, 256
RH, RDK, RDV = 4, 64, 128
RQK, RW = RH * RDK, RH * RDV
WH, WN = 8, 64
WW = WH * WN
LW, LA, LG = 64, 64, 128
NRET = 2 * RQK + 2 * RW
NRW = 3 * WW + LW + LA + LG
NIN = NRET + NRW
NG, EPG = 4, 8
NE = NG * EPG
DE = 512
EPS = 1e-6
LNX_EPS = 64e-5
CH = 64
LEVELS = 6
CAP = P
A_MAX = 2 * (SEQ + NS)
NOVER = (A_MAX - 1) // P
NBLK = NE + NOVER
NMASK = 4 + LEVELS
LEVELS_S = 3
N_CONST = 18
PER_PAIR = 35
PER_AT = 6


class Steps:

    def __init__(self, eng, sem, base=0):
        self.eng, self.sem, self.base, self.n = eng, sem, base, 0

    def __call__(self, ins):
        self.n += 1
        ins.then_inc(self.sem, 1)
        self.eng.wait_ge(self.sem, self.base + self.n)


def shape_constants():
    f = np.float32
    c = {}
    c["ident"] = np.eye(P, dtype=f)
    half = RDK // 2
    inv = (10000.0 ** (-np.arange(half, dtype=f) / f(half))).astype(f)
    pos = np.concatenate([np.arange(SEQ), PAST + np.arange(NS) % DS, np.zeros(ROWS - SEQ - NS)]).astype(f)
    ang = (pos[:, None] * inv[None, :]).astype(f)
    cos, sin = np.cos(ang).astype(f), np.sin(ang).astype(f)
    lg = np.log1p(-np.exp2(-5.0 - np.arange(RH)))
    step = np.concatenate([np.arange(SEQ) % P, np.arange(ROWS - SEQ) % DS]) + 1.0
    qdec = np.exp(step[:, None] * lg[None, :])
    kdec = np.exp(-step[:, None] * lg[None, :]) * RDK ** -0.5
    dec = np.concatenate([qdec, kdec], axis=1)
    c["rope"] = np.concatenate([(dec[:, :, None] * cos[:, None, :]).reshape(ROWS, -1),
                                (dec[:, :, None] * sin[:, None, :]).reshape(ROWS, -1)], axis=1).astype(f)
    c["cdec"] = np.stack([np.broadcast_to(np.repeat(np.exp(n * lg), RDV)[None], (RDK, RW)) for n in (P, DS)], 1).astype(f)
    s, t = np.arange(P)[:, None], np.arange(P)[None, :]
    for name, ch, rc in (("mask_p", CH, P), ("mask_s", DS, DS)):
        same = s // ch == t // ch
        strict, incl = same & (s < t), same & (s <= t)
        ret = (s // rc == t // rc) & (s <= t)
        lev = []
        for l in range(LEVELS):
            b = 2 ** l
            lev.append((s // (2 * b) == t // (2 * b)) & (s // b % 2 == 0) & (t // b % 2 == 1))
        c[name] = np.stack([strict, incl, ret, s < t] + lev, 1).astype(f)
    c["chunk_p"] = (s // CH == np.arange(DB)[None]).astype(f)
    c["chunk_s"] = (s // DS == np.arange(DB)[None]).astype(f)
    bt = (np.arange(NS)[None, None, :] // DS == np.arange(DB)[None, :, None])
    c["expand_k"] = np.broadcast_to(bt, (WN, DB, NS)).reshape(WN, -1).astype(f)
    c["expand_t"] = np.broadcast_to((np.arange(NS)[:, None, None] // DS == np.arange(DB)[None, :, None]),
                                    (NS, DB, RDV)).reshape(NS, -1).astype(f)
    row = np.arange(TILES)[None, :] * P + np.arange(P)[:, None]
    c["valid"] = (row < SEQ + NS).astype(f)
    c["token"] = row.astype(np.int32)
    cnt = np.concatenate([np.arange(NE) * CAP, np.arange(NE), np.arange(NOVER), EPG - np.arange(EPG),
                          CAP * (1.0 + np.arange(8))])
    c["count"] = np.broadcast_to(cnt[None], (P, cnt.size)).astype(f)
    return {k: np.ascontiguousarray(v) for k, v in c.items()}


class Core:

    def __init__(self, nc, ctx, dram):
        self.nc, self.ctx, self.dram, self.sems = nc, ctx, dram, {}

    def sem(self, name):
        if name not in self.sems:
            self.sems[name] = self.nc.alloc_semaphore(name=name)
        return self.sems[name]

    def end_phase(self):
        self.nc.clear_and_free_semaphores(list(self.sems.values()))
        self.nc.all_engine_barrier()
        self.sems = {}


def wide_row(ap, n):
    return ap.rearrange("(a n) -> a n", a=1).broadcast_to([P, n])


def phase_project(core, PS):
    nc, d, sem = core.nc, core.dram, core.sem
    NCH = -(-NIN // 512)
    cols = [(c * 512, min(512, NIN - c * 512)) for c in range(NCH)]
    with ExitStack() as ctx:
        sb = lambda n, s, t=F32: ctx.enter_context(nc.sbuf_tensor(n, s, t))
        w = sb("pj_w", [P, KC, NIN])
        x = sb("pj_x", [P, D])
        sq = sb("pj_sq", [P, D])
        xT = sb("pj_xT", [P, KC, P])
        g = sb("pj_g", [P, KC])
        ident = sb("pj_id", [P, P])
        out = sb("pj_out", [P, NIN])
        st = sb("pj_st", [P, 4])
        expo = sb("pj_expo", [P, 1])
        x_loaded, c_loaded = sem("pj_x_loaded"), sem("pj_c_loaded")
        w_loaded = [sem(f"pj_w_loaded{c}") for c in range(NCH)]
        ms, rstd, xn, tT, tR, pr, ev = [sem("pj_" + n) for n in
            ("ms_ready", "rstd_ready", "xn_ready", "transposed", "xT_ready", "projected", "evacuated")]
        stored, chain = [sem(f"pj_stored{c}") for c in range(NCH)], sem("pj_dve")
        with nc.Block() as block:
            @block.sync
            def _(sp):
                sp.dma_start(ident[:], d["ident"][:]).then_inc(c_loaded, 16)
                with nc.allow_non_contiguous_dma(reason="a gain by channel"):
                    sp.dma_start(g[:], d["g_mix"][0].rearrange("(c p) -> p c", p=P)).then_inc(c_loaded, 16)
                sp.dma_start(x[:], d["x"][0:P, :]).then_inc(x_loaded, 16)
                sp.dma_start(d["proj"][0:1, NRET:NIN], d["zero_row"][:]).then_inc(sem("pj_zero_stored"), 16)
                wv = d["w_in"][0].rearrange("(c p) n -> p c n", p=P)
                for c, (a, n) in enumerate(cols):
                    sp.dma_start(w[:, :, a:a + n], wv[:, :, a:a + n]).then_inc(w_loaded[c], 16)
                with sp.Fori(0, TILES) as i:
                    sp.wait_ge(tT, 2 * i + 2)
                    sp.dma_start(x[:], d["x"][bass.ds(i * P + P, P), :]).then_inc(x_loaded, 16)
                    for c, (a, n) in enumerate(cols):
                        sp.wait_ge(ev, NCH * i + NCH + c + 1)
                        sp.dma_start(d["proj"][bass.ds(i * P + 1, P), a:a + n], out[:, a:a + n]).then_inc(stored[c], 16)
                for c in range(NCH):
                    sp.wait_ge(stored[c], 16 * TILES)
                sp.wait_ge(x_loaded, 16 * (TILES + 1))
                sp.wait_ge(sem("pj_zero_stored"), 16)

            @block.vector
            def _(v):
                v.wait_ge(c_loaded, 32)
                PER = 1
                with v.Fori(0, TILES) as i:
                    lk = Steps(v, chain, i * PER)
                    v.wait_ge(x_loaded, 16 * i + 16)
                    lk(v.tensor_tensor_reduce(sq[:], x[:], x[:], 1.0, 0.0, ALU.mult, ALU.add, st[:, 0:1]))
                    v.tensor_scalar(st[:, 1:2], st[:, 0:1], 1.0 / D, EPS, ALU.mult, ALU.add).then_inc(ms, 1)
                    v.wait_ge(rstd, i + 1)
                    v.tensor_scalar(x[:], x[:], st[:, 2:3], None, ALU.mult).then_inc(xn, 1)
                    v.wait_ge(pr, NCH * i)
                    for b in range(2):
                        v.wait_ge(tT, 2 * i + b + 1)
                        v.tensor_tensor(xT[:, 4 * b:4 * b + 4, :], PS[:, b, :].rearrange("p (c t) -> p c t", c=4),
                                        g[:, 4 * b:4 * b + 4].unsqueeze(2).to_broadcast([P, 4, P]), ALU.mult).then_inc(tR, 1)
                    assert lk.n == PER

            @block.gpsimd
            def _(po):
                po.memset(expo[:], -0.5).then_inc(sem("pj_expo"), 1)
                po.wait_ge(sem("pj_expo"), 1)
                with po.Fori(0, TILES) as i:
                    po.wait_ge(ms, i + 1)
                    po.tensor_tensor(st[:, 2:3], st[:, 1:2], expo[:], ALU.pow).then_inc(rstd, 1)

            @block.tensor
            def _(pe):
                pe.wait_ge(c_loaded, 32)
                with pe.Fori(0, TILES) as i:
                    pe.wait_ge(xn, i + 1)
                    pe.wait_ge(ev, NCH * i + NCH)
                    for c in range(KC):
                        ins = pe.transpose(PS[:, c // 4, c % 4 * P:(c % 4 + 1) * P], x[:, c * P:(c + 1) * P], ident[:])
                        if c % 4 == 3:
                            ins.then_inc(tT, 1)
                    pe.wait_ge(tR, 2 * i + 2)
                    for c, (a, n) in enumerate(cols):
                        pe.wait_ge(w_loaded[c], 16)
                        pe.wait_ge(ev, NCH * i + c + 1)
                        bank = 1 + c
                        for k in range(KC):
                            ins = pe.matmul(PS[:, bank, 0:n], xT[:, k, :], w[:, k, a:a + n], start=k == 0, stop=k == KC - 1)
                        ins.then_inc(pr, 1)

            @block.scalar
            def _(act):
                act.sem_inc(ev, NCH)
                with act.Fori(0, TILES) as i:
                    for c, (a, n) in enumerate(cols):
                        act.wait_ge(pr, NCH * i + c + 1)
                        act.wait_ge(stored[c], 16 * i)
                        act.copy(out[:, a:a + n], PS[:, 1 + c, 0:n]).then_inc(ev, 1)


def phase_mixers(core, PS):
    nc, d, sem = core.nc, core.dram, core.sem
    OQ, OV, OG = 0, 2 * RQK, 2 * RQK + RW
    OR = NRET
    with ExitStack() as ctx:
        sb = lambda n, s, t=F32: ctx.enter_context(nc.sbuf_tensor("mx_" + n, s, t))
        pin, prev = sb("pin", [P, NIN]), sb("prev", [P, NRW])
        rope = sb("rope", [P, 2, 2 * RH, 32])
        mu = sb("mu", [P, NRW])
        names = ["rwkv_w0", "rwkv_a0", "rwkv_k_k", "rwkv_k_a", "rwkv_r_k", "rwkv_lnx_w", "rwkv_lnx_b", "ret_gn"]
        vec = sb("vec", [P, len(names), 512])
        V_ = {n: vec[:, j, :] for j, n in enumerate(names)}
        w2, a2, g2 = sb("w2", [LW, WW]), sb("a2", [LA, WW]), sb("g2", [LG, WW])
        ident = sb("ident", [P, P])
        masks = sb("masks", [P, NMASK, P])
        chunk = sb("chunk", [P, DB])
        cdec = sb("cdec", [RDK, 2, RW])
        expk, expt = sb("expk", [WN, DB, NS]), sb("expt", [NS, DB, RDV])
        expo = sb("expo", [P, 8])
        lora = sb("lora", [P, 256])
        loT, hgT = sb("loT", [64, 2, P]), sb("hgT", [P, P])
        sg = sb("sg", [P, 2, WW])
        lw = sb("lw", [P, WW])
        pinc, pinv = sb("pinc", [P, WW]), sb("pinv", [P, WW])
        t0, kk = sb("t0", [P, WW]), sb("kk", [P, WW])
        kr = sb("kr", [P, WW])
        stage = sb("stage", [P, 2, 8, WW])
        V_W, V_R, G_W, G_R = 4, 5, 6, 7
        bonus = sb("bonus", [P, 2, WH])
        stb = sb("stb", [P, 4, WH])
        st = sb("st", [P, 8, 8])
        T4 = sb("T4", [WN, WH, 4, P])
        M4 = sb("M4", [P, WH, 4, P])
        ALX = sb("ALX", [P, 2, 2, 4, P])
        AL, X = ALX[:, 0], ALX[:, 1]
        T, TT = sb("T", [P, 2, 4, P]), sb("TT", [P, 2, 4, P])
        U = sb("U", [WN, WH, WN])
        pc = sb("pc", [WN, 2, WH, DB])
        tb = sb("tb", [P, WW])
        xs, sas = sb("xs", [P, WW]), sb("sas", [P, WW])
        y, o_w, o_r = sb("y", [P, WW]), sb("o_w", [P, WW]), sb("o_r", [P, RW])
        qk, qkt = sb("qk", [P, 2 * RH, 64]), sb("qkt", [P, 2 * RH, 32])
        qkT = sb("qkT", [RDK, 2 * RH, P])
        att = sb("att", [P, RH, P])
        S = sb("S", [RDK, RH, RDV])
        Us = stage[0:WN, 1].rearrange("p a n -> p (a n)").rearrange("p (h b n) -> p h b n", h=WH, b=DB)
        Uv = M4[0:WN].rearrange("p h a t -> p (h a t)").rearrange("p (b h k) -> p b h k", b=DB, h=WH)
        Ss = T4[:].rearrange("p h a t -> p (h a t)").rearrange("p (b h e) -> p b h e", b=DB, h=RH)
        ex_k = ALX[0:WN].rearrange("p x g h t -> p (x g h t)").rearrange("p (f j b t) -> p f j b t", f=2, j=2, b=DB)
        ex_t = sb("ex_t", [NS, 2, DB, RDV])
        ro, rt = sb("ro", [P, RW]), sb("rt", [P, RW])

        B = lambda b, *ix: PS[:, b, :] if not ix else PS[ix[0], b, ix[1]]
        heads = lambda ap, h=WH: ap.rearrange("p (h n) -> p h n", h=h)
        over = lambda ap, n: ap.unsqueeze(2).to_broadcast([ap.shape[0], ap.shape[1], n])
        rows = [slice(0, CH), slice(CH, P)]

        loaded, c_loaded, states = sem("mx_tile_loaded"), sem("mx_consts_loaded"), sem("mx_states_loaded")
        shift_rows = sem("mx_shift_rows_loaded")
        chain = {e: sem("mx_own_" + e) for e in ("dve", "act", "pool")}
        S_ = lambda n: sem("mx_" + n)

        ctx2 = ExitStack()
        with ctx2, nc.Block() as block:
            @block.sync
            def _(sp):
                n = 0
                with nc.allow_non_contiguous_dma(reason="small rows, once"):
                    for dst, src in [(mu[:], wide_row(d["rwkv_mu"][0], NRW)),
                                     *[(V_[x], wide_row(d[x][0] if x != "rwkv_r_k" else d[x][0].rearrange("h n -> (h n)"), 512)) for x in names],
                                     (w2[:], d["rwkv_w2"][0]), (a2[:], d["rwkv_a2"][0]), (g2[:], d["rwkv_g2"][0]),
                                     (ident[:], d["ident"]), (masks[:], d["mask_p"]), (chunk[:], d["chunk_p"]),
                                     (cdec[:], d["cdec"]), (expk[:].rearrange("p a b -> p (a b)"), d["expand_k"]),
                                     (expt[:].rearrange("p a b -> p (a b)"), d["expand_t"])]:
                        sp.dma_start(dst, src).then_inc(c_loaded, 16)
                        n += 1
                assert n == N_CONST

                def load(at, i):
                    sp.dma_start(pin[:], d["proj"][bass.ds(at + 1, P), :]).then_inc(loaded, 16)
                    sp.dma_start(prev[:], d["proj"][bass.ds(at, P), OR:NIN]).then_inc(loaded, 16)
                    sp.dma_start(rope[:].rearrange("p a b c -> p (a b c)"), d["rope"][bass.ds(at, P), :]).then_inc(loaded, 16)

                def store_ret(at, j):
                    sp.wait_ge(S_("o_r_ready"), j + 1)
                    sp.dma_start(d["mixed"][bass.ds(at, P), 0:RW], o_r[:]).then_inc(S_("o_r_stored"), 16)

                def store_rwkv(at, i):
                    sp.wait_ge(S_("o_w_ready"), i + 1)
                    sp.dma_start(d["mixed"][bass.ds(at, P), RW:D], o_w[:]).then_inc(S_("o_w_stored"), 16)

                sp.sem_inc(S_("o_r_stored"), 16)
                sp.sem_inc(S_("o_w_stored"), 16)
                load(0, 0)
                sp.wait_ge(S_("pin_used"), 1)
                load(P, 1)
                store_ret(0, 0)
                with sp.Fori(0, NT - 2) as i:
                    sp.wait_ge(S_("pin_used"), i + 2)
                    load(i * P + 2 * P, i)
                    store_ret(i * P + P, i + 1)
                    store_rwkv(i * P, i)
                store_ret((NT - 1) * P, NT - 1)
                store_rwkv((NT - 2) * P, NT - 2)
                store_rwkv((NT - 1) * P, NT - 1)
                sp.dma_start(Uv, d["state_rwkv"][0].rearrange("b h v k -> v b h k")).then_inc(states, 16)
                sp.dma_start(Ss, d["state_ret"][0].rearrange("b h k e -> k b h e")).then_inc(states, 16)
                sp.dma_start(d["out_ret_p"].rearrange("h k e -> k h e"), S[:]).then_inc(S_("states_stored"), 16)
                sp.wait_ge(S_("U_turned"), 1)
                sp.dma_start(d["out_rwkv_p"].rearrange("h v k -> v h k"), xs[0:WN, :].rearrange("p (h n) -> p h n", h=WH)).then_inc(S_("states_stored"), 16)
                sp.dma_start(masks[:], d["mask_s"]).then_inc(c_loaded, 16)
                sp.dma_start(chunk[:], d["chunk_s"]).then_inc(c_loaded, 16)
                load(SEQ, NT)
                sp.wait_ge(loaded, 48 * (NT + 1))
                sp.dma_start(prev[0:NS:DS, :], d["state_shift"][0]).then_inc(shift_rows, 16)
                sp.wait_ge(S_("Ss_ready"), RH)
                sp.dma_start(d["out_ret_s"].rearrange("b h k e -> k b h e"), Ss).then_inc(S_("Ss_stored"), 16)
                store_ret(SEQ, NT)
                store_rwkv(SEQ, NT)
                sp.dma_start(d["out_shift_p"], d["proj"][SEQ:SEQ + 1, OR:NIN]).then_inc(S_("states_stored"), 16)
                sp.dma_start(d["out_shift_s"], d["proj"][SEQ + 1:SEQ + 1 + NS, OR:NIN].rearrange("(b s) n -> b s n", s=DS)[:, DS - 1, :]).then_inc(S_("states_stored"), 16)
                sp.wait_ge(S_("Ss_stored"), 16)
                sp.wait_ge(S_("Us_turned"), WH)
                sp.dma_start(d["out_rwkv_s"].rearrange("b h v k -> v b h k"), Uv).then_inc(S_("states_stored"), 16)
                sp.wait_ge(S_("states_stored"), 80)
                sp.wait_ge(S_("o_r_stored"), 16 * (TILES + 1))
                sp.wait_ge(S_("o_w_stored"), 16 * (TILES + 1))

            def a_shift(v, j, lk):
                lk(v.tensor_tensor(prev[:], prev[:], pin[:, OR:NIN], ALU.subtract))
                lk(v.tensor_tensor(prev[:], prev[:], mu[:], ALU.mult))
                v.tensor_tensor(pin[:, OR:NIN], pin[:, OR:NIN], prev[:], ALU.add).then_inc(S_("shifted"), 1)

            def a_rotary(v, j, lk):
                qin = pin[:, OQ:OV].rearrange("p (h n) -> p h n", n=64)
                lo, hi = qin[:, :, 0:32], qin[:, :, 32:64]
                cs, sn = rope[:, 0], rope[:, 1]
                lk(v.tensor_tensor(qk[:, :, 0:32], lo, cs, ALU.mult))
                lk(v.tensor_tensor(qkt[:], hi, sn, ALU.mult))
                lk(v.tensor_tensor(qk[:, :, 0:32], qk[:, :, 0:32], qkt[:], ALU.subtract))
                lk(v.tensor_tensor(qk[:, :, 32:64], hi, cs, ALU.mult))
                lk(v.tensor_tensor(qkt[:], lo, sn, ALU.mult))
                v.tensor_tensor(qk[:, :, 32:64], qk[:, :, 32:64], qkt[:], ALU.add).then_inc(S_("qk_ready"), 1)

            def a_keys(v, j, lk):
                v.wait_ge(S_("shifted"), j + 1)
                lk(v.tensor_tensor(kk[:], K_(), V_["rwkv_k_k"], ALU.mult))
                lk(v.tensor_tensor(t0[:], kk[:], kk[:], ALU.mult))
                lk(v.tensor_reduce(st[:, 0, :], heads(t0[:]), AX.X, ALU.add))
                v.tensor_scalar(st[:, 1, :], st[:, 0, :], 1e-24, None, ALU.max).then_inc(S_("kk_sq"), 1)

            def a_turned_qk(v, j, lk):
                v.wait_ge(S_("qkT"), j + 1)
                v.tensor_copy(qkT[:].rearrange("p (a h) t -> p a (h t)", a=2), PS[0:RDK, 6:8, :]).then_inc(S_("qkT_ready"), 1)
                v.wait_ge(S_("lora_act"), j + 1)
                v.tensor_scalar(lora[:, 128:256], lora[:, 128:256], 0.5, 0.5, ALU.mult, ALU.add).then_inc(S_("lora_ready"), 1)

            def a_turned_lora(v, j, lk):
                v.wait_ge(S_("kk_rn"), j + 1)
                lk(v.tensor_tensor(heads(kk[:]), heads(kk[:]), over(st[:, 2, :], WN), ALU.mult))
                v.wait_ge(S_("loraT"), j + 1)
                v.tensor_copy(loT[:], B(6, slice(0, 64), slice(0, 256)).rearrange("p (a b) -> p a b", a=2))
                v.tensor_copy(hgT[:], B(6, slice(0, P), slice(256, 384))).then_inc(S_("loraT_ready"), 1)

            def a_rates(v, j, lk):
                v.wait_ge(S_("rates"), j + 1)
                v.tensor_tensor(sg[:, 0, :], B(6), V_["rwkv_w0"], ALU.add)
                v.tensor_tensor(sg[:, 1, :], B(7), V_["rwkv_a0"], ALU.add).then_inc(S_("z_ready"), 1)

            def a_att(v, j, lk):
                v.wait_ge(S_("att_done"), j + 1)
                v.tensor_tensor(att[:], B(5).rearrange("p (h t) -> p h t", h=RH),
                                masks[:, 2, :].unsqueeze(1).to_broadcast([P, RH, P]), ALU.mult).then_inc(S_("att_ready"), 1)

            def a_decay(v, j, bf, lk):
                v.wait_ge(S_("z_tanh"), j + 1)
                c = -0.5 * float(np.exp(-0.5))
                v.tensor_scalar(lw[:], sg[:, 0, :], c, c, ALU.mult, ALU.add).then_inc(S_("lw_ready"), 1)
                lk(v.tensor_scalar(sg[:, 1, :], sg[:, 1, :], 0.5, 0.5, ALU.mult, ALU.add))
                lk(v.scalar_tensor_tensor(t0[:], sg[:, 1, :], -1.0, V_["rwkv_k_a"], ALU.add, ALU.mult))
                lk(v.scalar_tensor_tensor(kr[:], t0[:], 1.0, K_(), ALU.add, ALU.mult))
                lk(v.tensor_tensor(t0[:], R_(), kr[:], ALU.mult))
                lk(v.tensor_tensor(t0[:], t0[:], V_["rwkv_r_k"], ALU.mult))
                lk(v.tensor_reduce(bonus[:, bf, :], heads(t0[:]), AX.X, ALU.add))
                v.tensor_tensor(t0[:], kk[:], sg[:, 1, :], ALU.mult)

            def a_ret_state(v, j, lk):
                v.wait_ge(S_("ret_done"), j + 1)
                lk(v.tensor_copy(ro[:], B(6)))
                lk(v.tensor_tensor(flat(S[:]), flat(S[:]), B(7, slice(0, RDK), slice(0, 512)), ALU.add))
                v.tensor_tensor(flat(S[:]), flat(S[:]), cdec[:, 0, :], ALU.mult).then_inc(S_("S_ready"), 1)

            def a_before(v, j, lk):
                v.wait_ge(S_("L_read"), j + 1)
                v.tensor_tensor(sg[:, 0, :], B(4), lw[:], ALU.subtract).then_inc(S_("lx_ready"), 1)

            def a_operands(v, j, bf, lk):
                v.wait_ge(S_("decays"), j + 1)
                v.scalar_tensor_tensor(stage[:, bf, 0, :], kk[:], -1.0, sg[:, 0, :], ALU.mult, ALU.mult)
                v.tensor_tensor(stage[:, bf, 1, :], R_(), pinc[:], ALU.mult).then_inc(S_("pin_used"), 1)
                v.tensor_tensor(stage[:, bf, 2, :], t0[:], pinv[:], ALU.mult)
                v.tensor_tensor(stage[:, bf, 3, :], kr[:], pinv[:], ALU.mult).then_inc(S_("arbk_ready"), 1)

            def a_ret_gate(v, j, bf, lk):
                rg = stage[:, bf, G_R, :]
                v.wait_ge(S_("lora_act"), j + 1)
                lk(v.scalar_tensor_tensor(rg, rg, 1.0, pin[:, OG:OG + RW], ALU.add, ALU.mult))
                lk(v.scalar_tensor_tensor(rg, rg, 0.5, V_["ret_gn"], ALU.mult, ALU.mult))

            def a_ret_norm(v, j, lk):
                lk(v.tensor_tensor(rt[:], ro[:], ro[:], ALU.mult))
                lk(v.tensor_reduce(st[:, 3, 0:RH], heads(rt[:], RH), AX.X, ALU.add))
                v.tensor_scalar(st[:, 4, 0:RH], st[:, 3, 0:RH], 1.0 / RDV, EPS, ALU.mult, ALU.add).then_inc(S_("ret_ms"), 1)

            def a_ret_out(v, j, bf, lk):
                v.wait_ge(S_("ret_rn"), j + 1)
                lk(v.tensor_tensor(heads(rt[:], RH), heads(ro[:], RH), over(st[:, 5, 0:RH], RDV), ALU.mult))
                v.wait_ge(S_("o_r_stored"), 16 * j + 16)
                v.tensor_tensor(o_r[:], rt[:], stage[:, bf, G_R, :], ALU.mult).then_inc(S_("o_r_ready"), 1)

            def b_turned(v, i):
                for h in range(0, WH, 2):
                    v.wait_ge(S_("headT"), WH * i + h + 1)
                    v.tensor_copy(T4[:, h, :, :], B(h % 4, slice(0, WN), slice(0, 512)).rearrange("p (a b) -> p a b", a=4)).then_inc(S_("T4_ready_dve"), 1)

            def b_masked(v, i):
                for h in range(WH):
                    v.wait_ge(S_("products"), WH * i + h + 1)
                    v.tensor_tensor(M4[:, h].rearrange("p (x a) b -> p x a b", x=2), B(4 + h % 4).rearrange("p (x a b) -> p x a b", x=2, a=2),
                                    masks[:, 0:2, :].unsqueeze(1).to_broadcast([P, 2, 2, P]), ALU.mult).then_inc(S_("M4_ready"), 1)

            def b_first(v, i):
                for g in range(2):
                    v.wait_ge(S_("AL_ready"), 2 * levels_before(i) + g + 1)
                    v.tensor_tensor(TT[:, g], AL[:, g], ident[:].unsqueeze(1).to_broadcast([P, 4, P]), ALU.add).then_inc(S_("TT_first"), 1)

            def b_level(v, i, l):
                for g in range(2):
                    v.wait_ge(S_("dTT"), 2 * updates_before(i) + 2 * (l - 1) + g + 1)
                    v.tensor_tensor(TT[:, g], TT[:, g], B(4 + g).rearrange("p (a b) -> p a b", a=4), ALU.add).then_inc(S_("TT_ready"), 1)

            def b_state(v, i, c, bf, lk):
                v.wait_ge(S_("U_products"), 2 * i + c + 1)
                lk(v.tensor_tensor(flat(U[:]), flat(U[:]), B(1, slice(0, WN), slice(0, 512)), ALU.add))
                v.tensor_tensor(U[:], U[:], pc[:, bf, :, c:c + 1].to_broadcast([WN, WH, WN]), ALU.mult).then_inc(S_("U_ready"), 1)

            def b_center(v, i, lk):
                lk(v.tensor_reduce(stb[:, 0, :], heads(B(0)), AX.X, ALU.add))
                lk(v.tensor_scalar(stb[:, 0, :], stb[:, 0, :], 1.0 / WN, None, ALU.mult))
                v.tensor_tensor(heads(y[:]), heads(B(0)), over(stb[:, 0, :], WN), ALU.subtract).then_inc(S_("y_read"), 1)
                v.wait_ge(S_("y_read"), i + 1)
                lk(v.tensor_tensor(tb[:], y[:], y[:], ALU.mult))
                lk(v.tensor_reduce(stb[:, 1, :], heads(tb[:]), AX.X, ALU.add))
                v.tensor_scalar(stb[:, 2, :], stb[:, 1, :], 1.0 / WN, LNX_EPS, ALU.mult, ALU.add).then_inc(S_("y_ms"), 1)

            def b_out(v, i, bf, lk):
                lk(v.tensor_tensor(heads(tb[:]), heads(stage[:, bf, V_W, :]), over(bonus[:, bf, :], WN), ALU.mult))
                lk(v.tensor_tensor(tb[:], tb[:], V_["rwkv_lnx_b"], ALU.add))
                v.wait_ge(S_("y_rn"), i + 1)
                lk(v.tensor_tensor(heads(y[:]), heads(y[:]), over(stb[:, 3, :], WN), ALU.mult))
                lk(v.tensor_tensor(y[:], y[:], V_["rwkv_lnx_w"], ALU.mult))
                lk(v.tensor_tensor(y[:], y[:], tb[:], ALU.add))
                v.wait_ge(S_("o_w_stored"), 16 * i + 16)
                v.tensor_tensor(o_w[:], y[:], stage[:, bf, G_W, :], ALU.mult).then_inc(S_("o_w_ready"), 1)

            def dve_a(v, j, bf, lk, sample=False):
                a_shift(v, j, lk)
                a_rotary(v, j, lk)
                a_keys(v, j, lk)
                a_turned_qk(v, j, lk)
                a_ret_gate(v, j, bf, lk)
                a_turned_lora(v, j, lk)
                a_rates(v, j, lk)
                a_att(v, j, lk)
                a_decay(v, j, bf, lk)
                if sample:
                    dve_retention_sample(v, lk)
                else:
                    a_ret_state(v, j, lk)
                a_before(v, j, lk)
                a_ret_norm(v, j, lk)
                a_operands(v, j, bf, lk)
                a_ret_out(v, j, bf, lk)

            def dve_pair(v, i, bf, lk):
                b_turned(v, i)
                b_masked(v, i)
                b_first(v, i)
                v.wait_ge(loaded, 48 * i + 96)
                a_shift(v, i + 1, lk)
                b_level(v, i, 1)
                a_rotary(v, i + 1, lk)
                b_level(v, i, 2)
                a_keys(v, i + 1, lk)
                b_level(v, i, 3)
                a_turned_qk(v, i + 1, lk)
                a_ret_gate(v, i + 1, 1 - bf, lk)
                b_level(v, i, 4)
                a_turned_lora(v, i + 1, lk)
                b_level(v, i, 5)
                a_rates(v, i + 1, lk)
                a_att(v, i + 1, lk)
                b_state(v, i, 0, bf, lk)
                a_decay(v, i + 1, 1 - bf, lk)
                b_state(v, i, 1, bf, lk)
                b_center(v, i, lk)
                a_ret_state(v, i + 1, lk)
                a_before(v, i + 1, lk)
                a_ret_norm(v, i + 1, lk)
                a_operands(v, i + 1, 1 - bf, lk)
                b_out(v, i, bf, lk)
                a_ret_out(v, i + 1, 1 - bf, lk)

            flat = lambda ap: ap.rearrange("p h n -> p (h n)")
            K_ = lambda: pin[:, OR + WW:OR + 2 * WW]
            R_ = lambda: pin[:, OR:OR + WW]
            def dve_retention_sample(v, lk):
                for h in range(RH):
                    if h >= 2:
                        v.wait_ge(S_("ret_s_done"), h - 1)
                    v.tensor_tensor(ex_k[:, h % 2, 0], qkT[:, h, 0:NS].unsqueeze(1).to_broadcast([RDK, DB, NS]), expk[:], ALU.mult)
                    v.tensor_tensor(ex_t[:, h % 2], stage[0:NS, 0, V_R, h * RDV:(h + 1) * RDV].unsqueeze(1).to_broadcast([NS, DB, RDV]),
                                    expt[:], ALU.mult).then_inc(S_("ret_ex"), 1)
                    if h >= 1:
                        ret_state(v, h - 1, lk)
                ret_state(v, RH - 1, lk)
                v.wait_ge(S_("ret_s_done"), RH)
                v.tensor_copy(ro[0:NS, :], B(6, slice(0, NS), slice(0, 512))).then_inc(S_("ro_s"), 1)
                v.wait_ge(S_("ro_s"), 1)

            def ret_state(v, h, lk):
                v.wait_ge(S_("ret_s_done"), h + 1)
                for j in range(2):
                    sv = Ss[:, 4 * j:4 * j + 4, h, :]
                    lk(v.tensor_tensor(sv, sv, B(2 * (h % 2) + j, slice(0, RDK), slice(0, 512)).rearrange("p (b e) -> p b e", b=4), ALU.add))
                v.tensor_scalar(Ss[:, :, h, :], Ss[:, :, h, :], float(np.exp(DS * np.log1p(-2.0 ** (-5.0 - h)))), None, ALU.mult).then_inc(S_("Ss_ready"), 1)

            def dve_scan_sample(v, lk):
                vr = stage[:, 0, V_W, :]
                for h in range(WH):
                    if h >= 2:
                        v.wait_ge(S_("scan_s_x"), h - 1)
                    for j in range(2):
                        ins = v.tensor_tensor(ex_k[:, h % 2, j], T4[:, h, j, 0:NS].unsqueeze(1).to_broadcast([WN, DB, NS]), expk[:], ALU.mult)
                    ins.then_inc(S_("scan_ex_k"), 1)
                v.wait_ge(S_("sas_ready"), 2 * NT + 1)
                for h in range(WH):
                    hs = slice(h * WN, (h + 1) * WN)
                    if h >= 2:
                        v.wait_ge(S_("scan_s_u"), h - 1)
                    v.tensor_tensor(ex_t[:, h % 2, :, 0:WN], sas[0:NS, hs].unsqueeze(1).to_broadcast([NS, DB, WN]), expt[:, :, 0:WN], ALU.mult)
                    v.tensor_tensor(ex_t[:, h % 2, :, WN:2 * WN], vr[0:NS, hs].unsqueeze(1).to_broadcast([NS, DB, WN]), expt[:, :, 0:WN],
                                    ALU.mult).then_inc(S_("scan_ex_t"), 1)
                    if h >= 1:
                        u_state(v, h - 1, lk)
                u_state(v, WH - 1, lk)

            def u_state(v, h, lk):
                v.wait_ge(S_("scan_s_u"), h + 1)
                lk(v.tensor_tensor(Us[:, h], Us[:, h], B(1 + h % 2, slice(0, WN), slice(0, 512)).rearrange("p (b n) -> p b n", b=DB), ALU.add))
                v.tensor_tensor(Us[:, h], Us[:, h], over(pc[:, 0, h, :], WN), ALU.mult).then_inc(S_("Us_ready"), 1)

            levels_before = lambda i: i * LEVELS
            updates_before = lambda i: i * (LEVELS - 1)
            grown_before = lambda i: i * (LEVELS - 2)

            @block.vector
            def _(v):
                v.memset(U[:], 0.0)
                v.memset(sas[:], 0.0)
                v.memset(S[:], 0.0).then_inc(S_("U_ready"), 1)
                v.wait_ge(S_("U_ready"), 1)
                v.sem_inc(S_("S_ready"), 1)
                v.wait_ge(c_loaded, 16 * N_CONST)
                v.wait_ge(loaded, 48)
                dve_a(v, 0, 0, Steps(v, S_("dve_start")))
                with v.Fori(0, NT // 2 - 1) as m:
                    for bf in range(2):
                        lk = Steps(v, chain["dve"], (2 * m + bf) * PER_PAIR)
                        dve_pair(v, 2 * m + bf, bf, lk)
                        assert lk.n == PER_PAIR, lk.n
                lk = Steps(v, S_("dve_end"))
                dve_pair(v, NT - 2, 0, lk)
                i, bf = NT - 1, 1
                b_turned(v, i)
                b_masked(v, i)
                b_first(v, i)
                for l in range(1, LEVELS):
                    b_level(v, i, l)
                b_state(v, i, 0, bf, lk)
                b_state(v, i, 1, bf, lk)
                b_center(v, i, lk)
                b_out(v, i, bf, lk)
                v.wait_ge(c_loaded, 16 * (N_CONST + 2))
                v.wait_ge(loaded, 48 * (NT + 1))
                v.wait_ge(shift_rows, 16)
                v.wait_ge(states, 32)
                dve_a(v, NT, 0, lk, True)
                v.wait_ge(S_("Ss_stored"), 16)
                v.wait_ge(S_("state_turned"), WH)
                b_turned(v, NT)
                b_masked(v, NT)
                b_first(v, NT)
                for l in range(1, LEVELS_S):
                    b_level(v, NT, l)
                dve_scan_sample(v, lk)
                v.wait_ge(S_("y_s_done"), 1)
                b_center(v, NT, lk)
                b_out(v, NT, 0, lk)

            @block.gpsimd
            def _(po):
                po.memset(expo[:], -0.5).then_inc(S_("expo"), 1)
                po.wait_ge(S_("expo"), 1)
                po.wait_ge(c_loaded, 16 * N_CONST)

                def level(i, l):
                    for g in range(2):
                        if l == 0:
                            po.wait_ge(S_("M4_ready"), WH * i + 4 * g + 4)
                        if l == 1:
                            po.wait_ge(S_("TT_first"), 2 * i + g + 1)
                        if l >= 2:
                            po.wait_ge(S_("X_done"), 2 * updates_before(i) + 2 * (l - 2) + g + 1)
                        po.tensor_tensor(AL[:, g], M4[:, 4 * g:4 * g + 4, 0, :],
                                         masks[:, 4 + l, :].unsqueeze(1).to_broadcast([P, 4, P]), ALU.mult).then_inc(S_("AL_ready"), 1)

                def key_norm(j):
                    po.wait_ge(S_("kk_sq"), j + 1)
                    po.tensor_tensor(st[:, 2, :], st[:, 1, :], expo[:], ALU.pow).then_inc(S_("kk_rn"), 1)

                def ret_norm(j):
                    po.wait_ge(S_("ret_ms"), j + 1)
                    po.tensor_tensor(st[:, 5, 0:RH], st[:, 4, 0:RH], expo[:, 0:RH], ALU.pow).then_inc(S_("ret_rn"), 1)

                def y_norm(i):
                    po.wait_ge(S_("y_ms"), i + 1)
                    po.tensor_tensor(stb[:, 3, :], stb[:, 2, :], expo[:], ALU.pow).then_inc(S_("y_rn"), 1)

                def pair(i):
                    for l in range(4):
                        level(i, l)
                    key_norm(i + 1)
                    level(i, 4)
                    level(i, 5)
                    y_norm(i)
                    ret_norm(i + 1)

                key_norm(0)
                ret_norm(0)
                with po.Fori(0, NT - 1) as i:
                    pair(i)
                for l in range(LEVELS):
                    level(NT - 1, l)
                y_norm(NT - 1)
                po.wait_ge(c_loaded, 16 * (N_CONST + 2))
                key_norm(NT)
                ret_norm(NT)
                for l in range(LEVELS_S):
                    level(NT, l)
                y_norm(NT)

            def act_lora(act, j, bf):
                act.wait_ge(S_("shifted"), j + 1)
                hw = OR + 3 * WW
                act.activation(lora[:, 0:64], pin[:, hw:hw + 64], ACT.Tanh)
                act.copy(lora[:, 64:128], pin[:, hw + 64:hw + 128])
                act.activation(stage[:, bf, G_R, :], pin[:, OG:OG + RW], ACT.Tanh, scale=0.5)
                act.copy(stage[:, bf, V_W, :], pin[:, OR + 2 * WW:OR + 3 * WW])
                act.copy(stage[:, bf, V_R, :], pin[:, OV:OV + RW])
                act.activation(lora[:, 128:256], pin[:, hw + 128:hw + 256], ACT.Tanh, scale=0.5).then_inc(S_("lora_act"), 1)

            def act_rates(act, j):
                act.wait_ge(S_("z_ready"), j + 1)
                act.activation(sg[:], sg[:], ACT.Tanh, scale=0.5).then_inc(S_("z_tanh"), 1)

            def act_gate(act, j, bf):
                act.wait_ge(S_("g_done"), j + 1)
                act.copy(stage[:, bf, G_W, :], B(4)).then_inc(S_("gate_copied"), 1)

            def act_decays(act, j, bf, nch):
                act.wait_ge(S_("L_ready"), j + 1)
                act.activation(pinc[:], B(4), ACT.Exp)
                act.activation(pinv[:], B(4), ACT.Exp, scale=-1.0).then_inc(S_("L_read"), 1)
                act.activation(pc[:, bf, :, 0:nch], B(5, slice(0, WN), slice(0, WH * nch)).rearrange("p (h c) -> p h c", h=WH), ACT.Exp)
                act.wait_ge(S_("lx_ready"), j + 1)
                act.activation(sg[:, 0, :], sg[:, 0, :], ACT.Exp).then_inc(S_("decays"), 1)

            def act_turned(act, i):
                for h in range(1, WH, 2):
                    act.wait_ge(S_("headT"), WH * i + h + 1)
                    act.copy(T4[:, h, :, :], B(h % 4, slice(0, WN), slice(0, 512)).rearrange("p (a b) -> p a b", a=4)).then_inc(S_("T4_ready_act"), 1)

            def act_T(act, i, l, levels):
                for g in range(2):
                    act.wait_ge(S_("T_turned"), 2 * updates_before(i) + 2 * l + g + 1)
                    act.copy(T[:, g], B(2 + g).rearrange("p (a b) -> p a b", a=4)).then_inc(S_("T_ready"), 1)

            def act_X(act, i, l):
                for g in range(2):
                    act.wait_ge(S_("X_done"), 2 * updates_before(i) + 2 * (l - 1) + g + 1)
                    act.copy(X[:, g], B(g).rearrange("p (a b) -> p a b", a=4)).then_inc(S_("X_ready"), 1)

            def act_scan(act, i, c):
                act.wait_ge(S_("x_done"), 2 * i + c + 1)
                act.copy(xs[rows[c], :], PS[rows[c], 2, :]).then_inc(S_("xs_ready"), 1)
                act.wait_ge(S_("sa_done"), 2 * i + c + 1)
                act.copy(sas[rows[c], :], PS[rows[c], 3, :]).then_inc(S_("sas_ready"), 1)

            def act_levels(act, i, levels, lora_of=None):
                act_T(act, i, 0, levels)
                if lora_of:
                    act_lora(act, *lora_of)
                for l in range(1, levels):
                    act_X(act, i, l)
                    if l < levels - 1:
                        act_T(act, i, l, levels)

            def act_pair(act, i, bf):
                act_turned(act, i)
                act_levels(act, i, LEVELS, (i + 1, 1 - bf))
                act_scan(act, i, 0)
                act_rates(act, i + 1)
                act_gate(act, i + 1, 1 - bf)
                act_scan(act, i, 1)
                act_decays(act, i + 1, 1 - bf, 2)

            @block.scalar
            def _(act):
                act.wait_ge(S_("U_ready"), 1)
                act_lora(act, 0, 0)
                act_rates(act, 0)
                act_gate(act, 0, 0)
                act_decays(act, 0, 0, 2)
                with act.Fori(0, NT // 2 - 1) as m:
                    for bf in range(2):
                        act_pair(act, 2 * m + bf, bf)
                act_pair(act, NT - 2, 0)
                act_turned(act, NT - 1)
                act_levels(act, NT - 1, LEVELS)
                for c in range(2):
                    act_scan(act, NT - 1, c)
                act.wait_ge(S_("U_turns"), 1)
                act.copy(xs[0:WN, :], B(2, slice(0, WN), slice(0, 512))).then_inc(S_("U_turned"), 1)
                act.wait_ge(S_("o_w_ready"), NT)
                for h in range(WH):
                    act.wait_ge(S_("state_turns"), h + 1)
                    act.copy(Us[:, h], B(4 + h % 4, slice(0, WN), slice(0, 512)).rearrange("p (b n) -> p b n", b=DB)).then_inc(S_("state_turned"), 1)
                act_lora(act, NT, 0)
                act_rates(act, NT)
                act_gate(act, NT, 0)
                act_decays(act, NT, 0, DB)
                act.wait_ge(S_("Ss_stored"), 16)
                act_turned(act, NT)
                act_levels(act, NT, LEVELS_S)
                act.wait_ge(S_("states_stored"), 32)
                act.wait_ge(S_("x_done"), 2 * NT + 1)
                act.copy(xs[0:NS, :], PS[0:NS, 6, :]).then_inc(S_("xs_ready"), 1)
                act.wait_ge(S_("sa_done"), 2 * NT + 1)
                act.copy(sas[0:NS, :], PS[0:NS, 7, :]).then_inc(S_("sas_ready"), 1)
                act.wait_ge(S_("y_s_done"), 1)
                for h in range(WH):
                    act.wait_ge(S_("back_turns"), h + 1)
                    act.copy(Uv[:, :, h, :], B(3 + h % 2, slice(0, WN), slice(0, 512)).rearrange("p (b n) -> p b n", b=DB)).then_inc(S_("Us_turned"), 1)

            def passed(pe):
                pe.sem_inc(S_("passed"), 1)

            def p_turn_qk(pe, j):
                pe.wait_ge(S_("qk_ready"), j + 1)
                passed(pe)
                for n in range(2 * RH):
                    ins = pe.transpose(B(6 + n // 4, slice(0, RDK), slice(n % 4 * P, n % 4 * P + P)), qk[:, n, :], ident[:])
                ins.then_inc(S_("qkT"), 1)

            def p_turn_lora(pe, j):
                pe.wait_ge(S_("lora_ready"), j + 1)
                passed(pe)
                for n in range(2):
                    pe.transpose(B(6, slice(0, 64), slice(n * P, (n + 1) * P)), lora[:, 64 * n:64 * n + 64], ident[:])
                pe.transpose(B(6, slice(0, P), slice(256, 384)), lora[:, 128:256], ident[:]).then_inc(S_("loraT"), 1)

            def p_rates(pe, j):
                pe.wait_ge(S_("loraT_ready"), j + 1)
                pe.matmul(B(6), loT[:, 0, :], w2[:], start=True, stop=True)
                pe.matmul(B(7), loT[:, 1, :], a2[:], start=True, stop=True).then_inc(S_("rates"), 1)

            def p_gate_att(pe, j):
                pe.matmul(B(4), hgT[:], g2[:], start=True, stop=True).then_inc(S_("g_done"), 1)
                for h in range(RH):
                    ins = pe.matmul(B(5, slice(0, P), slice(h * P, h * P + P)), qkT[:, RH + h, :], qkT[:, h, :], start=True, stop=True)
                ins.then_inc(S_("att_done"), 1)

            def p_retention(pe, j, bf):
                pe.wait_ge(S_("att_ready"), j + 1)
                pe.wait_ge(S_("z_ready"), j + 1)
                pe.wait_ge(S_("S_ready"), j + 1)
                for h in range(RH):
                    vh = stage[:, bf, V_R, h * RDV:(h + 1) * RDV]
                    pe.matmul(B(6, slice(0, P), slice(h * P, h * P + P)), att[:, h, :], vh, start=True, stop=False)
                    pe.matmul(B(6, slice(0, P), slice(h * P, h * P + P)), qkT[:, h, :], S[:, h, :], start=False, stop=True)
                    ins = pe.matmul(B(7, slice(0, RDK), slice(h * P, h * P + P)), qk[:, RH + h, :], vh, start=True, stop=True)
                ins.then_inc(S_("ret_done"), 1)

            def p_decays(pe, j, nch):
                pe.wait_ge(S_("gate_copied"), j + 1)
                pe.wait_ge(S_("lw_ready"), j + 1)
                pe.matmul(B(4), masks[:, 1, :], lw[:], start=True, stop=True)
                for h in range(WH):
                    ins = pe.matmul(B(5, slice(0, WN), slice(h * nch, (h + 1) * nch)), lw[:, h * WN:(h + 1) * WN], chunk[:, 0:nch], start=True, stop=True)
                ins.then_inc(S_("L_ready"), 1)

            def p_turn_heads(pe, i, bf):
                pe.wait_ge(S_("arbk_ready"), i + 1)
                passed(pe)
                for h in range(WH):
                    if h >= 4:
                        pe.wait_ge(S_("T4_ready_act" if h % 2 else "T4_ready_dve"), 4 * i + (h - 4) // 2 + 1)
                        passed(pe)
                    for n in range(4):
                        ins = pe.transpose(B(h % 4, slice(0, WN), slice(n * P, n * P + P)), stage[:, bf, n, h * WN:(h + 1) * WN], ident[:])
                    ins.then_inc(S_("headT"), 1)

            def p_products(pe, i):
                for h in range(WH):
                    pe.wait_ge(S_("T4_ready_act" if h % 2 else "T4_ready_dve"), 4 * i + h // 2 + 1)
                    if h >= 4:
                        pe.wait_ge(S_("M4_ready"), WH * i + h - 3)
                    ar = T4[:, h, 0:2, :]
                    pe.matmul(B(4 + h % 4, slice(0, P), slice(0, 256)), T4[:, h, 2, :], ar, start=True, stop=True)
                    pe.matmul(B(4 + h % 4, slice(0, P), slice(256, 512)), T4[:, h, 3, :], ar, start=True, stop=True).then_inc(S_("products"), 1)

            def p_turn_T(pe, i, l):
                for g in range(2):
                    if l:
                        pe.wait_ge(S_("TT_ready"), 2 * updates_before(i) + 2 * (l - 1) + g + 1)
                    else:
                        pe.wait_ge(S_("TT_first"), 2 * i + g + 1)
                    for h in range(4):
                        ins = pe.transpose(B(2 + g, slice(0, P), slice(h * P, h * P + P)), TT[:, g, h, :], ident[:])
                    ins.then_inc(S_("T_turned"), 1)

            def p_level(pe, i, l, levels):
                n0 = 2 * updates_before(i) + 2 * (l - 1)
                for g in range(2):
                    pe.wait_ge(S_("AL_ready"), 2 * levels_before(i) + 2 * l + g + 1)
                    pe.wait_ge(S_("T_ready"), n0 + g + 1)
                    for h in range(4):
                        ins = pe.matmul(B(g, slice(0, P), slice(h * P, h * P + P)), AL[:, g, h, :], T[:, g, h, :], start=True, stop=True)
                    ins.then_inc(S_("X_done"), 1)
                for g in range(2):
                    pe.wait_ge(S_("X_ready"), n0 + g + 1)
                    for h in range(4):
                        ins = pe.matmul(B(4 + g, slice(0, P), slice(h * P, h * P + P)), X[:, g, h, :], TT[:, g, h, :], start=True, stop=True)
                    ins.then_inc(S_("dTT"), 1)
                if l < levels - 1:
                    p_turn_T(pe, i, l)

            hcol = [slice(h * WN, (h + 1) * WN) for h in range(WH)]

            def p_scan_x(pe, i, c, bf):
                r = rows[c]
                pe.wait_ge(S_("U_ready"), 2 * i + c + 1)
                passed(pe)
                for h in range(WH):
                    pe.matmul(PS[r, 2, hcol[h]], M4[:, h, 2, r], stage[:, bf, V_W, hcol[h]], start=True, stop=False)
                    ins = pe.matmul(PS[r, 2, hcol[h]], T4[:, h, 0, r], U[:, h, :], start=False, stop=True)
                ins.then_inc(S_("x_done"), 1)

            def p_scan_sa(pe, i, c):
                r = rows[c]
                pe.wait_ge(S_("xs_ready"), 2 * i + c + 1)
                passed(pe)
                for h in range(WH):
                    ins = pe.matmul(PS[r, 3, hcol[h]], TT[r, h // 4, h % 4, r], xs[r, hcol[h]], start=True, stop=True)
                ins.then_inc(S_("sa_done"), 1)

            def p_scan_u(pe, i, c, bf):
                r = rows[c]
                pe.wait_ge(S_("sas_ready"), 2 * i + c + 1)
                passed(pe)
                for h in range(WH):
                    vh = stage[:, bf, V_W, hcol[h]]
                    pe.matmul(PS[0:WN, 1, hcol[h]], stage[r, bf, 2, hcol[h]], sas[r, hcol[h]], start=True, stop=False)
                    pe.matmul(PS[0:WN, 1, hcol[h]], stage[r, bf, 3, hcol[h]], stage[r, bf, V_W, hcol[h]], start=False, stop=True)
                    pe.matmul(PS[r, 0, hcol[h]], T4[:, h, 1, r], U[:, h, :], start=True, stop=False)
                    pe.matmul(PS[r, 0, hcol[h]], M4[:, h, 1, r], sas[:, hcol[h]], start=False, stop=False)
                    ins = pe.matmul(PS[r, 0, hcol[h]], M4[:, h, 3, r], vh, start=False, stop=True)
                ins.then_inc(S_("U_products"), 1)

            def pe_pair(pe, i, bf):
                p_turn_heads(pe, i, bf)
                p_products(pe, i)
                p_turn_T(pe, i, 0)
                p_level(pe, i, 1, LEVELS)
                p_level(pe, i, 2, LEVELS)
                p_turn_qk(pe, i + 1)
                p_level(pe, i, 3, LEVELS)
                pe.wait_ge(S_("qkT_ready"), i + 2)
                p_turn_lora(pe, i + 1)
                p_level(pe, i, 4, LEVELS)
                p_rates(pe, i + 1)
                p_level(pe, i, 5, LEVELS)
                pe.wait_ge(S_("TT_ready"), 2 * updates_before(i) + 2 * (LEVELS - 1))
                p_scan_x(pe, i, 0, bf)
                p_gate_att(pe, i + 1)
                p_scan_sa(pe, i, 0)
                p_scan_u(pe, i, 0, bf)
                p_scan_x(pe, i, 1, bf)
                p_scan_sa(pe, i, 1)
                p_scan_u(pe, i, 1, bf)
                p_retention(pe, i + 1, 1 - bf)
                p_decays(pe, i + 1, 2)
                pe.wait_ge(S_("y_read"), i + 1)
                pe.wait_ge(S_("S_ready"), i + 3)

            def pe_a(pe, j, bf, nch, retention):
                p_turn_qk(pe, j)
                pe.wait_ge(S_("qkT_ready"), j + 1)
                p_turn_lora(pe, j)
                p_rates(pe, j)
                p_gate_att(pe, j)
                retention()
                p_decays(pe, j, nch)

            def retention_sample(pe):
                pe.wait_ge(S_("att_ready"), NT + 1)
                pe.wait_ge(S_("z_ready"), NT + 1)
                for h in range(RH):
                    pe.wait_ge(S_("ret_ex"), h + 1)
                    if h >= 2:
                        pe.wait_ge(S_("Ss_ready"), h - 1)
                    col = slice(h * P, h * P + P)
                    pe.matmul(B(6, slice(0, NS), col), att[0:NS, h, 0:NS], stage[0:NS, 0, V_R, h * RDV:(h + 1) * RDV], start=True, stop=False)
                    for b in range(DB):
                        pe.matmul(B(6, slice(0, NS), col), ex_k[:, h % 2, 0, b, :], Ss[:, b, h, :], start=False, stop=b == DB - 1)
                    for j in range(2):
                        ins = pe.matmul(B(2 * (h % 2) + j, slice(0, RDK), slice(0, 512)), qk[0:NS, RH + h, :],
                                        ex_t[:, h % 2, 4 * j:4 * j + 4, :], start=True, stop=True)
                    ins.then_inc(S_("ret_s_done"), 1)
                pe.wait_ge(S_("ro_s"), 1)

            def turn_back(pe, h):
                pe.wait_ge(S_("Us_ready"), h + 1)
                if h >= 2:
                    pe.wait_ge(S_("Us_turned"), h - 1)
                for b in range(DB):
                    ins = pe.transpose(B(3 + h % 2, slice(0, WN), slice(b * WN, (b + 1) * WN)), Us[:, h, b, :], ident[0:WN, 0:WN])
                ins.then_inc(S_("back_turns"), 1)

            @block.tensor
            def _(pe):
                pe.wait_ge(c_loaded, 16 * N_CONST)
                pe_a(pe, 0, 0, 2, lambda: p_retention(pe, 0, 0))
                pe.wait_ge(S_("S_ready"), 2)
                with pe.Fori(0, NT // 2 - 1) as m:
                    for bf in range(2):
                        pe_pair(pe, 2 * m + bf, bf)
                pe_pair(pe, NT - 2, 0)
                i, bf = NT - 1, 1
                p_turn_heads(pe, i, bf)
                p_products(pe, i)
                p_turn_T(pe, i, 0)
                for l in range(1, LEVELS):
                    p_level(pe, i, l, LEVELS)
                pe.wait_ge(S_("TT_ready"), 2 * updates_before(i) + 2 * (LEVELS - 1))
                for c in range(2):
                    p_scan_x(pe, i, c, bf)
                    p_scan_sa(pe, i, c)
                    p_scan_u(pe, i, c, bf)
                pe.wait_ge(S_("U_ready"), 2 * NT + 1)
                for h in range(WH):
                    ins = pe.transpose(B(2, slice(0, WN), slice(h * WN, (h + 1) * WN)), U[:, h, :], ident[0:WN, 0:WN])
                ins.then_inc(S_("U_turns"), 1)
                pe.wait_ge(states, 32)
                for h in range(WH):
                    if h >= 4:
                        pe.wait_ge(S_("state_turned"), h - 3)
                    for b in range(DB):
                        ins = pe.transpose(B(4 + h % 4, slice(0, WN), slice(b * WN, (b + 1) * WN)), Uv[:, b, h, :], ident[0:WN, 0:WN])
                    ins.then_inc(S_("state_turns"), 1)
                pe.wait_ge(S_("U_turned"), 1)
                pe.wait_ge(S_("state_turned"), WH)
                pe.wait_ge(c_loaded, 16 * (N_CONST + 2))
                pe.wait_ge(loaded, 48 * (NT + 1))
                pe_a(pe, NT, 0, DB, lambda: retention_sample(pe))
                pe.wait_ge(S_("y_read"), NT)
                p_turn_heads(pe, NT, 0)
                p_products(pe, NT)
                p_turn_T(pe, NT, 0)
                for l in range(1, LEVELS_S):
                    p_level(pe, NT, l, LEVELS_S)
                hs = [slice(h * WN, (h + 1) * WN) for h in range(WH)]
                vh = [stage[0:NS, 0, V_W, h * WN:(h + 1) * WN] for h in range(WH)]
                r = slice(0, NS)
                pe.wait_ge(S_("TT_ready"), 2 * updates_before(NT) + 2 * (LEVELS_S - 1))
                for h in range(WH):
                    pe.wait_ge(S_("scan_ex_k"), h + 1)
                    pe.matmul(PS[r, 6, hs[h]], M4[r, h, 2, r], vh[h], start=True, stop=False)
                    for b in range(DB):
                        pe.matmul(PS[r, 6, hs[h]], ex_k[:, h % 2, 0, b, :], Us[:, h, b, :], start=False, stop=b == DB - 1)
                    pe.matmul(PS[r, 0, hs[h]], M4[r, h, 3, r], vh[h], start=h == 0, stop=False, skip_group_check=True)
                    for b in range(DB):
                        ins = pe.matmul(PS[r, 0, hs[h]], ex_k[:, h % 2, 1, b, :], Us[:, h, b, :], start=False, stop=False, skip_group_check=True)
                    ins.then_inc(S_("scan_s_x" if h < WH - 1 else "x_done"), 1)
                pe.wait_ge(S_("xs_ready"), 2 * NT + 1)
                for h in range(WH):
                    ins = pe.matmul(PS[r, 7, hs[h]], TT[r, h // 4, h % 4, r], xs[r, hs[h]], start=True, stop=True)
                ins.then_inc(S_("sa_done"), 1)
                pe.wait_ge(S_("sas_ready"), 2 * NT + 1)
                for h in range(WH):
                    ins = pe.matmul(PS[r, 0, hs[h]], M4[r, h, 1, r], sas[r, hs[h]], start=False, stop=True, skip_group_check=True)
                ins.then_inc(S_("y_s_done"), 1)
                for h in range(WH):
                    pe.wait_ge(S_("scan_ex_t"), h + 1)
                    if h >= 2:
                        pe.wait_ge(S_("Us_ready"), h - 1)
                    bank = 1 + h % 2
                    pe.matmul(PS[0:WN, bank, :], stage[r, 0, 2, hs[h]], ex_t[:, h % 2, :, 0:WN], start=True, stop=False)
                    pe.matmul(PS[0:WN, bank, :], stage[r, 0, 3, hs[h]], ex_t[:, h % 2, :, WN:2 * WN], start=False, stop=True).then_inc(S_("scan_s_u"), 1)
                    if h >= 1:
                        turn_back(pe, h - 1)
                turn_back(pe, WH - 1)




def phase_memory_kv(core, PS, kT, Vm):
    nc, d, sem = core.nc, core.dram, core.sem
    MT = NMEM // P
    S_ = lambda n: sem("kv_" + n)
    with ExitStack() as ctx:
        sb = lambda n, s, t=F32: ctx.enter_context(nc.sbuf_tensor("kv_" + n, s, t))
        w = sb("w", [P, 2, KC, D])
        x, sq, xT = sb("x", [P, MT, D]), sb("sq", [P, D]), sb("xT", [P, MT, KC, P])
        g, ident, st, expo, kt = sb("g", [P, KC]), sb("ident", [P, P]), sb("st", [P, 8]), sb("expo", [P, MT]), sb("k", [P, MT, D])
        with nc.Block() as block:
            @block.sync
            def _(sp):
                sp.dma_start(x[:], d["mem_prompt"][0].rearrange("(m p) n -> p m n", p=P)).then_inc(S_("small"), 16)
                sp.dma_start(ident[:], d["ident"]).then_inc(S_("small"), 16)
                with nc.allow_non_contiguous_dma(reason="a gain by channel"):
                    sp.dma_start(g[:], d["g_mem_kv"][0].rearrange("(c p) -> p c", p=P)).then_inc(S_("small"), 16)
                for j, n in enumerate(("w_mk", "w_mv")):
                    wv = d[n][0].rearrange("(c p) n -> p c n", p=P)
                    for hf in range(2):
                        sp.dma_start(w[:, j, :, hf * 512:hf * 512 + 512], wv[:, :, hf * 512:hf * 512 + 512]).then_inc(S_(f"w{j}{hf}"), 16)
                sp.wait_ge(S_("k_ready"), 4)
                sp.dma_start(d["out_mk"].rearrange("(m p) n -> p m n", p=P), kt[:]).then_inc(S_("stored"), 16)
                sp.wait_ge(S_("v_ready"), 4)
                sp.dma_start(d["out_mv"].rearrange("(m p) n -> p m n", p=P), Vm[:]).then_inc(S_("stored"), 16)
                sp.wait_ge(S_("stored"), 32)

            @block.vector
            def _(v):
                lk = Steps(v, S_("dve"))
                v.wait_ge(S_("small"), 48)
                for m in range(MT):
                    lk(v.tensor_tensor_reduce(sq[:], x[:, m], x[:, m], 1.0, 0.0, ALU.mult, ALU.add, st[:, m:m + 1]))
                v.tensor_scalar(st[:, 2:4], st[:, 0:2], 1.0 / D, EPS, ALU.mult, ALU.add).then_inc(S_("ms"), 1)
                v.wait_ge(S_("rstd"), 1)
                for m in range(MT):
                    v.tensor_scalar(x[:, m], x[:, m], st[:, 4 + m:5 + m], None, ALU.mult).then_inc(S_("xn"), 1)
                for m in range(MT):
                    for b in range(2):
                        v.wait_ge(S_("turned"), 2 * m + b + 1)
                        v.tensor_tensor(xT[:, m, 4 * b:4 * b + 4, :], PS[:, 2 * m + b, :].rearrange("p (c t) -> p c t", c=4),
                                        g[:, 4 * b:4 * b + 4].unsqueeze(2).to_broadcast([P, 4, P]), ALU.mult).then_inc(S_("xT"), 1)
                for n in range(4):
                    v.wait_ge(S_("k_turned"), n + 1)
                    v.tensor_copy(kT[:, 4 * (n % 2):4 * (n % 2) + 4, (n // 2) * P:(n // 2) * P + P],
                                  PS[:, n, :].rearrange("p (c t) -> p c t", c=4)).then_inc(S_("kT"), 1)

            @block.gpsimd
            def _(po):
                po.memset(expo[:], -0.5).then_inc(S_("expo"), 1)
                po.wait_ge(S_("expo"), 1)
                po.wait_ge(S_("ms"), 1)
                po.tensor_tensor(st[:, 4:6], st[:, 2:4], expo[:], ALU.pow).then_inc(S_("rstd"), 1)

            @block.tensor
            def _(pe):
                for m in range(MT):
                    pe.wait_ge(S_("xn"), m + 1)
                    for c in range(KC):
                        ins = pe.transpose(PS[:, 2 * m + c // 4, c % 4 * P:c % 4 * P + P], x[:, m, c * P:(c + 1) * P], ident[:])
                        if c % 4 == 3:
                            ins.then_inc(S_("turned"), 1)
                for j in range(2):
                    for hf in range(2):
                        pe.wait_ge(S_(f"w{j}{hf}"), 16)
                        for m in range(MT):
                            pe.wait_ge(S_("xT"), 2 * m + 2)
                            if j == 1:
                                pe.wait_ge(S_("k_ready"), 2 * hf + m + 1)
                            for k in range(KC):
                                ins = pe.matmul(PS[:, 4 + 2 * hf + m, :], xT[:, m, k, :], w[:, j, k, hf * 512:hf * 512 + 512], start=k == 0, stop=k == KC - 1)
                            ins.then_inc(S_("projected"), 1)
                    if j == 0:
                        pe.wait_ge(S_("k_ready"), 4)
                        pe.wait_ge(S_("xT"), 4)
                        for m in range(MT):
                            for c in range(KC):
                                ins = pe.transpose(PS[:, 2 * m + c // 4, c % 4 * P:c % 4 * P + P], kt[:, m, c * P:(c + 1) * P], ident[:])
                                if c % 4 == 3:
                                    ins.then_inc(S_("k_turned"), 1)

            @block.scalar
            def _(act):
                for j in range(2):
                    for hf in range(2):
                        for m in range(MT):
                            act.wait_ge(S_("projected"), 4 * j + 2 * hf + m + 1)
                            dst = (kt, Vm)[j][:, m, hf * 512:hf * 512 + 512]
                            act.copy(dst, PS[:, 4 + 2 * hf + m, :]).then_inc(S_("k_ready" if j == 0 else "v_ready"), 1)


def phase_attention(core, PS, kT, Vm):
    nc, d, sem = core.nc, core.dram, core.sem
    S_ = lambda n: sem("at_" + n)
    NR = NG + NE
    SC = MDH ** -0.5
    with ExitStack() as ctx:
        sb = lambda n, s, t=F32: ctx.enter_context(nc.sbuf_tensor("at_" + n, s, t))
        w = sb("w", [P, 3, KC, D])
        wr = sb("wr", [P, KC, NR])
        br, gf = sb("br", [P, NR]), sb("gf", [P, D])
        g, ident, expo = sb("g", [P, KC]), sb("ident", [P, P]), sb("expo", [P, 1])
        mt, h, q = sb("mt", [P, D]), sb("h", [P, D]), sb("q", [P, D])
        sq = sb("sq", [P, D])
        aT, qT = sb("aT", [P, KC, P]), sb("qT", [P, KC, P])
        p, lg, st = sb("p", [P, MH, NMEM]), sb("lg", [P, NR]), sb("st", [P, 24])
        kc, kcT = sb("kc", [P, 2, 2, D]), sb("kcT", [P, KC, NMEM])
        sT = sb("sT", [P, 2, 256])
        flat = lambda ap: ap.rearrange("p c t -> p (c t)")
        two = lambda b: PS[:, b:b + 2, :].rearrange("p a (c t) -> p (a c) t", t=P)

        with nc.Block() as block:
            @block.sync
            def _(sp):
                def load(at):
                    sp.dma_start(h[:], d["x"][bass.ds(at, P), :]).then_inc(S_("loaded"), 16)
                    sp.dma_start(mt[:], d["mixed"][bass.ds(at, P), :]).then_inc(S_("loaded"), 16)

                with nc.allow_non_contiguous_dma(reason="small"):
                    for dst, src in [(ident[:], d["ident"]), (g[:], d["g_mem_q"][0].rearrange("(c p) -> p c", p=P)),
                                     (wr[:, :, 0:NG], d["w_group_router"][0].rearrange("(c p) n -> p c n", p=P)),
                                     (wr[:, :, NG:NR], d["w_expert_router"][0].rearrange("(c p) n -> p c n", p=P)),
                                     (br[:, 0:NG], wide_row(d["b_group_router"][0], NG)), (br[:, NG:NR], wide_row(d["b_expert_router"][0], NE)),
                                     (gf[:], wide_row(d["g_ffn"][0], D))]:
                        sp.dma_start(dst, src).then_inc(S_("small"), 16)
                for j, n in enumerate(("w_out", "w_mq", "w_mo")):
                    sp.dma_start(w[:, j], d[n][0].rearrange("(c p) n -> p c n", p=P)).then_inc(S_(f"w{j}"), 16)

                def stores(at, i):
                    sp.wait_ge(S_("h2_ready"), i + 1)
                    sp.dma_start(d["h2"][bass.ds(at, P), :], h[:]).then_inc(S_("h2_stored"), 16)
                    sp.wait_ge(S_("hn_ready"), i + 1)
                    sp.dma_start(d["hn"][bass.ds(at, P), :], mt[:]).then_inc(S_("hn_stored"), 16)
                    sp.wait_ge(S_("lg_ready"), i + 1)
                    sp.dma_start(d["logits"][bass.ds(at, P), :], lg[:]).then_inc(S_("lg_stored"), 16)

                with sp.Fori(0, NT) as i:
                    sp.wait_ge(S_("h2_stored"), 16 * i)
                    sp.wait_ge(S_("hn_stored"), 16 * i)
                    sp.wait_ge(S_("turned3"), i)
                    load(i * P)
                    stores(i * P, i)
                sp.wait_ge(S_("h2_stored"), 16 * NT)
                sp.wait_ge(S_("hn_stored"), 16 * NT)
                load(SEQ)
                for half, name in enumerate(("cache_mem_k", "cache_mem_v")):
                    for b in range(DB):
                        if half == 0 and b >= 2:
                            sp.wait_ge(S_("kc_turned"), b - 1)
                        if half == 1 and b < 2:
                            sp.wait_ge(S_("kc_turned"), DB - 1 + b)
                        if half == 1 and b >= 2:
                            sp.wait_ge(S_("cache_used"), b - 1)
                        sp.dma_start(kc[:, b % 2], d[name][0, b].rearrange("(m p) h n -> p m (h n)", p=P)).then_inc(S_(f"cache_loaded{b % 2}"), 16)
                stores(SEQ, NT)
                for n in ("h2_stored", "hn_stored", "lg_stored"):
                    sp.wait_ge(S_(n), 16 * TILES)

            def rms(v, i, src, k, lk):
                lk(v.tensor_tensor_reduce(sq[:], src, src, 1.0, 0.0, ALU.mult, ALU.add, st[:, 0:1]))
                v.tensor_scalar(st[:, 1:2], st[:, 0:1], 1.0 / D, EPS, ALU.mult, ALU.add).then_inc(S_("ms"), 1)
                v.wait_ge(S_("rstd"), 2 * i + k + 1)

            def dve_front(v, i, lk):
                v.wait_ge(S_("turned0"), i + 1)
                v.tensor_copy(aT[:], two(0)).then_inc(S_("aT0"), 1)
                v.wait_ge(S_("proj0"), i + 1)
                lk(v.tensor_tensor(h[:], h[:], PS[:, 2:4, :].rearrange("p a n -> p (a n)"), ALU.add))
                rms(v, i, h[:], 0, lk)
                v.tensor_scalar(mt[:], h[:], st[:, 2:3], None, ALU.mult).then_inc(S_("hq"), 1)
                v.wait_ge(S_("turned1"), i + 1)
                v.tensor_tensor(aT[:], two(0), g[:].unsqueeze(2).to_broadcast([P, KC, P]), ALU.mult).then_inc(S_("aT1"), 1)
                v.wait_ge(S_("turned2"), i + 1)
                v.tensor_copy(qT[:], two(0)).then_inc(S_("qT"), 1)

            def dve_softmax(v, i, lk, n, bank):
                v.wait_ge(S_("scores"), i + 1)
                src = PS[:, bank:bank + 2, :].rearrange("p a (b m) -> p (a b) m", m=NMEM)[:, 0:n, :]
                lk(v.tensor_reduce(st[:, 4:4 + n], src, AX.X, ALU.max))
                v.tensor_scalar(st[:, 8:8 + n], st[:, 4:4 + n], -SC, None, ALU.mult).then_inc(S_("nmax"), 1)
                v.wait_ge(S_("exps"), i + 1)
                lk(v.reciprocal(st[:, 16:16 + n], st[:, 12:12 + n]))
                v.tensor_tensor(p[:, 0:n, :], p[:, 0:n, :], st[:, 16:16 + n].unsqueeze(2).to_broadcast([P, n, NMEM]), ALU.mult).then_inc(S_("p_ready"), 1)

            def dve_attn(v, i, lk):
                dve_softmax(v, i, lk, MH, 4)
                v.wait_ge(S_("pT_done"), i + 1)
                v.tensor_copy(qT[:], two(0)).then_inc(S_("pT"), 1)
                v.wait_ge(S_("oT_done"), i + 1)
                v.tensor_copy(aT[:], two(2)).then_inc(S_("oT"), 1)

            def dve_attn_sample(v, lk):
                i = NT
                for b in range(DB):
                    v.wait_ge(S_("kc_turned"), b + 1)
                    if b:
                        v.wait_ge(S_("sT_done"), b)
                    v.tensor_copy(kcT[:].rearrange("p c (m t) -> p m c t", m=2),
                                  PS[:, 0:4, :].rearrange("p (m a) (c t) -> p m (a c) t", m=2, t=P)).then_inc(S_("kcT"), 1)
                v.wait_ge(S_("sT_done"), DB)
                v.tensor_copy(sT[:].rearrange("p m n -> p (m n)"), PS[:, 4, :]).then_inc(S_("sT"), 1)
                dve_softmax(v, i, lk, 2, 6)
                v.wait_ge(S_("pT_done"), i + 1)
                v.tensor_copy(sT[:].rearrange("p m n -> p (m n)"), PS[:, 0, :]).then_inc(S_("pT"), 1)
                v.wait_ge(S_("oT_done"), i + 1)
                v.tensor_copy(aT[:, :, 0:NS], PS[:, 2, :].rearrange("p (c t) -> p c t", c=KC)).then_inc(S_("oT"), 1)

            def dve_back(v, i, lk):
                v.wait_ge(S_("proj2"), i + 1)
                v.tensor_tensor(h[:], h[:], PS[:, 4:6, :].rearrange("p a n -> p (a n)"), ALU.add).then_inc(S_("h2_ready"), 1)
                v.wait_ge(S_("h2_ready"), i + 1)
                rms(v, i, h[:], 1, lk)
                lk(v.tensor_scalar(mt[:], h[:], st[:, 2:3], None, ALU.mult))
                v.tensor_tensor(mt[:], mt[:], gf[:], ALU.mult).then_inc(S_("hn_ready"), 1)
                v.wait_ge(S_("turned3"), i + 1)
                v.tensor_copy(aT[:], two(0)).then_inc(S_("aT3"), 1)
                v.wait_ge(S_("routed"), i + 1)
                v.wait_ge(S_("lg_stored"), 16 * i)
                v.tensor_tensor(lg[:], PS[:, 6, 0:NR], br[:], ALU.add).then_inc(S_("lg_ready"), 1)

            @block.vector
            def _(v):
                v.wait_ge(S_("small"), 16 * 7)
                with v.Fori(0, NT) as i:
                    lk = Steps(v, S_("dve"), i * PER_AT)
                    v.wait_ge(S_("loaded"), 32 * i + 32)
                    dve_front(v, i, lk)
                    dve_attn(v, i, lk)
                    dve_back(v, i, lk)
                    assert lk.n == PER_AT, lk.n
                lk = Steps(v, S_("dve"), NT * PER_AT)
                v.wait_ge(S_("loaded"), 32 * TILES)
                dve_front(v, NT, lk)
                dve_attn_sample(v, lk)
                dve_back(v, NT, lk)

            @block.gpsimd
            def _(po):
                po.memset(expo[:], -0.5).then_inc(S_("expo"), 1)
                po.wait_ge(S_("expo"), 1)
                with po.Fori(0, 2 * TILES) as i:
                    po.wait_ge(S_("ms"), i + 1)
                    po.tensor_tensor(st[:, 2:3], st[:, 1:2], expo[:], ALU.pow).then_inc(S_("rstd"), 1)

            @block.scalar
            def _(act):
                def body(i, n, bank):
                    act.wait_ge(S_("proj1"), i + 1)
                    act.copy(q[:], PS[:, 2:4, :].rearrange("p a n -> p (a n)")).then_inc(S_("q_ready"), 1)
                    act.wait_ge(S_("nmax"), i + 1)
                    for j in range(n):
                        ins = act.activation(p[:, j, :], PS[:, bank + j // 2, j % 2 * NMEM:(j % 2 + 1) * NMEM], ACT.Exp,
                                             bias=st[:, 8 + j:9 + j], scale=SC, accum_out=st[:, 12 + j:13 + j])
                    ins.then_inc(S_("exps"), 1)
                with act.Fori(0, NT) as i:
                    body(i, MH, 4)
                body(NT, 2, 6)

            def turn(pe, src, bank):
                for c in range(KC):
                    ins = pe.transpose(PS[:, bank + c // 4, c % 4 * P:c % 4 * P + P], src[:, c * P:(c + 1) * P], ident[:])
                return ins

            def project(pe, j, bank, src):
                for hf in range(2):
                    for k in range(KC):
                        ins = pe.matmul(PS[:, bank + hf, :], src[:, k, :], w[:, j, k, hf * 512:hf * 512 + 512], start=k == 0, stop=k == KC - 1)
                return ins

            def pe_front(pe, i):
                pe.wait_ge(S_("aT3"), i)
                turn(pe, mt, 0).then_inc(S_("turned0"), 1)
                pe.wait_ge(S_("aT0"), i + 1)
                pe.wait_ge(S_("w0"), 16)
                project(pe, 0, 2, aT).then_inc(S_("proj0"), 1)
                pe.wait_ge(S_("hq"), i + 1)
                turn(pe, mt, 0).then_inc(S_("turned1"), 1)
                pe.wait_ge(S_("aT1"), i + 1)
                pe.wait_ge(S_("w1"), 16)
                project(pe, 1, 2, aT).then_inc(S_("proj1"), 1)
                pe.wait_ge(S_("q_ready"), i + 1)
                turn(pe, q, 0).then_inc(S_("turned2"), 1)
                pe.wait_ge(S_("qT"), i + 1)

            def pe_attn(pe, i):
                for hd in range(MH):
                    for c in range(2):
                        ins = pe.matmul(PS[:, 4 + hd // 2, hd % 2 * NMEM:(hd % 2 + 1) * NMEM], qT[:, 2 * hd + c, :], kT[:, 2 * hd + c, :],
                                        start=c == 0, stop=c == 1)
                ins.then_inc(S_("scores"), 1)
                pe.wait_ge(S_("p_ready"), i + 1)
                turn(pe, p[:].rearrange("p h m -> p (h m)"), 0).then_inc(S_("pT_done"), 1)
                pe.wait_ge(S_("pT"), i + 1)
                for cc in range(KC):
                    for m in range(2):
                        ins = pe.matmul(PS[:, 2 + cc // 4, cc % 4 * P:cc % 4 * P + P], Vm[:, m, cc * P:(cc + 1) * P], qT[:, cc // 2 * 2 + m, :],
                                        start=m == 0, stop=m == 1)
                ins.then_inc(S_("oT_done"), 1)

            def pe_attn_sample(pe):
                i = NT
                for b in range(DB):
                    pe.wait_ge(S_(f"cache_loaded{b % 2}"), 16 * (b // 2 + 1))
                    pe.wait_ge(S_("kcT"), b)
                    for m in range(2):
                        ins = turn(pe, kc[:, b % 2, m], 2 * m)
                    ins.then_inc(S_("kc_turned"), 1)
                    pe.wait_ge(S_("kcT"), b + 1)
                    for m in range(2):
                        for hd in range(MH):
                            col = m * 256 + b * 32 + hd * 8
                            for c in range(2):
                                ins = pe.matmul(PS[:, 4, col:col + 8], kcT[:, 2 * hd + c, m * P:(m + 1) * P], qT[:, 2 * hd + c, b * DS:(b + 1) * DS],
                                                start=c == 0, stop=c == 1)
                    ins.then_inc(S_("sT_done"), 1)
                pe.wait_ge(S_("sT"), 1)
                for gq in range(2):
                    for m in range(2):
                        ins = pe.transpose(PS[:, 6, gq * NMEM + m * P:gq * NMEM + (m + 1) * P], sT[:, m, gq * P:(gq + 1) * P], ident[:])
                ins.then_inc(S_("scores"), 1)
                pe.wait_ge(S_("p_ready"), i + 1)
                for gq in range(2):
                    for m in range(2):
                        ins = pe.transpose(PS[:, 0, (gq * 2 + m) * P:(gq * 2 + m + 1) * P], p[:, gq, m * P:(m + 1) * P], ident[:])
                ins.then_inc(S_("pT_done"), 1)
                pe.wait_ge(S_("pT"), i + 1)
                pT = sT[:].rearrange("p m n -> p (m n)")
                for b in range(DB):
                    pe.wait_ge(S_(f"cache_loaded{b % 2}"), 16 * (DB // 2 + b // 2 + 1))
                    for cc in range(KC):
                        for m in range(2):
                            at = (b // 4 * 2 + m) * P + b % 4 * 32 + cc // 2 * 8
                            ins = pe.matmul(PS[:, 2, cc * NS + b * DS:cc * NS + (b + 1) * DS], kc[:, b % 2, m, cc * P:(cc + 1) * P], pT[:, at:at + 8],
                                            start=m == 0, stop=m == 1)
                    ins.then_inc(S_("cache_used" if b < DB - 1 else "oT_done"), 1)

            def pe_back(pe, i):
                pe.wait_ge(S_("oT"), i + 1)
                pe.wait_ge(S_("w2"), 16)
                project(pe, 2, 4, aT).then_inc(S_("proj2"), 1)
                pe.wait_ge(S_("hn_ready"), i + 1)
                turn(pe, mt, 0).then_inc(S_("turned3"), 1)
                pe.wait_ge(S_("aT3"), i + 1)
                pe.wait_ge(S_("lg_ready"), i)
                for k in range(KC):
                    ins = pe.matmul(PS[:, 6, 0:NR], aT[:, k, :], wr[:, k, :], start=k == 0, stop=k == KC - 1)
                ins.then_inc(S_("routed"), 1)

            @block.tensor
            def _(pe):
                pe.wait_ge(S_("small"), 16 * 7)
                with pe.Fori(0, NT) as i:
                    pe.wait_ge(S_("loaded"), 32 * i + 32)
                    pe_front(pe, i)
                    pe_attn(pe, i)
                    pe_back(pe, i)
                pe.wait_ge(S_("loaded"), 32 * TILES)
                pe_front(pe, NT)
                pe_attn_sample(pe)
                pe_back(pe, NT)


def phase_route(core, PS, dest, comb, slot_tok, over_info):
    nc, d, sem = core.nc, core.dram, core.sem
    S_ = lambda n: sem("rt_" + n)
    NR = NG + NE
    NCNT = 2 * NE + NOVER + EPG + 8
    with ExitStack() as ctx:
        sb = lambda n, s, t=F32: ctx.enter_context(nc.sbuf_tensor("rt_" + n, s, t))
        L, masks, ones, cnt_c = sb("L", [P, TILES, NR]), sb("strict", [P, P]), sb("ones", [P, P]), sb("cnt", [P, NCNT])
        valid, token, zero = sb("valid", [P, TILES]), sb("token", [P, TILES], I32), sb("zero", [P, NBLK], I32)
        s = sb("s", [P, 12, TILES])
        og, tg = sb("og", [P, TILES, NG]), sb("tg", [P, TILES, NG])
        sel, el, te = sb("sel", [P, TILES, EPG, NG]), sb("el", [P, TILES, EPG]), sb("te", [P, TILES, EPG])
        o1, o2 = sb("o1", [P, TILES, EPG]), sb("o2", [P, TILES, EPG])
        O = sb("O", [P, 2, TILES, NG, EPG])
        M = sb("M", [P, TILES, NE])
        a, b = sb("a", [P, TILES, NE]), sb("b", [P, TILES, NE])
        e32 = sb("e32", [P, 8, NE])
        nbt = sb("nbt", [P, NE, 8])
        own, own2 = sb("own", [P, NOVER, NE]), sb("own2", [P, NOVER, NE])
        df, of = sb("df", [P, 2, TILES]), sb("of", [P, NOVER + 1])
        ebase, eid, ovn, desc, full = (cnt_c[:, 0:NE], cnt_c[:, NE:2 * NE], cnt_c[:, 2 * NE:2 * NE + NOVER],
                                       cnt_c[:, 2 * NE + NOVER:2 * NE + NOVER + EPG], cnt_c[:, 2 * NE + NOVER + EPG:])
        bc = lambda ap, *shape: ap.to_broadcast([P, *shape])
        with nc.Block() as block:
            @block.sync
            def _(sp):
                with nc.allow_non_contiguous_dma(reason="small"):
                    sp.dma_start(L[:], d["logits"].rearrange("(t p) n -> p t n", p=P)).then_inc(S_("in"), 16)
                for dst, src in ((masks[:], d["mask_p"][:, 3, :]), (cnt_c[:], d["count"]), (valid[:], d["valid"]), (token[:], d["token"])):
                    sp.dma_start(dst, src).then_inc(S_("in"), 16)
                sp.dma_start(d["blocks"][NE * P:NBLK * P, :], d["zero_row"][0:1, 0:D].broadcast_to([NOVER * P, D])).then_inc(S_("cleared"), 16)
                sp.wait_ge(S_("cleared"), 16)

            @block.vector
            def _(v):
                lk = Steps(v, S_("dve"))
                tt, red = v.tensor_tensor, v.tensor_reduce
                v.memset(ones[:], 1.0).then_inc(S_("ones"), 1)
                v.wait_ge(S_("in"), 80)

                def pick(dst, src, best, t, n):
                    lk(red(best, src, AX.X, ALU.max))
                    lk(tt(t, src, bc(best.unsqueeze(2), TILES, n), ALU.is_equal))
                    lk(tt(t, t, bc(desc[:, 0:n].unsqueeze(1), TILES, n), ALU.mult))
                    lk(red(s[:, 11], t, AX.X, ALU.max))
                    lk(tt(dst, t, bc(s[:, 11].unsqueeze(2), TILES, n), ALU.is_equal))

                gl = L[:, :, 0:NG]
                pick(og[:], gl, s[:, 0], tg[:], NG)
                tt(tg[:], gl, bc(s[:, 0].unsqueeze(2), TILES, NG), ALU.subtract).then_inc(S_("g_shift"), 1)
                lk(tt(sel[:], L[:, :, NG:NR].rearrange("p t (g e) -> p t e g", g=NG), bc(og[:].unsqueeze(2), TILES, EPG, NG), ALU.mult))
                lk(red(el[:], sel[:], AX.X, ALU.add))
                pick(o1[:], el[:], s[:, 1], te[:], EPG)
                lk(v.scalar_tensor_tensor(el[:], o1[:], -1e30, el[:], ALU.mult, ALU.add))
                pick(o2[:], el[:], s[:, 2], te[:], EPG)
                tt(s[:, 3], s[:, 2], s[:, 1], ALU.subtract).then_inc(S_("e_shift"), 1)
                for k, o in enumerate((o1, o2)):
                    ins = tt(O[:, k], bc(og[:].unsqueeze(3), TILES, NG, EPG), bc(o[:].unsqueeze(2), TILES, NG, EPG), ALU.mult)
                lk(ins)
                O_ = lambda k: O[:, k].rearrange("p t g e -> p t (g e)")
                lk(tt(M[:], O_(0), O_(1), ALU.add))
                tt(M[:], M[:], bc(valid[:].unsqueeze(2), TILES, NE), ALU.mult).then_inc(S_("M_ready"), 1)
                v.wait_ge(S_("exps"), 1)
                lk(red(s[:, 5], tg[:], AX.X, ALU.add))
                lk(v.tensor_scalar(s[:, 6], s[:, 4], 1.0, None, ALU.add))
                lk(tt(s[:, 6], s[:, 6], s[:, 5], ALU.mult))
                lk(v.reciprocal(comb[:, 0], s[:, 6]))
                lk(tt(comb[:, 1], comb[:, 0], s[:, 4], ALU.mult))
                v.wait_ge(S_("ranks"), 1)
                cnt, nb, c0, c1, start, corr = (e32[:, j] for j in range(6))
                lk(v.tensor_copy(cnt, PS[:, 1, 0:NE]))
                lk(v.tensor_copy(b[:].rearrange("p t e -> p (t e)"), PS[:, 0, 0:TILES * NE]))
                lk(tt(nbt[:], bc(cnt.unsqueeze(2), NE, 8), bc(full.unsqueeze(1), NE, 8), ALU.is_gt))
                lk(red(nb, nbt[:], AX.X, ALU.add))
                lk(v.tensor_copy(c0, nb))
                step = 1
                while step < NE:
                    v.tensor_copy(c1[:, 0:step], c0[:, 0:step])
                    lk(tt(c1[:, step:NE], c0[:, step:NE], c0[:, 0:NE - step], ALU.add))
                    c0, c1, step = c1, c0, 2 * step
                lk(tt(start, c0, nb, ALU.subtract))
                lk(v.tensor_scalar(corr, start, float(CAP), float(NE * CAP - CAP), ALU.mult, ALU.add))
                lk(tt(corr, corr, ebase, ALU.subtract))
                lk(v.tensor_scalar(a[:], b[:], float(CAP), None, ALU.is_ge))
                lk(tt(a[:], a[:], bc(corr.unsqueeze(1), TILES, NE), ALU.mult))
                lk(tt(a[:], a[:], b[:], ALU.add))
                lk(tt(a[:], a[:], bc(ebase.unsqueeze(1), TILES, NE), ALU.add))
                for k in range(2):
                    lk(tt(b[:], a[:], O_(k), ALU.mult))
                    lk(red(df[:, k], b[:], AX.X, ALU.add))
                v.tensor_copy(dest[:], df[:]).then_inc(S_("dest"), 1)
                lk(tt(own[:], bc(start.unsqueeze(1), NOVER, NE), bc(ovn.unsqueeze(2), NOVER, NE), ALU.is_le))
                lk(tt(own2[:], bc(c0.unsqueeze(1), NOVER, NE), bc(ovn.unsqueeze(2), NOVER, NE), ALU.is_gt))
                lk(tt(own[:], own[:], own2[:], ALU.mult))
                lk(tt(own[:], own[:], bc(eid.unsqueeze(1), NOVER, NE), ALU.mult))
                lk(red(of[:, 0:NOVER], own[:], AX.X, ALU.add))
                lk(v.tensor_copy(of[:, NOVER:NOVER + 1], c0[:, NE - 1:NE]))
                lk(v.tensor_copy(over_info[:], of[:]))

            @block.scalar
            def _(act):
                act.wait_ge(S_("g_shift"), 1)
                act.activation(tg[:], tg[:], ACT.Exp)
                act.wait_ge(S_("e_shift"), 1)
                act.activation(s[:, 4], s[:, 3], ACT.Exp).then_inc(S_("exps"), 1)

            @block.tensor
            def _(pe):
                pe.wait_ge(S_("ones"), 1)
                pe.wait_ge(S_("M_ready"), 1)
                for t in range(TILES):
                    pe.matmul(PS[:, 0, t * NE:(t + 1) * NE], masks[:], M[:, t, :], start=True, stop=t == 0)
                    for j in range(t):
                        pe.matmul(PS[:, 0, t * NE:(t + 1) * NE], ones[:], M[:, j, :], start=False, stop=j == t - 1)
                for t in range(TILES):
                    ins = pe.matmul(PS[:, 1, 0:NE], ones[:], M[:, t, :], start=t == 0, stop=t == TILES - 1)
                ins.then_inc(S_("ranks"), 1)

            @block.gpsimd
            def _(po):
                po.memset(zero[:], 0).then_inc(S_("zero"), 1)
                po.wait_ge(S_("zero"), 1)
                po.dma_start(d["slots"].rearrange("(p n) o -> p (n o)", p=P), zero[:]).then_inc(S_("slots_zero"), 16)
                po.wait_ge(S_("slots_zero"), 16)
                po.wait_ge(S_("in"), 80)
                po.wait_ge(S_("dest"), 1)
                n = 0
                for k in range(2):
                    for t in range(TILES):
                        rows = P if t < NT else NS
                        po.indirect_dma_start(d["slots"], bass.IndirectOffsetOnAxis(ap=dest[0:rows, k, t:t + 1], axis=0),
                                              token[0:rows, t:t + 1], None).then_inc(S_("scattered"), 16)
                        n += 16
                po.wait_ge(S_("scattered"), n)
                with nc.allow_non_contiguous_dma(reason="a table turned"):
                    po.dma_start(slot_tok[:], d["slots"].rearrange("(b p) o -> p (b o)", p=P)).then_inc(S_("slots_in"), 16)
                po.wait_ge(S_("slots_in"), 16)


def phase_experts(core, PS, slot_tok, over_info):
    nc, d, sem = core.nc, core.dram, core.sem
    S_ = lambda n: sem("ex_" + n)
    HC = DE // P
    with ExitStack() as ctx:
        sb = lambda n, s, t=F32: ctx.enter_context(nc.sbuf_tensor("ex_" + n, s, t))
        wg, wu = sb("wg", [P, 2, KC, DE]), sb("wu", [P, 2, KC, DE])
        wd = sb("wd", [P, 2, HC, D])
        xg, xT = sb("xg", [P, 2, D]), sb("xT", [P, 2, KC, P])
        idx = sb("idx", [P, 2], I32)
        e, h, hT, y = sb("e", [P, 2, DE]), sb("h", [P, 2, DE]), sb("hT", [P, HC, P]), sb("y", [P, 2, D])
        ident = sb("ident", [P, P])
        GATE, UP, HT, OUT = 2, 3, 4, 5

        def weights(n, name):
            return d[name][0][bass.ds(n, 1)].rearrange("a (c p) m -> p (a c) m", p=P)

        def over_blocks(eng, body):
            n_over = eng.value_load(over_info[0:1, NOVER:NOVER + 1], min_val=0, max_val=NOVER)
            with eng.Fori(0, NOVER) as j:
                with eng.If(j < n_over):
                    body(j)

        def gate_up(pe, bf):
            for bank, w in ((GATE, wg), (UP, wu)):
                for k in range(KC):
                    ins = pe.matmul(PS[:, bank, :], xT[:, bf, k, :], w[:, bf, k, :], start=k == 0, stop=k == KC - 1)
            return ins

        def down(pe, bf):
            for hf in range(2):
                for k in range(HC):
                    ins = pe.matmul(PS[:, OUT + hf, :], hT[:, k, :], wd[:, bf, k, hf * 512:hf * 512 + 512], start=k == 0, stop=k == HC - 1)
            return ins

        def turn_rows(pe, bf):
            for c in range(KC):
                ins = pe.transpose(PS[:, c // 4, c % 4 * P:c % 4 * P + P], xg[:, bf, c * P:(c + 1) * P], ident[:])
            return ins

        def turn_h(pe, bf):
            for c in range(HC):
                ins = pe.transpose(PS[:, HT, c * P:(c + 1) * P], h[:, bf, c * P:(c + 1) * P], ident[:])
            return ins

        def silu_up(v, bf, lk):
            lk(v.tensor_scalar(e[:, bf], e[:, bf], 1.0, None, ALU.add))
            lk(v.reciprocal(e[:, bf], e[:, bf]))
            lk(v.tensor_tensor(e[:, bf], e[:, bf], PS[:, GATE, :], ALU.mult))
            return v.tensor_tensor(h[:, bf], e[:, bf], PS[:, UP, :], ALU.mult)

        rows_out = lambda: PS[:, OUT:OUT + 2, :].rearrange("p a n -> p (a n)")
        rows_in = lambda: PS[:, 0:2, :].rearrange("p a (c t) -> p (a c) t", t=P)

        with nc.Block() as block:
            @block.sync
            def _(sp):
                sp.dma_start(ident[:], d["ident"]).then_inc(S_("ident"), 16)

                def load(it, bf, n):
                    sp.wait_ge(S_(f"gu_used{bf}"), it)
                    sp.dma_start(wg[:, bf], weights(n, "w_e_gate")).then_inc(S_(f"wg{bf}"), 16)
                    sp.dma_start(wu[:, bf], weights(n, "w_e_up")).then_inc(S_(f"wu{bf}"), 16)
                    sp.wait_ge(S_(f"d_used{bf}"), it)
                    sp.dma_start(wd[:, bf], weights(n, "w_e_down")).then_inc(S_(f"wd{bf}"), 16)

                with sp.Fori(0, NE // 2) as it:
                    load(it, 0, 2 * it)
                    load(it, 1, 2 * it + 1)
                sp.wait_ge(S_("gu_used0"), NE // 2)
                sp.wait_ge(S_("d_used0"), NE // 2)

                def over(j):
                    n = sp.value_load(over_info[0:1, bass.ds(j, 1)], min_val=0, max_val=NE - 1)
                    sp.wait_ge(S_("ov_d"), j)
                    for dst, name in ((wg[:, 0], "w_e_gate"), (wu[:, 0], "w_e_up"), (wd[:, 0], "w_e_down")):
                        sp.dma_start(dst, weights(n, name)).then_inc(S_("ov_w"), 16)
                over_blocks(sp, over)

            @block.gpsimd
            def _(po):
                def gather(n, bf):
                    po.tensor_copy(idx[:, bf:bf + 1], slot_tok[:, bass.ds(n, 1)]).then_inc(S_("idx"), 1)
                    po.wait_ge(S_("idx"), n + 1)
                    po.sem_inc(S_("passed"), 1)
                    po.indirect_dma_start(xg[:, bf], None, d["hn"], bass.IndirectOffsetOnAxis(ap=idx[:, bf:bf + 1], axis=0)).then_inc(S_(f"rows{bf}"), 16)

                with po.Fori(0, NE // 2) as it:
                    for bf in range(2):
                        po.wait_ge(S_(f"rows_used{bf}"), it)
                        gather(2 * it + bf, bf)
                po.wait_ge(S_("rows_used0"), NE // 2)
                po.wait_ge(S_("rows0"), 16 * (NE // 2))

                def over(j):
                    po.wait_ge(S_("ov_turned"), j)
                    po.tensor_copy(idx[:, 0:1], slot_tok[:, bass.ds(j + NE, 1)]).then_inc(S_("ov_idx"), 1)
                    po.wait_ge(S_("ov_idx"), j + 1)
                    po.sem_inc(S_("passed"), 1)
                    po.indirect_dma_start(xg[:, 0], None, d["hn"], bass.IndirectOffsetOnAxis(ap=idx[:, 0:1], axis=0)).then_inc(S_("ov_rows"), 16)
                over_blocks(po, over)

            @block.tensor
            def _(pe):
                pe.wait_ge(S_("ident"), 16)

                def T(n, it, bf):
                    pe.wait_ge(S_(f"rows{bf}"), 16 * it + 16)
                    turn_rows(pe, bf).then_inc(S_(f"rows_used{bf}"), 1)

                def GU(n, it, bf):
                    pe.wait_ge(S_("xT"), n + 1)
                    pe.wait_ge(S_(f"wg{bf}"), 16 * it + 16)
                    pe.wait_ge(S_(f"wu{bf}"), 16 * it + 16)
                    pe.wait_ge(S_("h"), n)
                    gate_up(pe, bf).then_inc(S_(f"gu_used{bf}"), 1)

                def HT_(n, bf):
                    pe.wait_ge(S_("h"), n + 1)
                    turn_h(pe, bf).then_inc(S_("h_turned"), 1)

                def DN(n, it, bf):
                    pe.wait_ge(S_("hT"), n + 1)
                    pe.wait_ge(S_(f"wd{bf}"), 16 * it + 16)
                    pe.wait_ge(S_("y"), n)
                    down(pe, bf).then_inc(S_(f"d_used{bf}"), 1)

                T(0, 0, 0)
                GU(0, 0, 0)
                T(1, 0, 1)
                with pe.Fori(0, NE // 2 - 1) as it:
                    n = 2 * it + 1
                    GU(n, it, 1)
                    HT_(n - 1, 0)
                    T(n + 1, it + 1, 0)
                    DN(n - 1, it, 0)
                    GU(n + 1, it + 1, 0)
                    HT_(n, 1)
                    T(n + 2, it + 1, 1)
                    DN(n, it, 1)
                L = NE - 1
                GU(L, NE // 2 - 1, 1)
                HT_(L - 1, 0)
                DN(L - 1, NE // 2 - 1, 0)
                HT_(L, 1)
                DN(L, NE // 2 - 1, 1)

                def over(j):
                    pe.wait_ge(S_("ov_rows"), 16 * j + 16)
                    pe.wait_ge(S_("ov_h"), j)
                    turn_rows(pe, 0).then_inc(S_("ov_turned"), 1)
                    pe.wait_ge(S_("ov_xT"), j + 1)
                    pe.wait_ge(S_("ov_w"), 48 * j + 48)
                    gate_up(pe, 0).then_inc(S_("ov_gu"), 1)
                    pe.wait_ge(S_("ov_h"), j + 1)
                    turn_h(pe, 0).then_inc(S_("ov_ht"), 1)
                    pe.wait_ge(S_("ov_hT"), j + 1)
                    pe.wait_ge(S_("ov_y"), j)
                    down(pe, 0).then_inc(S_("ov_d"), 1)
                pe.wait_ge(S_("y"), NE)
                over_blocks(pe, over)

            @block.vector
            def _(v):
                def block_h(n, it, bf, lk):
                    v.wait_ge(S_("exp"), n + 1)
                    silu_up(v, bf, lk).then_inc(S_("h"), 1)

                def block_hT(n):
                    v.wait_ge(S_("h_turned"), n + 1)
                    v.tensor_copy(hT[:].rearrange("p c t -> p (c t)"), PS[:, HT, :]).then_inc(S_("hT"), 1)

                block_h(0, 0, 0, Steps(v, S_("dve"), 0))
                with v.Fori(0, NE // 2 - 1) as it:
                    n = 2 * it + 1
                    lk = Steps(v, S_("dve"), 6 * it + 3)
                    block_hT(n - 1)
                    block_h(n, it, 1, lk)
                    v.wait_ge(S_("d_used0"), it + 1)
                    block_hT(n)
                    block_h(n + 1, it + 1, 0, lk)
                    v.wait_ge(S_("d_used1"), it + 1)
                lk = Steps(v, S_("dve"), 6 * (NE // 2 - 1) + 3)
                block_hT(NE - 2)
                block_h(NE - 1, 0, 1, lk)
                v.wait_ge(S_("d_used0"), NE // 2)
                block_hT(NE - 1)

                def over(j):
                    lk = Steps(v, S_("ov_dve"), 3 * j)
                    v.wait_ge(S_("ov_exp"), j + 1)
                    silu_up(v, 0, lk).then_inc(S_("ov_h"), 1)
                    v.wait_ge(S_("ov_ht"), j + 1)
                    v.wait_ge(S_("ov_d"), j)
                    v.tensor_copy(hT[:].rearrange("p c t -> p (c t)"), PS[:, HT, :]).then_inc(S_("ov_hT"), 1)
                over_blocks(v, over)

            @block.scalar
            def _(act):
                def X(n, it, bf):
                    act.wait_ge(S_(f"rows_used{bf}"), it + 1)
                    act.copy(xT[:, bf], rows_in()).then_inc(S_("xT"), 1)

                def E(it, bf):
                    act.wait_ge(S_(f"gu_used{bf}"), it + 1)
                    act.activation(e[:, bf], PS[:, GATE, :], ACT.Exp, scale=-1.0).then_inc(S_("exp"), 1)

                def Y(n, it, bf):
                    act.wait_ge(S_(f"d_used{bf}"), it + 1)
                    act.wait_ge(S_(f"y_stored{bf}"), 16 * it)
                    act.copy(y[:, bf], rows_out()).then_inc(S_("y"), 1)
                    act.wait_ge(S_("y"), n + 1)
                    act.dma_start(d["blocks"][bass.ds(n * P, P), :], y[:, bf]).then_inc(S_(f"y_stored{bf}"), 16)

                X(0, 0, 0)
                E(0, 0)
                X(1, 0, 1)
                with act.Fori(0, NE // 2 - 1) as it:
                    n = 2 * it + 1
                    E(it, 1)
                    X(n + 1, it + 1, 0)
                    Y(n - 1, it, 0)
                    E(it + 1, 0)
                    X(n + 2, it + 1, 1)
                    Y(n, it, 1)
                E(NE // 2 - 1, 1)
                Y(NE - 2, NE // 2 - 1, 0)
                Y(NE - 1, NE // 2 - 1, 1)
                act.wait_ge(S_("y_stored0"), 16 * (NE // 2))
                act.wait_ge(S_("y_stored1"), 16 * (NE // 2))

                def over(j):
                    act.wait_ge(S_("ov_turned"), j + 1)
                    act.copy(xT[:, 0], rows_in()).then_inc(S_("ov_xT"), 1)
                    act.wait_ge(S_("ov_gu"), j + 1)
                    act.activation(e[:, 0], PS[:, GATE, :], ACT.Exp, scale=-1.0).then_inc(S_("ov_exp"), 1)
                    act.wait_ge(S_("ov_d"), j + 1)
                    act.copy(y[:, 0], rows_out()).then_inc(S_("ov_y"), 1)
                    act.wait_ge(S_("ov_y"), j + 1)
                    act.dma_start(d["blocks"][bass.ds(j * P + NE * P, P), :], y[:, 0]).then_inc(S_("ov_stored"), 16)
                    act.wait_ge(S_("ov_stored"), 16 * j + 16)
                    act.sem_inc(S_("ov_finished"), 1)
                over_blocks(act, over)


def phase_combine(core, PS, dest, comb):
    nc, d, sem = core.nc, core.dram, core.sem
    S_ = lambda n: sem("cb_" + n)
    with ExitStack() as ctx:
        sb = lambda n, s, t=F32: ctx.enter_context(nc.sbuf_tensor("cb_" + n, s, t))
        h, y1, y2, sq, o = sb("h", [P, TILES, D]), sb("y1", [P, TILES, D]), sb("y2", [P, TILES, D]), sb("sq", [P, D]), sb("o", [P, 2, D])
        gf, expo, st = sb("gf", [P, D]), sb("expo", [P, 1]), sb("st", [P, TILES, 4])
        rows = [P if t < NT else NS for t in range(TILES)]
        with nc.Block() as block:
            @block.sync
            def _(sp):
                sp.dma_start(gf[:], wide_row(d["g_final"], D)).then_inc(S_("g"), 16)
                for t in range(TILES):
                    sp.dma_start(h[:, t], d["h2"][t * P:(t + 1) * P, :]).then_inc(S_(f"h{t}"), 16)
                for t in range(TILES):
                    sp.wait_ge(S_("out"), t + 1)
                    dst = d["y_p"][t * P:(t + 1) * P, :] if t < NT else d["y_s"]
                    sp.dma_start(dst, o[0:rows[t], t % 2]).then_inc(S_(f"stored{t % 2}"), 16)
                sp.wait_ge(S_("stored0"), 16 * 5)
                sp.wait_ge(S_("stored1"), 16 * 4)

            @block.gpsimd
            def _(po):
                po.memset(expo[:], -0.5).then_inc(S_("expo"), 1)
                po.wait_ge(S_("expo"), 1)
                for t in range(TILES):
                    for k, y in enumerate((y1, y2)):
                        po.indirect_dma_start(y[0:rows[t], t], None, d["blocks"],
                                              bass.IndirectOffsetOnAxis(ap=dest[0:rows[t], k, t:t + 1], axis=0)).then_inc(S_(f"y{t}"), 16)
                for t in range(TILES):
                    po.wait_ge(S_("ms"), t + 1)
                    po.tensor_tensor(st[:, t, 2:3], st[:, t, 1:2], expo[:], ALU.pow).then_inc(S_("rstd"), 1)

            @block.vector
            def _(v):
                lk = Steps(v, S_("dve"))
                v.wait_ge(S_("g"), 16)
                v.memset(st[:], 1.0)
                for t in range(TILES):
                    r = slice(0, rows[t])
                    v.wait_ge(S_(f"h{t}"), 16)
                    v.wait_ge(S_(f"y{t}"), 32)
                    lk(v.scalar_tensor_tensor(h[r, t], y1[r, t], comb[r, 0, t:t + 1], h[r, t], ALU.mult, ALU.add))
                    lk(v.scalar_tensor_tensor(h[r, t], y2[r, t], comb[r, 1, t:t + 1], h[r, t], ALU.mult, ALU.add))
                    lk(v.tensor_tensor_reduce(sq[r], h[r, t], h[r, t], 1.0, 0.0, ALU.mult, ALU.add, st[r, t, 0:1]))
                    v.tensor_scalar(st[r, t, 1:2], st[r, t, 0:1], 1.0 / D, EPS, ALU.mult, ALU.add).then_inc(S_("ms"), 1)
                    v.wait_ge(S_("rstd"), t + 1)
                    if t >= 2:
                        v.wait_ge(S_(f"stored{t % 2}"), 16 * (t // 2))
                    lk(v.tensor_scalar(o[r, t % 2], h[r, t], st[r, t, 2:3], None, ALU.mult))
                    v.tensor_tensor(o[r, t % 2], o[r, t % 2], gf[r], ALU.mult).then_inc(S_("out"), 1)


def build(nc, dram):
    with ExitStack() as ctx:
        core = Core(nc, ctx, dram)
        PS = ctx.enter_context(nc.psum_tensor("banks", [P, 8, 512], F32))
        phase_project(core, PS)
        core.end_phase()
        phase_mixers(core, PS)
        core.end_phase()
        with ExitStack() as mem:
            kT = mem.enter_context(nc.sbuf_tensor("mem_kT", [P, KC, NMEM], F32))
            Vm = mem.enter_context(nc.sbuf_tensor("mem_v", [P, NMEM // P, D], F32))
            phase_memory_kv(core, PS, kT, Vm)
            core.end_phase()
            phase_attention(core, PS, kT, Vm)
            core.end_phase()
        sb = lambda n, s, t: ctx.enter_context(nc.sbuf_tensor("moe_" + n, s, t))
        dest, comb = sb("dest", [P, 2, TILES], I32), sb("comb", [P, 2, TILES], F32)
        slot_tok, over_info = sb("slot_tok", [P, NBLK], I32), sb("over_info", [P, NOVER + 1], I32)
        phase_route(core, PS, dest, comb, slot_tok, over_info)
        core.end_phase()
        phase_experts(core, PS, slot_tok, over_info)
        core.end_phase()
        phase_combine(core, PS, dest, comb)


SCRATCH = {"proj": ((ROWS + 8, NIN), F32), "mixed": ((ROWS, D), F32), "h2": ((ROWS, D), F32),
           "hn": ((ROWS, D), F32), "logits": ((ROWS, NG + NE), F32),
           "slots": ((NBLK * P, 1), I32), "blocks": ((NBLK * P, D), F32)}

INPUTS = ["w_in", "g_mix"]
OUTPUTS = [
    ("y_p", (SEQ, D)), ("y_s", (NS, D)),
    ("out_ret_p", (RH, RDK, RDV)), ("out_rwkv_p", (WH, WN, WN)), ("out_shift_p", (1, NRW)),
    ("out_ret_s", (DB, RH, RDK, RDV)), ("out_rwkv_s", (DB, WH, WN, WN)), ("out_shift_s", (DB, NRW)),
    ("out_mk", (NMEM, D)), ("out_mv", (NMEM, D)),
]


def program(nc, shapes):
    dram = {n: nc.dram_tensor(n, s, t, kind="ExternalInput").ap() for n, (s, t) in shapes.items()}
    for n, (s, t) in SCRATCH.items():
        dram[n] = nc.dram_tensor(n, s, t).ap()
    for n, s in OUTPUTS:
        dram[n] = nc.dram_tensor(n, s, F32, kind="ExternalOutput").ap()
    build(nc, dram)


def arrays_of(inputs):
    a = {k: np.ascontiguousarray(v) for k, v in inputs.items() if k not in ("x_prompt", "x_sample")}
    x = np.zeros((ROWS + P, D), np.float32)
    x[:SEQ] = inputs["x_prompt"][0]
    x[SEQ:SEQ + NS] = np.asarray(inputs["x_sample"]).reshape(NS, D)
    a["x"] = x
    a["zero_row"] = np.zeros((1, NRW), np.float32)
    a.update(shape_constants())
    return a


def kernel(**inputs):
    import concourse.bacc as bacc
    from concourse.bass_utils import run_bass_kernel_spmd

    arrays = arrays_of(inputs)
    nc = bacc.Bacc("TRN2", target_bir_lowering=False, num_devices=1)
    program(nc, {n: (a.shape, mybir.dt.from_np(a.dtype)) for n, a in arrays.items()})
    r = run_bass_kernel_spmd(nc, [arrays], core_ids=[0])
    got = r.results[0]
    order = [("y_p", (1, SEQ, D)), ("y_s", (DB, DS, D)), ("out_ret_p", (1, 1, RH, RDK, RDV)), ("out_rwkv_p", (1, 1, WH, WN, WN)),
             ("out_shift_p", (1, 1, NRW)), ("out_mk", (1, 1, NMEM, MH, MDH)), ("out_mv", (1, 1, NMEM, MH, MDH)),
             ("out_ret_s", (1, DB, RH, RDK, RDV)), ("out_rwkv_s", (1, DB, WH, WN, WN)), ("out_shift_s", (1, DB, NRW))]
    return tuple(got[n].reshape(s) for n, s in order)
```

```python
from contextlib import ExitStack

import numpy as np

import concourse.bass as bass
from concourse import mybir

ALU = mybir.AluOpType
ACT = mybir.ActivationFunctionType
AX = mybir.AxisListType
F32 = mybir.dt.float32
I32 = mybir.dt.int32
U32 = mybir.dt.uint32

P = 128
D = 1024
KC = D // P
SEQ = 1024
DB, DS = 8, 8
NS = DB * DS
NT = SEQ // P
TILES = NT + 1
ROWS = TILES * P
PAST = 8192
NMEM, MH, MDH = 256, 4, 256
RH, RDK, RDV = 4, 64, 128
RQK, RW = RH * RDK, RH * RDV
WH, WN = 8, 64
WW = WH * WN
LW, LA, LG = 64, 64, 128
NRET = 2 * RQK + 2 * RW
NRW = 3 * WW + LW + LA + LG
NIN = NRET + NRW
NG, EPG = 4, 8
NE = NG * EPG
DE = 512
EPS = 1e-6
LNX_EPS = 64e-5
CH = 64
LEVELS = 6
CAP = P
A_MAX = 2 * (SEQ + NS)
NOVER = (A_MAX - 1) // P
NBLK = NE + NOVER
NMASK = 4 + LEVELS
LEVELS_S = 3
N_CONST = 18
PER_PAIR = 35
PER_AT = 7


class Steps:

    def __init__(self, eng, sem, base=0):
        self.eng, self.sem, self.base, self.n = eng, sem, base, 0

    def __call__(self, ins):
        self.n += 1
        ins.then_inc(self.sem, 1)
        self.eng.wait_ge(self.sem, self.base + self.n)


def shape_constants():
    f = np.float32
    c = {}
    c["ident"] = np.eye(P, dtype=f)
    half = RDK // 2
    inv = (10000.0 ** (-np.arange(half, dtype=f) / f(half))).astype(f)
    pos = np.concatenate([np.arange(SEQ), PAST + np.arange(NS) % DS, np.zeros(ROWS - SEQ - NS)]).astype(f)
    ang = (pos[:, None] * inv[None, :]).astype(f)
    cos, sin = np.cos(ang).astype(f), np.sin(ang).astype(f)
    lg = np.log1p(-np.exp2(-5.0 - np.arange(RH)))
    step = np.concatenate([np.arange(SEQ) % P, np.arange(ROWS - SEQ) % DS]) + 1.0
    qdec = np.exp(step[:, None] * lg[None, :])
    kdec = np.exp(-step[:, None] * lg[None, :]) * RDK ** -0.5
    dec = np.concatenate([qdec, kdec], axis=1)
    c["rope"] = np.concatenate([(dec[:, :, None] * cos[:, None, :]).reshape(ROWS, -1),
                                (dec[:, :, None] * sin[:, None, :]).reshape(ROWS, -1)], axis=1).astype(f)
    c["cdec"] = np.stack([np.broadcast_to(np.repeat(np.exp(n * lg), RDV)[None], (RDK, RW)) for n in (P, DS)], 1).astype(f)
    s, t = np.arange(P)[:, None], np.arange(P)[None, :]
    for name, ch, rc in (("mask_p", CH, P), ("mask_s", DS, DS)):
        same = s // ch == t // ch
        strict, incl = same & (s < t), same & (s <= t)
        ret = (s // rc == t // rc) & (s <= t)
        lev = []
        for l in range(LEVELS):
            b = 2 ** l
            lev.append((s // (2 * b) == t // (2 * b)) & (s // b % 2 == 0) & (t // b % 2 == 1))
        c[name] = np.stack([strict, incl, ret, s < t] + lev, 1).astype(f)
    c["chunk_p"] = (s // CH == np.arange(DB)[None]).astype(f)
    c["chunk_s"] = (s // DS == np.arange(DB)[None]).astype(f)
    bt = (np.arange(NS)[None, None, :] // DS == np.arange(DB)[None, :, None])
    c["expand_k"] = np.broadcast_to(bt, (WN, DB, NS)).reshape(WN, -1).astype(f)
    c["expand_t"] = np.broadcast_to((np.arange(NS)[:, None, None] // DS == np.arange(DB)[None, :, None]),
                                    (NS, DB, RDV)).reshape(NS, -1).astype(f)
    row = np.arange(TILES)[None, :] * P + np.arange(P)[:, None]
    c["valid"] = (row < SEQ + NS).astype(f)
    c["token"] = row.astype(np.int32)
    cnt = np.concatenate([np.arange(NE) * CAP, np.arange(NE), np.arange(NOVER), EPG - np.arange(EPG),
                          CAP * (1.0 + np.arange(8))])
    c["count"] = np.broadcast_to(cnt[None], (P, cnt.size)).astype(f)
    return {k: np.ascontiguousarray(v) for k, v in c.items()}


class Core:

    def __init__(self, nc, ctx, dram):
        self.nc, self.ctx, self.dram, self.sems = nc, ctx, dram, {}

    def sem(self, name):
        if name not in self.sems:
            self.sems[name] = self.nc.alloc_semaphore(name=name)
        return self.sems[name]

    def end_phase(self):
        self.nc.clear_and_free_semaphores(list(self.sems.values()))
        self.nc.all_engine_barrier()
        self.sems = {}


def wide_row(ap, n):
    return ap.rearrange("(a n) -> a n", a=1).broadcast_to([P, n])


def phase_project(core, PS):
    nc, d, sem = core.nc, core.dram, core.sem
    S_ = lambda n: sem("pj_" + n)
    NCH = 8
    W = NIN // NCH
    BUFS = 3
    assert W * NCH == NIN and TILES % BUFS == 0 and W <= 512
    F32R = mybir.dt.float32r
    with ExitStack() as ctx:
        sb = lambda n, s, t=F32: ctx.enter_context(nc.sbuf_tensor("pj_" + n, s, t))
        w, w_hi, w_lo = sb("w", [P, 2, KC, W]), sb("w_hi", [P, 2, KC, W], F32R), sb("w_lo", [P, 2, KC, W], F32R)
        xT, x_hi, x_lo = sb("xT", [P, KC, P]), sb("x_hi", [P, TILES, KC, P], F32R), sb("x_lo", [P, TILES, KC, P], F32R)
        x, sq = sb("x", [P, 2, D]), sb("sq", [P, D])
        g, ident, expo, st = sb("g", [P, KC]), sb("ident", [P, P]), sb("expo", [P, 1]), sb("st", [P, TILES, 4])
        out = sb("out", [P, BUFS, W])
        as_f32 = lambda ap: ap.bitcast(F32)

        with nc.Block() as block:
            @block.sync
            def _(sp):
                wv = d["w_in"][0].rearrange("(c p) n -> p c n", p=P)

                def load_x(t):
                    sp.dma_start(x[:, t % 2], d["x"][t * P:(t + 1) * P, :]).then_inc(S_(f"x_loaded{t % 2}"), 16)

                def load_w(c, par):
                    sp.dma_start(w[:, par], wv[:, :, bass.ds(c * W, W)]).then_inc(S_(f"w_loaded{par}"), 16)

                load_x(0)
                sp.dma_start(ident[:], d["ident"][:]).then_inc(S_("consts"), 16)
                with nc.allow_non_contiguous_dma(reason="a gain by channel"):
                    sp.dma_start(g[:], d["g_mix"][0].rearrange("(c p) -> p c", p=P)).then_inc(S_("consts"), 16)
                load_w(0, 0)
                load_x(1)
                load_w(1, 1)
                sp.dma_start(d["proj"][0:1, NRET:NIN], d["zero_row"][:]).then_inc(S_("zero_stored"), 16)
                for t in range(2, TILES):
                    sp.wait_ge(S_("turned"), t - 1)
                    load_x(t)
                with sp.Fori(0, NCH // 2 - 1) as m:
                    for par in range(2):
                        sp.wait_ge(S_("w_split"), 2 * m + par + 1)
                        load_w(2 * m + par + 2, par)
                sp.wait_ge(S_("zero_stored"), 16)

            @block.vector
            def _(v):
                def split_w(c, par):
                    v.wait_ge(S_("w_high"), c + 1)
                    v.tensor_tensor(w_lo[:, par], w[:, par], as_f32(w_hi[:, par]), ALU.subtract).then_inc(S_("w_split"), 1)

                def mean_square(t):
                    v.wait_ge(S_("squares"), t + 1)
                    v.tensor_scalar(st[:, t, 1:2], st[:, t, 0:1], 1.0 / D, EPS, ALU.mult, ALU.add).then_inc(S_("ms"), 1)

                lk = Steps(v, S_("dve_first"))
                v.wait_ge(S_("consts"), 32)
                mean_square(0)
                split_w(0, 0)
                mean_square(1)
                for t in range(TILES):
                    v.wait_ge(S_("turned"), t + 1)
                    src = PS[:, 2 * (t % 2):2 * (t % 2) + 2, :].rearrange("p a (c t) -> p (a c) t", t=P)
                    gain = g[:].unsqueeze(2).to_broadcast([P, KC, P])
                    v.tensor_tensor(xT[:], src, gain, ALU.mult)
                    lk(v.tensor_tensor(x_hi[:, t], src, gain, ALU.mult))
                    lk(v.tensor_tensor(x_lo[:, t], xT[:], as_f32(x_hi[:, t]), ALU.subtract))
                    v.sem_inc(S_("xT"), 1)
                    if t + 2 < TILES:
                        mean_square(t + 2)
                    if t == 4:
                        split_w(1, 1)
                with v.Fori(0, NCH // 2 - 1) as m:
                    for par in range(2):
                        split_w(2 * m + 2 + par, par)

            @block.gpsimd
            def _(po):
                po.memset(expo[:], -0.5).then_inc(S_("expo"), 1)
                po.wait_ge(S_("expo"), 1)
                for t in range(TILES):
                    po.wait_ge(S_("ms"), t + 1)
                    po.tensor_tensor(st[:, t, 2:3], st[:, t, 1:2], expo[:], ALU.pow).then_inc(S_("rstd"), 1)

            @block.scalar
            def _(act):
                def norm(t):
                    act.wait_ge(S_(f"x_loaded{t % 2}"), 16 * (t // 2) + 16)
                    act.activation(sq[:], x[:, t % 2], ACT.Square, accum_out=st[:, t, 0:1]).then_inc(S_("squares"), 1)
                    act.wait_ge(S_("rstd"), t + 1)
                    act.activation(x[:, t % 2], x[:, t % 2], ACT.Copy, scale=st[:, t, 2:3]).then_inc(S_("xn"), 1)

                def store(c, t):
                    b = t % BUFS
                    act.wait_ge(S_("projected"), TILES * c + t + 1)
                    act.wait_ge(S_(f"stored{b}"), 16 * (TILES // BUFS * c + t // BUFS) + 16)
                    act.copy(out[:, b], PS[:, 4 + b, 0:W]).then_inc(S_("banked"), 1)
                    act.wait_ge(S_("banked"), TILES * c + t + BUFS + 1)
                    act.dma_start(d["proj"][t * P + 1:t * P + 1 + P, bass.ds(c * W, W)], out[:, b]).then_inc(S_(f"stored{b}"), 16)

                def split_w(n, par):
                    act.wait_ge(S_(f"w_loaded{par}"), 16 * n + 16)
                    act.copy(w_hi[:, par], w[:, par]).then_inc(S_("w_high"), 1)

                for b in range(BUFS):
                    act.sem_inc(S_(f"stored{b}"), 16)
                act.sem_inc(S_("banked"), BUFS)
                norm(0)
                split_w(0, 0)
                norm(1)
                for t in range(TILES):
                    if t + 2 < TILES:
                        norm(t + 2)
                    store(0, t)
                    if t == 3:
                        split_w(0, 1)
                with act.Fori(0, NCH // 2 - 1) as m:
                    for par in (1, 0):
                        for t in range(TILES):
                            store(2 * m + 2 - par, t)
                            if t == 3:
                                split_w(m + 1, 1 - par)
                for t in range(TILES):
                    store(NCH - 1, t)
                for b in range(BUFS):
                    act.wait_ge(S_(f"stored{b}"), 16 * (TILES // BUFS * NCH) + 16)

            @block.tensor
            def _(pe):
                def turn(t):
                    pe.wait_ge(S_("xn"), t + 1)
                    if t >= 2:
                        pe.wait_ge(S_("xT"), t - 1)
                    for c in range(KC):
                        ins = pe.transpose(PS[:, 2 * (t % 2) + c // 4, c % 4 * P:(c % 4 + 1) * P], x[:, t % 2, c * P:(c + 1) * P], ident[:])
                    ins.then_inc(S_("turned"), 1)

                def project(c, par, t):
                    pe.wait_ge(S_("w_split"), c + 1)
                    pe.wait_ge(S_("banked"), TILES * c + t + 1)
                    pairs = [(x_hi, w_hi), (x_hi, w_lo), (x_lo, w_hi)]
                    for k in range(KC):
                        for n, (a, b) in enumerate(pairs):
                            ins = pe.matmul(PS[:, 4 + t % BUFS, 0:W], a[:, t, k, :], b[:, par, k, :],
                                            start=k == 0 and n == 0, stop=k == KC - 1 and n == len(pairs) - 1)
                    ins.then_inc(S_("projected"), 1)

                pe.wait_ge(S_("consts"), 32)
                turn(0)
                for t in range(TILES):
                    if t + 1 < TILES:
                        turn(t + 1)
                    pe.wait_ge(S_("xT"), t + 1)
                    project(0, 0, t)
                with pe.Fori(0, NCH // 2 - 1) as m:
                    for par in (1, 0):
                        for t in range(TILES):
                            project(2 * m + 2 - par, par, t)
                for t in range(TILES):
                    project(NCH - 1, 1, t)


def phase_mixers(core, PS):
    nc, d, sem = core.nc, core.dram, core.sem
    OQ, OV, OG = 0, 2 * RQK, 2 * RQK + RW
    OR = NRET
    with ExitStack() as ctx:
        sb = lambda n, s, t=F32: ctx.enter_context(nc.sbuf_tensor("mx_" + n, s, t))
        pin, prev = sb("pin", [P, NIN]), sb("prev", [P, NRW])
        rope = sb("rope", [P, 2, 2 * RH, 32])
        mu = sb("mu", [P, NRW])
        names = ["rwkv_w0", "rwkv_a0", "rwkv_k_k", "rwkv_k_a", "rwkv_r_k", "rwkv_lnx_w", "rwkv_lnx_b", "ret_gn"]
        vec = sb("vec", [P, len(names), 512])
        V_ = {n: vec[:, j, :] for j, n in enumerate(names)}
        w2, a2, g2 = sb("w2", [LW, WW]), sb("a2", [LA, WW]), sb("g2", [LG, WW])
        ident = sb("ident", [P, P])
        masks = sb("masks", [P, NMASK, P])
        chunk = sb("chunk", [P, DB])
        cdec = sb("cdec", [RDK, 2, RW])
        expk, expt = sb("expk", [WN, DB, NS]), sb("expt", [NS, DB, RDV])
        expo = sb("expo", [P, 8])
        lora = sb("lora", [P, 256])
        loT, hgT = sb("loT", [64, 2, P]), sb("hgT", [P, P])
        sg = sb("sg", [P, 2, WW])
        lw = sb("lw", [P, WW])
        pinc, pinv = sb("pinc", [P, WW]), sb("pinv", [P, WW])
        t0, kk = sb("t0", [P, WW]), sb("kk", [P, WW])
        kr = sb("kr", [P, WW])
        stage = sb("stage", [P, 2, 8, WW])
        V_W, V_R, G_W, G_R = 4, 5, 6, 7
        bonus = sb("bonus", [P, 2, WH])
        stb = sb("stb", [P, 4, WH])
        st = sb("st", [P, 8, 8])
        T4 = sb("T4", [WN, WH, 4, P])
        M4 = sb("M4", [P, WH, 4, P])
        ALX = sb("ALX", [P, 2, 2, 4, P])
        AL, X = ALX[:, 0], ALX[:, 1]
        T, TT = sb("T", [P, 2, 4, P]), sb("TT", [P, 2, 4, P])
        U = sb("U", [WN, WH, WN])
        pc = sb("pc", [WN, 2, WH, DB])
        tb = sb("tb", [P, WW])
        xs, sas = sb("xs", [P, WW]), sb("sas", [P, WW])
        y, o_w, o_r = sb("y", [P, WW]), sb("o_w", [P, WW]), sb("o_r", [P, RW])
        qk, qkt = sb("qk", [P, 2 * RH, 64]), sb("qkt", [P, 2 * RH, 32])
        qkT = sb("qkT", [RDK, 2 * RH, P])
        att = sb("att", [P, RH, P])
        S = sb("S", [RDK, RH, RDV])
        Us = stage[0:WN, 1].rearrange("p a n -> p (a n)").rearrange("p (h b n) -> p h b n", h=WH, b=DB)
        Uv = M4[0:WN].rearrange("p h a t -> p (h a t)").rearrange("p (b h k) -> p b h k", b=DB, h=WH)
        Ss = T4[:].rearrange("p h a t -> p (h a t)").rearrange("p (b h e) -> p b h e", b=DB, h=RH)
        ex_k = ALX[0:WN].rearrange("p x g h t -> p (x g h t)").rearrange("p (f j b t) -> p f j b t", f=2, j=2, b=DB)
        ex_t = sb("ex_t", [NS, 2, DB, RDV])
        ro, rt = sb("ro", [P, RW]), sb("rt", [P, RW])

        B = lambda b, *ix: PS[:, b, :] if not ix else PS[ix[0], b, ix[1]]
        heads = lambda ap, h=WH: ap.rearrange("p (h n) -> p h n", h=h)
        over = lambda ap, n: ap.unsqueeze(2).to_broadcast([ap.shape[0], ap.shape[1], n])
        rows = [slice(0, CH), slice(CH, P)]

        loaded, c_loaded, states = sem("mx_tile_loaded"), sem("mx_consts_loaded"), sem("mx_states_loaded")
        shift_rows = sem("mx_shift_rows_loaded")
        chain = {e: sem("mx_own_" + e) for e in ("dve", "act", "pool")}
        S_ = lambda n: sem("mx_" + n)

        ctx2 = ExitStack()
        with ctx2, nc.Block() as block:
            @block.sync
            def _(sp):
                def load(at, i):
                    sp.dma_start(pin[:], d["proj"][bass.ds(at + 1, P), :]).then_inc(loaded, 16)
                    sp.dma_start(prev[:], d["proj"][bass.ds(at, P), OR:NIN]).then_inc(loaded, 16)
                    sp.dma_start(rope[:].rearrange("p a b c -> p (a b c)"), d["rope"][bass.ds(at, P), :]).then_inc(loaded, 16)

                load(0, 0)
                n = 0
                with nc.allow_non_contiguous_dma(reason="small rows, once"):
                    for dst, src in [(mu[:], wide_row(d["rwkv_mu"][0], NRW)),
                                     *[(V_[x], wide_row(d[x][0] if x != "rwkv_r_k" else d[x][0].rearrange("h n -> (h n)"), 512)) for x in names],
                                     (w2[:], d["rwkv_w2"][0]), (a2[:], d["rwkv_a2"][0]), (g2[:], d["rwkv_g2"][0]),
                                     (ident[:], d["ident"]), (masks[:], d["mask_p"]), (chunk[:], d["chunk_p"]),
                                     (cdec[:], d["cdec"]), (expk[:].rearrange("p a b -> p (a b)"), d["expand_k"]),
                                     (expt[:].rearrange("p a b -> p (a b)"), d["expand_t"])]:
                        sp.dma_start(dst, src).then_inc(c_loaded, 16)
                        n += 1
                assert n == N_CONST

                def store_ret(at, j):
                    sp.wait_ge(S_("o_r_ready"), j + 1)
                    sp.dma_start(d["mixed"][bass.ds(at, P), 0:RW], o_r[:]).then_inc(S_("o_r_stored"), 16)

                def store_rwkv(at, i):
                    sp.wait_ge(S_("o_w_ready"), i + 1)
                    sp.dma_start(d["mixed"][bass.ds(at, P), RW:D], o_w[:]).then_inc(S_("o_w_stored"), 16)

                sp.sem_inc(S_("o_r_stored"), 16)
                sp.sem_inc(S_("o_w_stored"), 16)
                sp.wait_ge(S_("pin_used"), 1)
                load(P, 1)
                sp.dma_start(d["blocks"][NE * P:NBLK * P, :], d["zero_row"][0:1, 0:D].broadcast_to([NOVER * P, D])).then_inc(S_("blocks_cleared"), 16)
                store_ret(0, 0)
                with sp.Fori(0, NT - 2) as i:
                    sp.wait_ge(S_("pin_used"), i + 2)
                    load(i * P + 2 * P, i)
                    store_ret(i * P + P, i + 1)
                    store_rwkv(i * P, i)
                sp.wait_ge(S_("pin_used"), NT)
                load(SEQ, NT)
                store_ret((NT - 1) * P, NT - 1)
                store_rwkv((NT - 2) * P, NT - 2)
                sp.wait_ge(loaded, 48 * (NT + 1))
                sp.dma_start(prev[0:NS:DS, :], d["state_shift"][0]).then_inc(shift_rows, 16)
                sp.wait_ge(S_("U_products"), 2 * NT)
                sp.dma_start(Uv, d["state_rwkv"][0].rearrange("b h v k -> v b h k")).then_inc(states, 16)
                sp.dma_start(Ss, d["state_ret"][0].rearrange("b h k e -> k b h e")).then_inc(states, 16)
                sp.dma_start(masks[:], d["mask_s"]).then_inc(c_loaded, 16)
                sp.dma_start(chunk[:], d["chunk_s"]).then_inc(c_loaded, 16)
                store_rwkv((NT - 1) * P, NT - 1)
                sp.dma_start(d["out_ret_p"].rearrange("h k e -> k h e"), S[:]).then_inc(S_("states_stored"), 16)
                sp.wait_ge(S_("U_turned"), 1)
                sp.dma_start(d["out_rwkv_p"].rearrange("h v k -> v h k"), xs[0:WN, :].rearrange("p (h n) -> p h n", h=WH)).then_inc(S_("states_stored"), 16)
                sp.wait_ge(S_("Ss_ready"), RH)
                sp.dma_start(d["out_ret_s"].rearrange("b h k e -> k b h e"), Ss).then_inc(S_("Ss_stored"), 16)
                store_ret(SEQ, NT)
                store_rwkv(SEQ, NT)
                sp.dma_start(d["out_shift_p"], d["proj"][SEQ:SEQ + 1, OR:NIN]).then_inc(S_("states_stored"), 16)
                sp.dma_start(d["out_shift_s"], d["proj"][SEQ + 1:SEQ + 1 + NS, OR:NIN].rearrange("(b s) n -> b s n", s=DS)[:, DS - 1, :]).then_inc(S_("states_stored"), 16)
                sp.wait_ge(S_("Ss_stored"), 16)
                sp.wait_ge(S_("Us_turned"), WH)
                sp.dma_start(d["out_rwkv_s"].rearrange("b h v k -> v b h k"), Uv).then_inc(S_("states_stored"), 16)
                sp.wait_ge(S_("states_stored"), 80)
                sp.wait_ge(S_("blocks_cleared"), 16)
                sp.wait_ge(S_("o_r_stored"), 16 * (TILES + 1))
                sp.wait_ge(S_("o_w_stored"), 16 * (TILES + 1))

            def a_shift(v, j, lk):
                lk(v.tensor_tensor(prev[:], prev[:], pin[:, OR:NIN], ALU.subtract))
                lk(v.tensor_tensor(prev[:], prev[:], mu[:], ALU.mult))
                v.tensor_tensor(pin[:, OR:NIN], pin[:, OR:NIN], prev[:], ALU.add).then_inc(S_("shifted"), 1)

            def a_rotary(v, j, lk):
                qin = pin[:, OQ:OV].rearrange("p (h n) -> p h n", n=64)
                lo, hi = qin[:, :, 0:32], qin[:, :, 32:64]
                cs, sn = rope[:, 0], rope[:, 1]
                lk(v.tensor_tensor(qk[:, :, 0:32], lo, cs, ALU.mult))
                lk(v.tensor_tensor(qkt[:], hi, sn, ALU.mult))
                lk(v.tensor_tensor(qk[:, :, 0:32], qk[:, :, 0:32], qkt[:], ALU.subtract))
                lk(v.tensor_tensor(qk[:, :, 32:64], hi, cs, ALU.mult))
                lk(v.tensor_tensor(qkt[:], lo, sn, ALU.mult))
                v.tensor_tensor(qk[:, :, 32:64], qk[:, :, 32:64], qkt[:], ALU.add).then_inc(S_("qk_ready"), 1)

            def a_keys(v, j, lk):
                v.wait_ge(S_("shifted"), j + 1)
                lk(v.tensor_tensor(kk[:], K_(), V_["rwkv_k_k"], ALU.mult))
                lk(v.tensor_tensor(t0[:], kk[:], kk[:], ALU.mult))
                lk(v.tensor_reduce(st[:, 0, :], heads(t0[:]), AX.X, ALU.add))
                v.tensor_scalar(st[:, 1, :], st[:, 0, :], 1e-24, None, ALU.max).then_inc(S_("kk_sq"), 1)

            def a_turned_qk(v, j, lk):
                v.wait_ge(S_("qkT"), j + 1)
                v.tensor_copy(qkT[:].rearrange("p (a h) t -> p a (h t)", a=2), PS[0:RDK, 6:8, :]).then_inc(S_("qkT_ready"), 1)
                v.wait_ge(S_("lora_act"), j + 1)
                v.tensor_scalar(lora[:, 128:256], lora[:, 128:256], 0.5, 0.5, ALU.mult, ALU.add).then_inc(S_("lora_ready"), 1)

            def a_turned_lora(v, j, lk):
                v.wait_ge(S_("kk_rn"), j + 1)
                lk(v.tensor_tensor(heads(kk[:]), heads(kk[:]), over(st[:, 2, :], WN), ALU.mult))
                v.wait_ge(S_("loraT"), j + 1)
                v.tensor_copy(loT[:], B(6, slice(0, 64), slice(0, 256)).rearrange("p (a b) -> p a b", a=2))
                v.tensor_copy(hgT[:], B(6, slice(0, P), slice(256, 384))).then_inc(S_("loraT_ready"), 1)

            def a_rates(v, j, lk):
                v.wait_ge(S_("rates"), j + 1)
                v.tensor_tensor(sg[:, 0, :], B(6), V_["rwkv_w0"], ALU.add)
                v.tensor_tensor(sg[:, 1, :], B(7), V_["rwkv_a0"], ALU.add).then_inc(S_("z_ready"), 1)

            def a_att(v, j, lk):
                v.wait_ge(S_("att_done"), j + 1)
                v.tensor_tensor(att[:], B(5).rearrange("p (h t) -> p h t", h=RH),
                                masks[:, 2, :].unsqueeze(1).to_broadcast([P, RH, P]), ALU.mult).then_inc(S_("att_ready"), 1)

            def a_decay(v, j, bf, lk):
                v.wait_ge(S_("z_tanh"), j + 1)
                c = -0.5 * float(np.exp(-0.5))
                v.tensor_scalar(lw[:], sg[:, 0, :], c, c, ALU.mult, ALU.add).then_inc(S_("lw_ready"), 1)
                lk(v.tensor_scalar(sg[:, 1, :], sg[:, 1, :], 0.5, 0.5, ALU.mult, ALU.add))
                lk(v.scalar_tensor_tensor(t0[:], sg[:, 1, :], -1.0, V_["rwkv_k_a"], ALU.add, ALU.mult))
                lk(v.scalar_tensor_tensor(kr[:], t0[:], 1.0, K_(), ALU.add, ALU.mult))
                lk(v.tensor_tensor(t0[:], R_(), kr[:], ALU.mult))
                lk(v.tensor_tensor(t0[:], t0[:], V_["rwkv_r_k"], ALU.mult))
                lk(v.tensor_reduce(bonus[:, bf, :], heads(t0[:]), AX.X, ALU.add))
                v.tensor_tensor(t0[:], kk[:], sg[:, 1, :], ALU.mult)

            def a_ret_state(v, j, lk):
                v.wait_ge(S_("ret_done"), j + 1)
                lk(v.tensor_copy(ro[:], B(6)))
                lk(v.tensor_tensor(flat(S[:]), flat(S[:]), B(7, slice(0, RDK), slice(0, 512)), ALU.add))
                v.tensor_tensor(flat(S[:]), flat(S[:]), cdec[:, 0, :], ALU.mult).then_inc(S_("S_ready"), 1)

            def a_before(v, j, lk):
                v.wait_ge(S_("L_read"), j + 1)
                v.tensor_tensor(sg[:, 0, :], B(4), lw[:], ALU.subtract).then_inc(S_("lx_ready"), 1)

            def a_operands(v, j, bf, lk):
                v.wait_ge(S_("decays"), j + 1)
                v.scalar_tensor_tensor(stage[:, bf, 0, :], kk[:], -1.0, sg[:, 0, :], ALU.mult, ALU.mult)
                v.tensor_tensor(stage[:, bf, 1, :], R_(), pinc[:], ALU.mult).then_inc(S_("pin_used"), 1)
                v.tensor_tensor(stage[:, bf, 2, :], t0[:], pinv[:], ALU.mult)
                v.tensor_tensor(stage[:, bf, 3, :], kr[:], pinv[:], ALU.mult).then_inc(S_("arbk_ready"), 1)

            def a_ret_gate(v, j, bf, lk):
                rg = stage[:, bf, G_R, :]
                v.wait_ge(S_("lora_act"), j + 1)
                lk(v.scalar_tensor_tensor(rg, rg, 1.0, pin[:, OG:OG + RW], ALU.add, ALU.mult))
                lk(v.scalar_tensor_tensor(rg, rg, 0.5, V_["ret_gn"], ALU.mult, ALU.mult))

            def a_ret_norm(v, j, lk):
                lk(v.tensor_tensor(rt[:], ro[:], ro[:], ALU.mult))
                lk(v.tensor_reduce(st[:, 3, 0:RH], heads(rt[:], RH), AX.X, ALU.add))
                v.tensor_scalar(st[:, 4, 0:RH], st[:, 3, 0:RH], 1.0 / RDV, EPS, ALU.mult, ALU.add).then_inc(S_("ret_ms"), 1)

            def a_ret_out(v, j, bf, lk):
                v.wait_ge(S_("ret_rn"), j + 1)
                lk(v.tensor_tensor(heads(rt[:], RH), heads(ro[:], RH), over(st[:, 5, 0:RH], RDV), ALU.mult))
                v.wait_ge(S_("o_r_stored"), 16 * j + 16)
                v.tensor_tensor(o_r[:], rt[:], stage[:, bf, G_R, :], ALU.mult).then_inc(S_("o_r_ready"), 1)

            def b_turned(v, i):
                for h in range(0, WH, 2):
                    v.wait_ge(S_("headT"), WH * i + h + 1)
                    v.tensor_copy(T4[:, h, :, :], B(h % 4, slice(0, WN), slice(0, 512)).rearrange("p (a b) -> p a b", a=4)).then_inc(S_("T4_ready_dve"), 1)

            def b_masked(v, i):
                for h in range(WH):
                    v.wait_ge(S_("products"), WH * i + h + 1)
                    v.tensor_tensor(M4[:, h].rearrange("p (x a) b -> p x a b", x=2), B(4 + h % 4).rearrange("p (x a b) -> p x a b", x=2, a=2),
                                    masks[:, 0:2, :].unsqueeze(1).to_broadcast([P, 2, 2, P]), ALU.mult).then_inc(S_("M4_ready"), 1)

            def b_first(v, i):
                for g in range(2):
                    v.wait_ge(S_("AL_ready"), 2 * levels_before(i) + g + 1)
                    v.tensor_tensor(TT[:, g], AL[:, g], ident[:].unsqueeze(1).to_broadcast([P, 4, P]), ALU.add).then_inc(S_("TT_first"), 1)

            def b_level(v, i, l):
                for g in range(2):
                    v.wait_ge(S_("dTT"), 2 * updates_before(i) + 2 * (l - 1) + g + 1)
                    v.tensor_tensor(TT[:, g], TT[:, g], B(4 + g).rearrange("p (a b) -> p a b", a=4), ALU.add).then_inc(S_("TT_ready"), 1)

            def b_state(v, i, c, bf, lk):
                v.wait_ge(S_("U_products"), 2 * i + c + 1)
                lk(v.tensor_tensor(flat(U[:]), flat(U[:]), B(1, slice(0, WN), slice(0, 512)), ALU.add))
                v.tensor_tensor(U[:], U[:], pc[:, bf, :, c:c + 1].to_broadcast([WN, WH, WN]), ALU.mult).then_inc(S_("U_ready"), 1)

            def b_center(v, i, lk):
                lk(v.tensor_reduce(stb[:, 0, :], heads(B(0)), AX.X, ALU.add))
                lk(v.tensor_scalar(stb[:, 0, :], stb[:, 0, :], 1.0 / WN, None, ALU.mult))
                v.tensor_tensor(heads(y[:]), heads(B(0)), over(stb[:, 0, :], WN), ALU.subtract).then_inc(S_("y_read"), 1)
                v.wait_ge(S_("y_read"), i + 1)
                lk(v.tensor_tensor(tb[:], y[:], y[:], ALU.mult))
                lk(v.tensor_reduce(stb[:, 1, :], heads(tb[:]), AX.X, ALU.add))
                v.tensor_scalar(stb[:, 2, :], stb[:, 1, :], 1.0 / WN, LNX_EPS, ALU.mult, ALU.add).then_inc(S_("y_ms"), 1)

            def b_out(v, i, bf, lk):
                lk(v.tensor_tensor(heads(tb[:]), heads(stage[:, bf, V_W, :]), over(bonus[:, bf, :], WN), ALU.mult))
                lk(v.tensor_tensor(tb[:], tb[:], V_["rwkv_lnx_b"], ALU.add))
                v.wait_ge(S_("y_rn"), i + 1)
                lk(v.tensor_tensor(heads(y[:]), heads(y[:]), over(stb[:, 3, :], WN), ALU.mult))
                lk(v.tensor_tensor(y[:], y[:], V_["rwkv_lnx_w"], ALU.mult))
                lk(v.tensor_tensor(y[:], y[:], tb[:], ALU.add))
                v.wait_ge(S_("o_w_stored"), 16 * i + 16)
                v.tensor_tensor(o_w[:], y[:], stage[:, bf, G_W, :], ALU.mult).then_inc(S_("o_w_ready"), 1)

            def dve_a(v, j, bf, lk):
                a_shift(v, j, lk)
                a_rotary(v, j, lk)
                a_keys(v, j, lk)
                a_turned_qk(v, j, lk)
                a_ret_gate(v, j, bf, lk)
                a_turned_lora(v, j, lk)
                a_rates(v, j, lk)
                a_att(v, j, lk)
                a_decay(v, j, bf, lk)
                a_ret_state(v, j, lk)
                a_before(v, j, lk)
                a_ret_norm(v, j, lk)
                a_operands(v, j, bf, lk)
                a_ret_out(v, j, bf, lk)

            def dve_pair(v, i, bf, lk):
                b_turned(v, i)
                b_masked(v, i)
                b_first(v, i)
                v.wait_ge(loaded, 48 * i + 96)
                a_shift(v, i + 1, lk)
                b_level(v, i, 1)
                a_rotary(v, i + 1, lk)
                b_level(v, i, 2)
                a_keys(v, i + 1, lk)
                b_level(v, i, 3)
                a_turned_qk(v, i + 1, lk)
                a_ret_gate(v, i + 1, 1 - bf, lk)
                b_level(v, i, 4)
                a_turned_lora(v, i + 1, lk)
                b_level(v, i, 5)
                a_rates(v, i + 1, lk)
                a_att(v, i + 1, lk)
                b_state(v, i, 0, bf, lk)
                a_decay(v, i + 1, 1 - bf, lk)
                a_before(v, i + 1, lk)
                b_state(v, i, 1, bf, lk)
                a_operands(v, i + 1, 1 - bf, lk)
                b_center(v, i, lk)
                a_ret_state(v, i + 1, lk)
                a_ret_norm(v, i + 1, lk)
                b_out(v, i, bf, lk)
                a_ret_out(v, i + 1, 1 - bf, lk)

            flat = lambda ap: ap.rearrange("p h n -> p (h n)")
            K_ = lambda: pin[:, OR + WW:OR + 2 * WW]
            R_ = lambda: pin[:, OR:OR + WW]
            def dve_retention_sample(v, lk):
                for h in range(RH):
                    if h >= 2:
                        v.wait_ge(S_("ret_s_done"), h - 1)
                    v.tensor_tensor(ex_k[:, h % 2, 0], qkT[:, h, 0:NS].unsqueeze(1).to_broadcast([RDK, DB, NS]), expk[:], ALU.mult)
                    v.tensor_tensor(ex_t[:, h % 2], stage[0:NS, 0, V_R, h * RDV:(h + 1) * RDV].unsqueeze(1).to_broadcast([NS, DB, RDV]),
                                    expt[:], ALU.mult).then_inc(S_("ret_ex"), 1)
                    if h >= 1:
                        ret_state(v, h - 1, lk)
                ret_state(v, RH - 1, lk)
                v.wait_ge(S_("ret_s_done"), RH)
                v.tensor_copy(ro[0:NS, :], B(6, slice(0, NS), slice(0, 512))).then_inc(S_("ro_s"), 1)
                v.wait_ge(S_("ro_s"), 1)

            def ret_state(v, h, lk):
                v.wait_ge(S_("ret_s_done"), h + 1)
                for j in range(2):
                    sv = Ss[:, 4 * j:4 * j + 4, h, :]
                    lk(v.tensor_tensor(sv, sv, B(2 * (h % 2) + j, slice(0, RDK), slice(0, 512)).rearrange("p (b e) -> p b e", b=4), ALU.add))
                v.tensor_scalar(Ss[:, :, h, :], Ss[:, :, h, :], float(np.exp(DS * np.log1p(-2.0 ** (-5.0 - h)))), None, ALU.mult).then_inc(S_("Ss_ready"), 1)

            def dve_scan_sample(v, lk):
                vr = stage[:, 0, V_W, :]
                for h in range(WH):
                    if h >= 2:
                        v.wait_ge(S_("scan_s_x"), h - 1)
                    for j in range(2):
                        ins = v.tensor_tensor(ex_k[:, h % 2, j], T4[:, h, j, 0:NS].unsqueeze(1).to_broadcast([WN, DB, NS]), expk[:], ALU.mult)
                    ins.then_inc(S_("scan_ex_k"), 1)
                v.wait_ge(S_("sas_ready"), 2 * NT + 1)
                for h in range(WH):
                    hs = slice(h * WN, (h + 1) * WN)
                    if h >= 2:
                        v.wait_ge(S_("scan_s_u"), h - 1)
                    v.tensor_tensor(ex_t[:, h % 2, :, 0:WN], sas[0:NS, hs].unsqueeze(1).to_broadcast([NS, DB, WN]), expt[:, :, 0:WN], ALU.mult)
                    v.tensor_tensor(ex_t[:, h % 2, :, WN:2 * WN], vr[0:NS, hs].unsqueeze(1).to_broadcast([NS, DB, WN]), expt[:, :, 0:WN],
                                    ALU.mult).then_inc(S_("scan_ex_t"), 1)
                    if h >= 1:
                        u_state(v, h - 1, lk)
                u_state(v, WH - 1, lk)

            def u_state(v, h, lk):
                v.wait_ge(S_("scan_s_u"), h + 1)
                lk(v.tensor_tensor(Us[:, h], Us[:, h], B(1 + h % 2, slice(0, WN), slice(0, 512)).rearrange("p (b n) -> p b n", b=DB), ALU.add))
                v.tensor_tensor(Us[:, h], Us[:, h], over(pc[:, 0, h, :], WN), ALU.mult).then_inc(S_("Us_ready"), 1)

            levels_before = lambda i: i * LEVELS
            updates_before = lambda i: i * (LEVELS - 1)
            grown_before = lambda i: i * (LEVELS - 2)

            @block.vector
            def _(v):
                v.memset(U[:], 0.0)
                v.memset(sas[:], 0.0)
                v.memset(S[:], 0.0).then_inc(S_("U_ready"), 1)
                v.wait_ge(S_("U_ready"), 1)
                v.sem_inc(S_("S_ready"), 1)
                v.wait_ge(c_loaded, 16 * N_CONST)
                v.wait_ge(loaded, 48)
                dve_a(v, 0, 0, Steps(v, S_("dve_start")))
                with v.Fori(0, NT // 2 - 1) as m:
                    for bf in range(2):
                        lk = Steps(v, chain["dve"], (2 * m + bf) * PER_PAIR)
                        dve_pair(v, 2 * m + bf, bf, lk)
                        assert lk.n == PER_PAIR, lk.n
                lk = Steps(v, S_("dve_end"))
                dve_pair(v, NT - 2, 0, lk)
                i, bf = NT - 1, 1
                b_turned(v, i)
                b_masked(v, i)
                b_first(v, i)
                v.wait_ge(loaded, 48 * (NT + 1))
                v.wait_ge(shift_rows, 16)
                a_shift(v, NT, lk)
                b_level(v, i, 1)
                a_rotary(v, NT, lk)
                b_level(v, i, 2)
                a_keys(v, NT, lk)
                b_level(v, i, 3)
                a_turned_qk(v, NT, lk)
                a_ret_gate(v, NT, 0, lk)
                b_level(v, i, 4)
                a_turned_lora(v, NT, lk)
                b_level(v, i, 5)
                a_rates(v, NT, lk)
                b_state(v, i, 0, bf, lk)
                a_decay(v, NT, 0, lk)
                b_state(v, i, 1, bf, lk)
                b_center(v, i, lk)
                b_out(v, i, bf, lk)
                v.wait_ge(c_loaded, 16 * (N_CONST + 2))
                v.wait_ge(states, 32)
                a_att(v, NT, lk)
                dve_retention_sample(v, lk)
                a_before(v, NT, lk)
                a_ret_norm(v, NT, lk)
                a_operands(v, NT, 0, lk)
                a_ret_out(v, NT, 0, lk)
                v.wait_ge(S_("Ss_stored"), 16)
                v.wait_ge(S_("state_turned"), WH)
                b_turned(v, NT)
                b_masked(v, NT)
                b_first(v, NT)
                for l in range(1, LEVELS_S):
                    b_level(v, NT, l)
                dve_scan_sample(v, lk)
                v.wait_ge(S_("y_s_done"), 1)
                b_center(v, NT, lk)
                b_out(v, NT, 0, lk)

            @block.gpsimd
            def _(po):
                po.memset(expo[:], -0.5).then_inc(S_("expo"), 1)
                po.wait_ge(S_("expo"), 1)
                po.wait_ge(c_loaded, 16 * N_CONST)

                def level(i, l):
                    for g in range(2):
                        if l == 0:
                            po.wait_ge(S_("M4_ready"), WH * i + 4 * g + 4)
                        if l == 1:
                            po.wait_ge(S_("TT_first"), 2 * i + g + 1)
                        if l >= 2:
                            po.wait_ge(S_("X_done"), 2 * updates_before(i) + 2 * (l - 2) + g + 1)
                        po.tensor_tensor(AL[:, g], M4[:, 4 * g:4 * g + 4, 0, :],
                                         masks[:, 4 + l, :].unsqueeze(1).to_broadcast([P, 4, P]), ALU.mult).then_inc(S_("AL_ready"), 1)

                def key_norm(j):
                    po.wait_ge(S_("kk_sq"), j + 1)
                    po.tensor_tensor(st[:, 2, :], st[:, 1, :], expo[:], ALU.pow).then_inc(S_("kk_rn"), 1)

                def ret_norm(j):
                    po.wait_ge(S_("ret_ms"), j + 1)
                    po.tensor_tensor(st[:, 5, 0:RH], st[:, 4, 0:RH], expo[:, 0:RH], ALU.pow).then_inc(S_("ret_rn"), 1)

                def y_norm(i):
                    po.wait_ge(S_("y_ms"), i + 1)
                    po.tensor_tensor(stb[:, 3, :], stb[:, 2, :], expo[:], ALU.pow).then_inc(S_("y_rn"), 1)

                def pair(i):
                    for l in range(4):
                        level(i, l)
                    key_norm(i + 1)
                    level(i, 4)
                    level(i, 5)
                    y_norm(i)
                    ret_norm(i + 1)

                key_norm(0)
                ret_norm(0)
                with po.Fori(0, NT - 1) as i:
                    pair(i)
                for l in range(LEVELS):
                    level(NT - 1, l)
                    if l == 3:
                        key_norm(NT)
                y_norm(NT - 1)
                po.wait_ge(c_loaded, 16 * (N_CONST + 2))
                ret_norm(NT)
                for l in range(LEVELS_S):
                    level(NT, l)
                y_norm(NT)

            def act_lora(act, j, bf):
                act_lora_first(act, j, bf)
                act_lora_last(act, j, bf)

            def act_lora_first(act, j, bf):
                act.wait_ge(S_("shifted"), j + 1)
                hw = OR + 3 * WW
                act.activation(lora[:, 0:64], pin[:, hw:hw + 64], ACT.Tanh)
                act.copy(lora[:, 64:128], pin[:, hw + 64:hw + 128])
                act.activation(stage[:, bf, G_R, :], pin[:, OG:OG + RW], ACT.Tanh, scale=0.5)

            def act_lora_last(act, j, bf):
                hw = OR + 3 * WW
                act.copy(stage[:, bf, V_W, :], pin[:, OR + 2 * WW:OR + 3 * WW])
                act.copy(stage[:, bf, V_R, :], pin[:, OV:OV + RW])
                act.activation(lora[:, 128:256], pin[:, hw + 128:hw + 256], ACT.Tanh, scale=0.5).then_inc(S_("lora_act"), 1)

            def act_rates(act, j):
                act.wait_ge(S_("z_ready"), j + 1)
                act.activation(sg[:], sg[:], ACT.Tanh, scale=0.5).then_inc(S_("z_tanh"), 1)

            def act_gate(act, j, bf):
                act.wait_ge(S_("g_done"), j + 1)
                act.copy(stage[:, bf, G_W, :], B(4)).then_inc(S_("gate_copied"), 1)

            def act_decays(act, j, bf, nch):
                act.wait_ge(S_("L_ready"), j + 1)
                act.activation(pinc[:], B(4), ACT.Exp)
                act.activation(pinv[:], B(4), ACT.Exp, scale=-1.0).then_inc(S_("L_read"), 1)
                act.activation(pc[:, bf, :, 0:nch], B(5, slice(0, WN), slice(0, WH * nch)).rearrange("p (h c) -> p h c", h=WH), ACT.Exp)
                act.wait_ge(S_("lx_ready"), j + 1)
                act.activation(sg[:, 0, :], sg[:, 0, :], ACT.Exp).then_inc(S_("decays"), 1)

            def act_turned(act, i):
                for h in range(1, WH, 2):
                    act.wait_ge(S_("headT"), WH * i + h + 1)
                    act.copy(T4[:, h, :, :], B(h % 4, slice(0, WN), slice(0, 512)).rearrange("p (a b) -> p a b", a=4)).then_inc(S_("T4_ready_act"), 1)

            def act_T(act, i, l, levels):
                for g in range(2):
                    act.wait_ge(S_("T_turned"), 2 * updates_before(i) + 2 * l + g + 1)
                    act.copy(T[:, g], B(2 + g).rearrange("p (a b) -> p a b", a=4)).then_inc(S_("T_ready"), 1)

            def act_X(act, i, l):
                for g in range(2):
                    act.wait_ge(S_("X_done"), 2 * updates_before(i) + 2 * (l - 1) + g + 1)
                    act.copy(X[:, g], B(g).rearrange("p (a b) -> p a b", a=4)).then_inc(S_("X_ready"), 1)

            def act_scan(act, i, c):
                act.wait_ge(S_("x_done"), 2 * i + c + 1)
                act.copy(xs[rows[c], :], PS[rows[c], 2, :]).then_inc(S_("xs_ready"), 1)
                act.wait_ge(S_("sa_done"), 2 * i + c + 1)
                act.copy(sas[rows[c], :], PS[rows[c], 3, :]).then_inc(S_("sas_ready"), 1)

            def act_levels(act, i, levels, lora_of=None):
                act_T(act, i, 0, levels)
                for l in range(1, levels):
                    act_X(act, i, l)
                    if l < levels - 1:
                        act_T(act, i, l, levels)
                    if lora_of and l == 1:
                        act_lora_first(act, *lora_of)
                    if lora_of and l == 2:
                        act_lora_last(act, *lora_of)

            def act_pair(act, i, bf):
                act_turned(act, i)
                act_levels(act, i, LEVELS, (i + 1, 1 - bf))
                act_scan(act, i, 0)
                act_rates(act, i + 1)
                act_gate(act, i + 1, 1 - bf)
                act_scan(act, i, 1)
                act_decays(act, i + 1, 1 - bf, 2)

            @block.scalar
            def _(act):
                act.wait_ge(S_("U_ready"), 1)
                act_lora(act, 0, 0)
                act_rates(act, 0)
                act_gate(act, 0, 0)
                act_decays(act, 0, 0, 2)
                with act.Fori(0, NT // 2 - 1) as m:
                    for bf in range(2):
                        act_pair(act, 2 * m + bf, bf)
                act_pair(act, NT - 2, 0)
                act_turned(act, NT - 1)
                act_levels(act, NT - 1, LEVELS, (NT, 0))
                act_scan(act, NT - 1, 0)
                act_rates(act, NT)
                act_scan(act, NT - 1, 1)
                act.wait_ge(S_("U_turns"), 1)
                act.copy(xs[0:WN, :], B(2, slice(0, WN), slice(0, 512))).then_inc(S_("U_turned"), 1)
                act.wait_ge(S_("o_w_ready"), NT)
                for h in range(WH):
                    act.wait_ge(S_("state_turns"), h + 1)
                    act.copy(Us[:, h], B(4 + h % 4, slice(0, WN), slice(0, 512)).rearrange("p (b n) -> p b n", b=DB)).then_inc(S_("state_turned"), 1)
                act_gate(act, NT, 0)
                act_decays(act, NT, 0, DB)
                act.wait_ge(S_("Ss_stored"), 16)
                act_turned(act, NT)
                act_levels(act, NT, LEVELS_S)
                act.wait_ge(S_("states_stored"), 32)
                act.wait_ge(S_("x_done"), 2 * NT + 1)
                act.copy(xs[0:NS, :], PS[0:NS, 6, :]).then_inc(S_("xs_ready"), 1)
                act.wait_ge(S_("sa_done"), 2 * NT + 1)
                act.copy(sas[0:NS, :], PS[0:NS, 7, :]).then_inc(S_("sas_ready"), 1)
                act.wait_ge(S_("y_s_done"), 1)
                for h in range(WH):
                    act.wait_ge(S_("back_turns"), h + 1)
                    act.copy(Uv[:, :, h, :], B(3 + h % 2, slice(0, WN), slice(0, 512)).rearrange("p (b n) -> p b n", b=DB)).then_inc(S_("Us_turned"), 1)

            def passed(pe):
                pe.sem_inc(S_("passed"), 1)

            def p_turn_qk(pe, j):
                pe.wait_ge(S_("qk_ready"), j + 1)
                passed(pe)
                for n in range(2 * RH):
                    ins = pe.transpose(B(6 + n // 4, slice(0, RDK), slice(n % 4 * P, n % 4 * P + P)), qk[:, n, :], ident[:])
                ins.then_inc(S_("qkT"), 1)

            def p_turn_lora(pe, j):
                pe.wait_ge(S_("lora_ready"), j + 1)
                passed(pe)
                for n in range(2):
                    pe.transpose(B(6, slice(0, 64), slice(n * P, (n + 1) * P)), lora[:, 64 * n:64 * n + 64], ident[:])
                pe.transpose(B(6, slice(0, P), slice(256, 384)), lora[:, 128:256], ident[:]).then_inc(S_("loraT"), 1)

            def p_rates(pe, j):
                pe.wait_ge(S_("loraT_ready"), j + 1)
                pe.matmul(B(6), loT[:, 0, :], w2[:], start=True, stop=True)
                pe.matmul(B(7), loT[:, 1, :], a2[:], start=True, stop=True).then_inc(S_("rates"), 1)

            def p_gate_att(pe, j):
                pe.matmul(B(4), hgT[:], g2[:], start=True, stop=True).then_inc(S_("g_done"), 1)
                for h in range(RH):
                    ins = pe.matmul(B(5, slice(0, P), slice(h * P, h * P + P)), qkT[:, RH + h, :], qkT[:, h, :], start=True, stop=True)
                ins.then_inc(S_("att_done"), 1)

            def p_retention(pe, j, bf):
                pe.wait_ge(S_("att_ready"), j + 1)
                pe.wait_ge(S_("z_ready"), j + 1)
                pe.wait_ge(S_("S_ready"), j + 1)
                for h in range(RH):
                    vh = stage[:, bf, V_R, h * RDV:(h + 1) * RDV]
                    pe.matmul(B(6, slice(0, P), slice(h * P, h * P + P)), att[:, h, :], vh, start=True, stop=False)
                    pe.matmul(B(6, slice(0, P), slice(h * P, h * P + P)), qkT[:, h, :], S[:, h, :], start=False, stop=True)
                    ins = pe.matmul(B(7, slice(0, RDK), slice(h * P, h * P + P)), qk[:, RH + h, :], vh, start=True, stop=True)
                ins.then_inc(S_("ret_done"), 1)

            def p_decays(pe, j, nch):
                pe.wait_ge(S_("gate_copied"), j + 1)
                pe.wait_ge(S_("lw_ready"), j + 1)
                pe.matmul(B(4), masks[:, 1, :], lw[:], start=True, stop=True)
                for h in range(WH):
                    ins = pe.matmul(B(5, slice(0, WN), slice(h * nch, (h + 1) * nch)), lw[:, h * WN:(h + 1) * WN], chunk[:, 0:nch], start=True, stop=True)
                ins.then_inc(S_("L_ready"), 1)

            def p_turn_heads(pe, i, bf):
                pe.wait_ge(S_("arbk_ready"), i + 1)
                passed(pe)
                for h in range(WH):
                    if h >= 4:
                        pe.wait_ge(S_("T4_ready_act" if h % 2 else "T4_ready_dve"), 4 * i + (h - 4) // 2 + 1)
                        passed(pe)
                    for n in range(4):
                        ins = pe.transpose(B(h % 4, slice(0, WN), slice(n * P, n * P + P)), stage[:, bf, n, h * WN:(h + 1) * WN], ident[:])
                    ins.then_inc(S_("headT"), 1)

            def p_products(pe, i):
                for h in range(WH):
                    pe.wait_ge(S_("T4_ready_act" if h % 2 else "T4_ready_dve"), 4 * i + h // 2 + 1)
                    if h >= 4:
                        pe.wait_ge(S_("M4_ready"), WH * i + h - 3)
                    ar = T4[:, h, 0:2, :]
                    pe.matmul(B(4 + h % 4, slice(0, P), slice(0, 256)), T4[:, h, 2, :], ar, start=True, stop=True)
                    pe.matmul(B(4 + h % 4, slice(0, P), slice(256, 512)), T4[:, h, 3, :], ar, start=True, stop=True).then_inc(S_("products"), 1)

            def p_turn_T(pe, i, l):
                for g in range(2):
                    if l:
                        pe.wait_ge(S_("TT_ready"), 2 * updates_before(i) + 2 * (l - 1) + g + 1)
                    else:
                        pe.wait_ge(S_("TT_first"), 2 * i + g + 1)
                    for h in range(4):
                        ins = pe.transpose(B(2 + g, slice(0, P), slice(h * P, h * P + P)), TT[:, g, h, :], ident[:])
                    ins.then_inc(S_("T_turned"), 1)

            def p_level(pe, i, l, levels):
                n0 = 2 * updates_before(i) + 2 * (l - 1)
                for g in range(2):
                    pe.wait_ge(S_("AL_ready"), 2 * levels_before(i) + 2 * l + g + 1)
                    pe.wait_ge(S_("T_ready"), n0 + g + 1)
                    for h in range(4):
                        ins = pe.matmul(B(g, slice(0, P), slice(h * P, h * P + P)), AL[:, g, h, :], T[:, g, h, :], start=True, stop=True)
                    ins.then_inc(S_("X_done"), 1)
                for g in range(2):
                    pe.wait_ge(S_("X_ready"), n0 + g + 1)
                    for h in range(4):
                        ins = pe.matmul(B(4 + g, slice(0, P), slice(h * P, h * P + P)), X[:, g, h, :], TT[:, g, h, :], start=True, stop=True)
                    ins.then_inc(S_("dTT"), 1)
                if l < levels - 1:
                    p_turn_T(pe, i, l)

            hcol = [slice(h * WN, (h + 1) * WN) for h in range(WH)]

            def p_scan_x(pe, i, c, bf):
                r = rows[c]
                pe.wait_ge(S_("U_ready"), 2 * i + c + 1)
                passed(pe)
                for h in range(WH):
                    pe.matmul(PS[r, 2, hcol[h]], M4[:, h, 2, r], stage[:, bf, V_W, hcol[h]], start=True, stop=False)
                    ins = pe.matmul(PS[r, 2, hcol[h]], T4[:, h, 0, r], U[:, h, :], start=False, stop=True)
                ins.then_inc(S_("x_done"), 1)

            def p_scan_sa(pe, i, c):
                r = rows[c]
                pe.wait_ge(S_("xs_ready"), 2 * i + c + 1)
                passed(pe)
                for h in range(WH):
                    ins = pe.matmul(PS[r, 3, hcol[h]], TT[r, h // 4, h % 4, r], xs[r, hcol[h]], start=True, stop=True)
                ins.then_inc(S_("sa_done"), 1)

            def p_scan_u(pe, i, c, bf):
                r = rows[c]
                pe.wait_ge(S_("sas_ready"), 2 * i + c + 1)
                passed(pe)
                for h in range(WH):
                    vh = stage[:, bf, V_W, hcol[h]]
                    pe.matmul(PS[0:WN, 1, hcol[h]], stage[r, bf, 2, hcol[h]], sas[r, hcol[h]], start=True, stop=False)
                    pe.matmul(PS[0:WN, 1, hcol[h]], stage[r, bf, 3, hcol[h]], stage[r, bf, V_W, hcol[h]], start=False, stop=True)
                    pe.matmul(PS[r, 0, hcol[h]], T4[:, h, 1, r], U[:, h, :], start=True, stop=False)
                    pe.matmul(PS[r, 0, hcol[h]], M4[:, h, 1, r], sas[:, hcol[h]], start=False, stop=False)
                    ins = pe.matmul(PS[r, 0, hcol[h]], M4[:, h, 3, r], vh, start=False, stop=True)
                ins.then_inc(S_("U_products"), 1)

            def pe_pair(pe, i, bf):
                p_turn_heads(pe, i, bf)
                p_products(pe, i)
                p_turn_T(pe, i, 0)
                p_level(pe, i, 1, LEVELS)
                p_level(pe, i, 2, LEVELS)
                p_turn_qk(pe, i + 1)
                p_level(pe, i, 3, LEVELS)
                pe.wait_ge(S_("qkT_ready"), i + 2)
                p_turn_lora(pe, i + 1)
                p_level(pe, i, 4, LEVELS)
                p_rates(pe, i + 1)
                p_level(pe, i, 5, LEVELS)
                pe.wait_ge(S_("TT_ready"), 2 * updates_before(i) + 2 * (LEVELS - 1))
                p_scan_x(pe, i, 0, bf)
                p_gate_att(pe, i + 1)
                p_scan_sa(pe, i, 0)
                p_scan_u(pe, i, 0, bf)
                p_scan_x(pe, i, 1, bf)
                p_decays(pe, i + 1, 2)
                p_scan_sa(pe, i, 1)
                p_scan_u(pe, i, 1, bf)
                p_retention(pe, i + 1, 1 - bf)
                pe.wait_ge(S_("y_read"), i + 1)
                pe.wait_ge(S_("S_ready"), i + 3)

            def pe_a(pe, j, bf):
                p_turn_qk(pe, j)
                pe.wait_ge(S_("qkT_ready"), j + 1)
                p_turn_lora(pe, j)
                p_rates(pe, j)
                p_gate_att(pe, j)
                p_retention(pe, j, bf)
                p_decays(pe, j, 2)

            def retention_sample(pe):
                pe.wait_ge(S_("att_ready"), NT + 1)
                pe.wait_ge(S_("z_ready"), NT + 1)
                for h in range(RH):
                    pe.wait_ge(S_("ret_ex"), h + 1)
                    if h >= 2:
                        pe.wait_ge(S_("Ss_ready"), h - 1)
                    col = slice(h * P, h * P + P)
                    pe.matmul(B(6, slice(0, NS), col), att[0:NS, h, 0:NS], stage[0:NS, 0, V_R, h * RDV:(h + 1) * RDV], start=True, stop=False)
                    for b in range(DB):
                        pe.matmul(B(6, slice(0, NS), col), ex_k[:, h % 2, 0, b, :], Ss[:, b, h, :], start=False, stop=b == DB - 1)
                    for j in range(2):
                        ins = pe.matmul(B(2 * (h % 2) + j, slice(0, RDK), slice(0, 512)), qk[0:NS, RH + h, :],
                                        ex_t[:, h % 2, 4 * j:4 * j + 4, :], start=True, stop=True)
                    ins.then_inc(S_("ret_s_done"), 1)
                pe.wait_ge(S_("ro_s"), 1)

            def turn_back(pe, h):
                pe.wait_ge(S_("Us_ready"), h + 1)
                if h >= 2:
                    pe.wait_ge(S_("Us_turned"), h - 1)
                for b in range(DB):
                    ins = pe.transpose(B(3 + h % 2, slice(0, WN), slice(b * WN, (b + 1) * WN)), Us[:, h, b, :], ident[0:WN, 0:WN])
                ins.then_inc(S_("back_turns"), 1)

            @block.tensor
            def _(pe):
                pe.wait_ge(c_loaded, 16 * N_CONST)
                pe_a(pe, 0, 0)
                pe.wait_ge(S_("S_ready"), 2)
                with pe.Fori(0, NT // 2 - 1) as m:
                    for bf in range(2):
                        pe_pair(pe, 2 * m + bf, bf)
                pe_pair(pe, NT - 2, 0)
                i, bf = NT - 1, 1
                p_turn_heads(pe, i, bf)
                p_products(pe, i)
                p_turn_T(pe, i, 0)
                p_level(pe, i, 1, LEVELS)
                p_level(pe, i, 2, LEVELS)
                p_turn_qk(pe, NT)
                p_level(pe, i, 3, LEVELS)
                pe.wait_ge(S_("qkT_ready"), NT + 1)
                p_turn_lora(pe, NT)
                p_level(pe, i, 4, LEVELS)
                p_rates(pe, NT)
                p_level(pe, i, 5, LEVELS)
                pe.wait_ge(S_("TT_ready"), 2 * updates_before(i) + 2 * (LEVELS - 1))
                for c in range(2):
                    p_scan_x(pe, i, c, bf)
                    p_scan_sa(pe, i, c)
                    p_scan_u(pe, i, c, bf)
                pe.wait_ge(S_("U_ready"), 2 * NT + 1)
                for h in range(WH):
                    ins = pe.transpose(B(2, slice(0, WN), slice(h * WN, (h + 1) * WN)), U[:, h, :], ident[0:WN, 0:WN])
                ins.then_inc(S_("U_turns"), 1)
                pe.wait_ge(states, 32)
                pe.wait_ge(S_("z_ready"), NT + 1)
                for h in range(WH):
                    if h >= 4:
                        pe.wait_ge(S_("state_turned"), h - 3)
                    for b in range(DB):
                        ins = pe.transpose(B(4 + h % 4, slice(0, WN), slice(b * WN, (b + 1) * WN)), Uv[:, b, h, :], ident[0:WN, 0:WN])
                    ins.then_inc(S_("state_turns"), 1)
                pe.wait_ge(S_("U_turned"), 1)
                pe.wait_ge(S_("state_turned"), WH)
                pe.wait_ge(c_loaded, 16 * (N_CONST + 2))
                p_gate_att(pe, NT)
                retention_sample(pe)
                p_decays(pe, NT, DB)
                pe.wait_ge(S_("y_read"), NT)
                p_turn_heads(pe, NT, 0)
                p_products(pe, NT)
                p_turn_T(pe, NT, 0)
                for l in range(1, LEVELS_S):
                    p_level(pe, NT, l, LEVELS_S)
                hs = [slice(h * WN, (h + 1) * WN) for h in range(WH)]
                vh = [stage[0:NS, 0, V_W, h * WN:(h + 1) * WN] for h in range(WH)]
                r = slice(0, NS)
                pe.wait_ge(S_("TT_ready"), 2 * updates_before(NT) + 2 * (LEVELS_S - 1))
                for h in range(WH):
                    pe.wait_ge(S_("scan_ex_k"), h + 1)
                    pe.matmul(PS[r, 6, hs[h]], M4[r, h, 2, r], vh[h], start=True, stop=False)
                    for b in range(DB):
                        pe.matmul(PS[r, 6, hs[h]], ex_k[:, h % 2, 0, b, :], Us[:, h, b, :], start=False, stop=b == DB - 1)
                    pe.matmul(PS[r, 0, hs[h]], M4[r, h, 3, r], vh[h], start=h == 0, stop=False, skip_group_check=True)
                    for b in range(DB):
                        ins = pe.matmul(PS[r, 0, hs[h]], ex_k[:, h % 2, 1, b, :], Us[:, h, b, :], start=False, stop=False, skip_group_check=True)
                    ins.then_inc(S_("scan_s_x" if h < WH - 1 else "x_done"), 1)
                pe.wait_ge(S_("xs_ready"), 2 * NT + 1)
                for h in range(WH):
                    ins = pe.matmul(PS[r, 7, hs[h]], TT[r, h // 4, h % 4, r], xs[r, hs[h]], start=True, stop=True)
                ins.then_inc(S_("sa_done"), 1)
                pe.wait_ge(S_("sas_ready"), 2 * NT + 1)
                for h in range(WH):
                    ins = pe.matmul(PS[r, 0, hs[h]], M4[r, h, 1, r], sas[r, hs[h]], start=False, stop=True, skip_group_check=True)
                ins.then_inc(S_("y_s_done"), 1)
                for h in range(WH):
                    pe.wait_ge(S_("scan_ex_t"), h + 1)
                    if h >= 2:
                        pe.wait_ge(S_("Us_ready"), h - 1)
                    bank = 1 + h % 2
                    pe.matmul(PS[0:WN, bank, :], stage[r, 0, 2, hs[h]], ex_t[:, h % 2, :, 0:WN], start=True, stop=False)
                    pe.matmul(PS[0:WN, bank, :], stage[r, 0, 3, hs[h]], ex_t[:, h % 2, :, WN:2 * WN], start=False, stop=True).then_inc(S_("scan_s_u"), 1)
                    if h >= 1:
                        turn_back(pe, h - 1)
                turn_back(pe, WH - 1)




def phase_attention(core, PS):
    nc, d, sem = core.nc, core.dram, core.sem
    S_ = lambda n: sem("at_" + n)
    NR = NG + NE
    SC = MDH ** -0.5
    MT = NMEM // P
    W_MQ, W_MO, W_OUT = 0, 1, 2
    with ExitStack() as ctx:
        sb = lambda n, s, t=F32: ctx.enter_context(nc.sbuf_tensor("at_" + n, s, t))
        w = sb("w", [P, 3, KC, D])
        kT, Vm = sb("kT", [P, KC, NMEM]), sb("v", [P, MT, D])
        wr = sb("wr", [P, KC, NR])
        br, gf = sb("br", [P, NR]), sb("gf", [P, D])
        gkv, g, ident, expo = sb("gkv", [P, KC]), sb("g", [P, KC]), sb("ident", [P, P]), sb("expo", [P, 2])
        h, mt, hq, hn = sb("h", [P, 2, D]), sb("mt", [P, D]), sb("hq", [P, D]), sb("hn", [P, D])
        aT, bT, qT, oT = sb("aT", [P, KC, P]), sb("bT", [P, KC, P]), sb("qT", [P, KC, P]), sb("oT", [P, KC, P])
        p, lg, st = sb("p", [P, MH, NMEM]), sb("lg", [P, NR]), sb("st", [P, 24])
        kc, kcT = sb("kc", [P, 2, MT, D]), sb("kcT", [P, MT, KC, P])
        sT = sb("sT", [P, 2, 256])
        mem, mk, memT = kc[:, 0], kc[:, 1], kcT
        slots = [kc[:, 0], kc[:, 1]] + [w[:, j, 2 * n:2 * n + 2] for j in (W_OUT, W_MQ) for n in range(4)]
        OWN, AFTER_OUT = 2, 6
        slot_of = lambda load: load if load < len(slots) else load - len(slots)
        uses = lambda load: load // len(slots) + 1
        two = lambda b: PS[:, b:b + 2, :].rearrange("p a (c t) -> p (a c) t", t=P)
        flat2 = lambda b: PS[:, b:b + 2, :].rearrange("p a n -> p (a n)")

        with nc.Block() as block:
            @block.sync
            def _(sp):
                def load_w(j, n):
                    wv = d[n][0].rearrange("(c p) n -> p c n", p=P)
                    for hf in range(2):
                        sp.dma_start(w[:, j, :, hf * 512:hf * 512 + 512], wv[:, :, hf * 512:hf * 512 + 512]).then_inc(S_(f"{n}{hf}"), 16)

                def load_mixed(i):
                    sp.dma_start(mt[:], d["mixed"][bass.ds(i * P, P), :]).then_inc(S_("mixed_loaded"), 16)

                def load_x(i, par):
                    sp.dma_start(h[:, par], d["x"][bass.ds(i * P, P), :]).then_inc(S_("x_loaded"), 16)

                def load_cache(first, last):
                    for n in range(first, last):
                        if n >= len(slots):
                            sp.wait_ge(S_("kc_turned"), MT * (n - len(slots) + 1))
                        src = d["cache_mem_k" if n < DB else "cache_mem_v"][0, n % DB]
                        sp.dma_start(slots[slot_of(n)], src.rearrange("(m p) h n -> p m (h n)", p=P)).then_inc(S_(f"slot{slot_of(n)}"), 16)

                sp.dma_start(mem, d["mem_prompt"][0].rearrange("(m p) n -> p m n", p=P)).then_inc(S_("small"), 16)
                sp.dma_start(ident[:], d["ident"]).then_inc(S_("small"), 16)
                with nc.allow_non_contiguous_dma(reason="a gain by channel"):
                    sp.dma_start(gkv[:], d["g_mem_kv"][0].rearrange("(c p) -> p c", p=P)).then_inc(S_("small"), 16)
                load_w(W_MQ, "w_mk")
                load_w(W_MO, "w_mv")
                load_mixed(0)
                for par in range(2):
                    load_x(par, par)
                load_w(W_OUT, "w_out")
                with nc.allow_non_contiguous_dma(reason="small"):
                    for dst, src in [(g[:], d["g_mem_q"][0].rearrange("(c p) -> p c", p=P)),
                                     (wr[:, :, 0:NG], d["w_group_router"][0].rearrange("(c p) n -> p c n", p=P)),
                                     (wr[:, :, NG:NR], d["w_expert_router"][0].rearrange("(c p) n -> p c n", p=P)),
                                     (br[:, 0:NG], wide_row(d["b_group_router"][0], NG)), (br[:, NG:NR], wide_row(d["b_expert_router"][0], NE)),
                                     (gf[:], wide_row(d["g_ffn"][0], D))]:
                        sp.dma_start(dst, src).then_inc(S_("consts"), 16)
                sp.wait_ge(S_("mem_projected"), 4)
                load_w(W_MQ, "w_mq")
                sp.wait_ge(S_("k_ready"), 4)
                sp.dma_start(d["out_mk"].rearrange("(m p) n -> p m n", p=P), mk).then_inc(S_("mk_stored"), 16)
                sp.wait_ge(S_("mem_projected"), 8)
                load_w(W_MO, "w_mo")
                sp.wait_ge(S_("v_ready"), 4)
                sp.dma_start(d["out_mv"].rearrange("(m p) n -> p m n", p=P), Vm[:]).then_inc(S_("mv_stored"), 16)
                sp.wait_ge(S_("mk_stored"), 16)
                sp.wait_ge(S_("k_turned"), 4)
                load_cache(0, OWN)
                sp.wait_ge(S_("turned0"), 1)
                load_mixed(1)

                def store_h2(i, par):
                    sp.wait_ge(S_("h2_ready"), i + 1)
                    sp.dma_start(d["h2"][bass.ds(i * P, P), :], h[:, par]).then_inc(S_("h2_stored"), 16)

                def store_hn(i):
                    sp.wait_ge(S_("hn_ready"), i + 1)
                    sp.dma_start(d["hn"][bass.ds(i * P, P), :], hn[:]).then_inc(S_("hn_stored"), 16)

                def store_lg(i):
                    sp.wait_ge(S_("lg_ready"), i + 2)
                    sp.dma_start(d["logits"][bass.ds(i * P, P), :], lg[:]).then_inc(S_("lg_stored"), 16)

                def steady(i, par):
                    sp.wait_ge(S_("turned0"), i + 2)
                    load_mixed(i + 2)
                    store_h2(i, par)
                    store_hn(i)
                    sp.wait_ge(S_("h2_stored"), 16 * i + 16)
                    load_x(i + 2, par)
                    store_lg(i)

                sp.sem_inc(S_("hn_stored"), 16)
                sp.sem_inc(S_("lg_stored"), 16)
                with sp.Fori(0, (NT - 1) // 2) as m:
                    for par in range(2):
                        steady(2 * m + par, par)
                steady(NT - 2, 0)
                sp.wait_ge(S_("proj0"), TILES)
                load_cache(OWN, AFTER_OUT)
                store_h2(NT - 1, 1)
                store_hn(NT - 1)
                sp.wait_ge(S_("proj1"), TILES)
                load_cache(AFTER_OUT, len(slots))
                store_lg(NT - 1)
                load_cache(len(slots), 2 * DB)
                store_h2(NT, 0)
                store_hn(NT)
                store_lg(NT)
                sp.wait_ge(S_("h2_stored"), 16 * TILES)
                for n in ("hn_stored", "lg_stored"):
                    sp.wait_ge(S_(n), 16 * TILES + 16)
                sp.wait_ge(S_("mv_stored"), 16)

            def dve_memory(v):
                lk = Steps(v, S_("dve_mem"))
                v.wait_ge(S_("small"), 48)
                for m in range(MT):
                    lk(v.tensor_tensor_reduce(hn[:], mem[:, m], mem[:, m], 1.0, 0.0, ALU.mult, ALU.add, st[:, m:m + 1]))
                v.tensor_scalar(st[:, 2:4], st[:, 0:2], 1.0 / D, EPS, ALU.mult, ALU.add).then_inc(S_("mem_ms"), 1)
                v.wait_ge(S_("mem_rstd"), 1)
                for m in range(MT):
                    v.tensor_scalar(mem[:, m], mem[:, m], st[:, 4 + m:5 + m], None, ALU.mult).then_inc(S_("mem_n"), 1)
                for m in range(MT):
                    for b in range(2):
                        v.wait_ge(S_("mem_turned"), 2 * m + b + 1)
                        v.tensor_tensor(memT[:, m, 4 * b:4 * b + 4, :], PS[:, 2 * m + b, :].rearrange("p (c t) -> p c t", c=4),
                                        gkv[:, 4 * b:4 * b + 4].unsqueeze(2).to_broadcast([P, 4, P]), ALU.mult).then_inc(S_("memT"), 1)
                for n in range(4):
                    v.wait_ge(S_("k_turned"), n + 1)
                    v.tensor_copy(kT[:, 4 * (n % 2):4 * (n % 2) + 4, (n // 2) * P:(n // 2) * P + P],
                                  PS[:, n, :].rearrange("p (c t) -> p c t", c=4)).then_inc(S_("kT"), 1)

            def mean_square(v, src, scratch, lk):
                lk(v.tensor_tensor_reduce(scratch, src, src, 1.0, 0.0, ALU.mult, ALU.add, st[:, 0:1]))
                v.tensor_scalar(st[:, 1:2], st[:, 0:1], 1.0 / D, EPS, ALU.mult, ALU.add).then_inc(S_("ms"), 1)

            def v_front(v, j, par, norm, lk):
                v.wait_ge(S_("x_loaded"), 16 * j + 16)
                v.wait_ge(S_("proj0"), j + 1)
                lk(v.tensor_tensor(h[:, par], h[:, par], flat2(2), ALU.add))
                mean_square(v, h[:, par], hq[:], lk)
                v.wait_ge(S_("rstd"), norm)
                v.tensor_scalar(hq[:], h[:, par], st[:, 2:3], None, ALU.mult).then_inc(S_("hq"), 1)

            def v_front_turned(v, j):
                v.wait_ge(S_("turned1"), j + 1)
                v.tensor_tensor(aT[:], two(0), g[:].unsqueeze(2).to_broadcast([P, KC, P]), ALU.mult).then_inc(S_("hT"), 1)

            def v_max(v, i, n, bank, lk):
                v.wait_ge(S_("scores"), i + 1)
                src = PS[:, bank:bank + 2, :].rearrange("p a (b m) -> p (a b) m", m=NMEM)[:, 0:n, :]
                lk(v.tensor_reduce(st[:, 4:4 + n], src, AX.X, ALU.max))
                v.tensor_scalar(st[:, 8:8 + n], st[:, 4:4 + n], -SC, None, ALU.mult).then_inc(S_("nmax"), 1)

            def v_divide(v, i, n, lk):
                v.wait_ge(S_("exps"), i + 1)
                lk(v.reciprocal(st[:, 16:16 + n], st[:, 12:12 + n]))
                v.tensor_tensor(p[:, 0:n, :], p[:, 0:n, :], st[:, 16:16 + n].unsqueeze(2).to_broadcast([P, n, NMEM]), ALU.mult).then_inc(S_("p_ready"), 1)

            def v_oT(v, i):
                v.wait_ge(S_("oT_done"), i + 1)
                v.tensor_copy(oT[:], two(6)).then_inc(S_("oT"), 1)

            def v_back(v, i, par, norm, lk):
                v.wait_ge(S_("proj2"), i + 1)
                lk(v.tensor_tensor(h[:, par], h[:, par], flat2(2), ALU.add))
                v.wait_ge(S_("hn_stored"), 16 * i + 16)
                v.sem_inc(S_("h2_ready"), 1)
                mean_square(v, h[:, par], hn[:], lk)
                v.wait_ge(S_("rstd"), norm)
                lk(v.tensor_scalar(hn[:], h[:, par], st[:, 2:3], None, ALU.mult))
                v.tensor_tensor(hn[:], hn[:], gf[:], ALU.mult).then_inc(S_("hn_ready"), 1)

            def v_logits(v, i):
                v.wait_ge(S_("turned3"), i + 1)
                v.tensor_copy(bT[:], two(0)).then_inc(S_("hnT"), 1)
                v.wait_ge(S_("routed"), i + 1)
                v.wait_ge(S_("lg_stored"), 16 * i + 16)
                v.tensor_tensor(lg[:], PS[:, 6, 0:NR], br[:], ALU.add).then_inc(S_("lg_ready"), 1)

            @block.vector
            def _(v):
                dve_memory(v)
                v.sem_inc(S_("lg_ready"), 1)
                v.wait_ge(S_("consts"), 16 * 6)
                v_front(v, 0, 0, 1, Steps(v, S_("dve_first")))
                v_front_turned(v, 0)
                with v.Fori(0, NT // 2) as m:
                    for par in range(2):
                        i = 2 * m + par
                        lk = Steps(v, S_("dve"), i * PER_AT)
                        v_max(v, i, MH, 4, lk)
                        v_divide(v, i, MH, lk)
                        v_front(v, i + 1, 1 - par, 2 * i + 2, lk)
                        v_oT(v, i)
                        v_front_turned(v, i + 1)
                        v_back(v, i, par, 2 * i + 3, lk)
                        v_logits(v, i)
                        assert lk.n == PER_AT, lk.n
                lk = Steps(v, S_("dve"), NT * PER_AT)
                for b in range(DB):
                    v.wait_ge(S_("kc_turned"), MT * b + 1)
                    if b:
                        v.wait_ge(S_("sT_done"), MT * (b - 1) + 1)
                    v.tensor_copy(kcT[:, 0], two(0)).then_inc(S_("kcT0"), 1)
                v.wait_ge(S_("sT_done"), MT * DB)
                v.tensor_copy(sT[:].rearrange("p m n -> p (m n)"), PS[:, 4, :]).then_inc(S_("sT"), 1)
                v_max(v, NT, 2, 6, lk)
                v_divide(v, NT, 2, lk)
                v.wait_ge(S_("pT_done"), TILES)
                v.tensor_copy(sT[:].rearrange("p m n -> p (m n)"), PS[:, 0, :]).then_inc(S_("pT"), 1)
                v.wait_ge(S_("oT_done"), TILES)
                v.tensor_copy(oT[:, :, 0:NS], PS[:, 4, :].rearrange("p (c t) -> p c t", c=KC)).then_inc(S_("oT"), 1)
                v_back(v, NT, 0, 2 * TILES, lk)
                v_logits(v, NT)

            @block.gpsimd
            def _(po):
                po.memset(expo[:], -0.5).then_inc(S_("expo"), 1)
                po.wait_ge(S_("expo"), 1)
                po.wait_ge(S_("mem_ms"), 1)
                po.tensor_tensor(st[:, 4:6], st[:, 2:4], expo[:], ALU.pow).then_inc(S_("mem_rstd"), 1)
                with po.Fori(0, 2 * TILES) as i:
                    po.wait_ge(S_("ms"), i + 1)
                    po.tensor_tensor(st[:, 2:3], st[:, 1:2], expo[:, 0:1], ALU.pow).then_inc(S_("rstd"), 1)

            def a_mixT(act, j):
                act.wait_ge(S_("turned0"), j + 1)
                act.copy(aT[:], two(0)).then_inc(S_("mixT"), 1)

            def a_exps(act, i, n, bank):
                act.wait_ge(S_("nmax"), i + 1)
                for j in range(n):
                    ins = act.activation(p[:, j, :], PS[:, bank + j // 2, j % 2 * NMEM:(j % 2 + 1) * NMEM], ACT.Exp,
                                         bias=st[:, 8 + j:9 + j], scale=SC, accum_out=st[:, 12 + j:13 + j])
                ins.then_inc(S_("exps"), 1)

            def a_pT(act, i):
                act.wait_ge(S_("pT_done"), i + 1)
                act.copy(bT[:], two(0)).then_inc(S_("pT"), 1)

            def a_queries(act, j):
                act.wait_ge(S_("proj1"), j + 1)
                act.copy(hq[:], flat2(4)).then_inc(S_("q_ready"), 1)
                act.wait_ge(S_("turned2"), j + 1)
                act.copy(qT[:], two(4)).then_inc(S_("qT"), 1)

            @block.scalar
            def _(act):
                for j in range(2):
                    for hf in range(2):
                        for m in range(MT):
                            act.wait_ge(S_("mem_projected"), 4 * j + 2 * hf + m + 1)
                            dst = (mk, Vm)[j][:, m, hf * 512:hf * 512 + 512]
                            act.copy(dst, PS[:, 4 + 2 * hf + m, :]).then_inc(S_("k_ready" if j == 0 else "v_ready"), 1)
                a_mixT(act, 0)
                a_queries(act, 0)
                with act.Fori(0, NT) as i:
                    a_mixT(act, i + 1)
                    a_exps(act, i, MH, 4)
                    a_pT(act, i)
                    a_queries(act, i + 1)
                for b in range(DB):
                    act.wait_ge(S_("kc_turned"), MT * b + 2)
                    if b:
                        act.wait_ge(S_("sT_done"), MT * (b - 1) + 2)
                    act.copy(kcT[:, 1], two(2)).then_inc(S_("kcT1"), 1)
                a_exps(act, NT, 2, 6)

            def turn(pe, src, bank):
                for c in range(KC):
                    ins = pe.transpose(PS[:, bank + c // 4, c % 4 * P:c % 4 * P + P], src[:, c * P:(c + 1) * P], ident[:])
                return ins

            def project(pe, name, j, bank, src):
                for hf in range(2):
                    pe.wait_ge(S_(f"{name}{hf}"), 16)
                    for k in range(KC):
                        ins = pe.matmul(PS[:, bank + hf, :], src[:, k, :], w[:, j, k, hf * 512:hf * 512 + 512], start=k == 0, stop=k == KC - 1)
                return ins

            def pe_memory(pe):
                for m in range(MT):
                    pe.wait_ge(S_("mem_n"), m + 1)
                    for c in range(KC):
                        ins = pe.transpose(PS[:, 2 * m + c // 4, c % 4 * P:c % 4 * P + P], mem[:, m, c * P:(c + 1) * P], ident[:])
                        if c % 4 == 3:
                            ins.then_inc(S_("mem_turned"), 1)
                for j, name in enumerate(("w_mk", "w_mv")):
                    for hf in range(2):
                        pe.wait_ge(S_(f"{name}{hf}"), 16)
                        for m in range(MT):
                            pe.wait_ge(S_("memT"), 2 * m + 2)
                            if j == 1:
                                pe.wait_ge(S_("k_ready"), 2 * hf + m + 1)
                            for k in range(KC):
                                ins = pe.matmul(PS[:, 4 + 2 * hf + m, :], memT[:, m, k, :], w[:, j, k, hf * 512:hf * 512 + 512], start=k == 0, stop=k == KC - 1)
                            ins.then_inc(S_("mem_projected"), 1)
                    if j == 0:
                        pe.wait_ge(S_("k_ready"), 4)
                        for m in range(MT):
                            for c in range(KC):
                                ins = pe.transpose(PS[:, 2 * m + c // 4, c % 4 * P:c % 4 * P + P], mk[:, m, c * P:(c + 1) * P], ident[:])
                                if c % 4 == 3:
                                    ins.then_inc(S_("k_turned"), 1)

            def p_turn_mixed(pe, j):
                pe.wait_ge(S_("mixed_loaded"), 16 * j + 16)
                turn(pe, mt, 0).then_inc(S_("turned0"), 1)

            def p_output(pe, j):
                pe.wait_ge(S_("mixT"), j + 1)
                project(pe, "w_out", W_OUT, 2, aT).then_inc(S_("proj0"), 1)

            def p_turn_h(pe, j):
                pe.wait_ge(S_("hq"), j + 1)
                turn(pe, hq, 0).then_inc(S_("turned1"), 1)

            def p_queries(pe, j):
                pe.wait_ge(S_("hT"), j + 1)
                project(pe, "w_mq", W_MQ, 4, aT).then_inc(S_("proj1"), 1)

            def p_turn_q(pe, j):
                pe.wait_ge(S_("q_ready"), j + 1)
                turn(pe, hq, 4).then_inc(S_("turned2"), 1)

            def p_scores(pe, i):
                pe.wait_ge(S_("qT"), i + 1)
                for hd in range(MH):
                    for c in range(2):
                        ins = pe.matmul(PS[:, 4 + hd // 2, hd % 2 * NMEM:(hd % 2 + 1) * NMEM], qT[:, 2 * hd + c, :], kT[:, 2 * hd + c, :],
                                        start=c == 0, stop=c == 1)
                ins.then_inc(S_("scores"), 1)

            def p_values(pe, i):
                pe.wait_ge(S_("p_ready"), i + 1)
                turn(pe, p[:].rearrange("p h m -> p (h m)"), 0).then_inc(S_("pT_done"), 1)
                pe.wait_ge(S_("pT"), i + 1)
                pe.wait_ge(S_("lg_ready"), i + 1)
                for cc in range(KC):
                    for m in range(MT):
                        ins = pe.matmul(PS[:, 6 + cc // 4, cc % 4 * P:cc % 4 * P + P], Vm[:, m, cc * P:(cc + 1) * P], bT[:, cc // 2 * 2 + m, :],
                                        start=m == 0, stop=m == MT - 1)
                ins.then_inc(S_("oT_done"), 1)

            def p_memory_output(pe, i):
                pe.wait_ge(S_("oT"), i + 1)
                project(pe, "w_mo", W_MO, 2, oT).then_inc(S_("proj2"), 1)

            def p_turn_hn(pe, i):
                pe.wait_ge(S_("hn_ready"), i + 1)
                turn(pe, hn, 0).then_inc(S_("turned3"), 1)

            def p_router(pe, i):
                pe.wait_ge(S_("hnT"), i + 1)
                for k in range(KC):
                    ins = pe.matmul(PS[:, 6, 0:NR], bT[:, k, :], wr[:, k, :], start=k == 0, stop=k == KC - 1)
                ins.then_inc(S_("routed"), 1)

            def p_attention_sample(pe):
                def turn_keys(u):
                    b, m = u // MT, u % MT
                    pe.wait_ge(S_(f"slot{slot_of(b)}"), 16)
                    if b:
                        pe.wait_ge(S_(f"kcT{m}"), b)
                    turn(pe, slots[slot_of(b)][:, m], 2 * m).then_inc(S_("kc_turned"), 1)
                turn_keys(0)
                for u in range(MT * DB):
                    b, m = u // MT, u % MT
                    if u + 1 < MT * DB:
                        turn_keys(u + 1)
                    pe.wait_ge(S_(f"kcT{m}"), b + 1)
                    for hd in range(MH):
                        col = m * 256 + b * 32 + hd * 8
                        for c in range(2):
                            ins = pe.matmul(PS[:, 4, col:col + 8], kcT[:, m, 2 * hd + c, :], qT[:, 2 * hd + c, b * DS:(b + 1) * DS],
                                            start=c == 0, stop=c == 1)
                    ins.then_inc(S_("sT_done"), 1)
                pe.wait_ge(S_("sT"), 1)
                for gq in range(2):
                    for m in range(MT):
                        ins = pe.transpose(PS[:, 6, gq * NMEM + m * P:gq * NMEM + (m + 1) * P], sT[:, m, gq * P:(gq + 1) * P], ident[:])
                ins.then_inc(S_("scores"), 1)
                pe.wait_ge(S_("p_ready"), TILES)
                for gq in range(2):
                    for m in range(MT):
                        ins = pe.transpose(PS[:, 0, (gq * 2 + m) * P:(gq * 2 + m + 1) * P], p[:, gq, m * P:(m + 1) * P], ident[:])
                ins.then_inc(S_("pT_done"), 1)
                pe.wait_ge(S_("pT"), TILES)
                pT = sT[:].rearrange("p m n -> p (m n)")
                for b in range(DB):
                    slot = slot_of(DB + b)
                    pe.wait_ge(S_(f"slot{slot}"), 16 * uses(DB + b))
                    for cc in range(KC):
                        for m in range(MT):
                            at = (b // 4 * 2 + m) * P + b % 4 * 32 + cc // 2 * 8
                            ins = pe.matmul(PS[:, 4, cc * NS + b * DS:cc * NS + (b + 1) * DS], slots[slot][:, m, cc * P:(cc + 1) * P], pT[:, at:at + 8],
                                            start=m == 0, stop=m == MT - 1)
                ins.then_inc(S_("oT_done"), 1)

            @block.tensor
            def _(pe):
                pe_memory(pe)
                pe.wait_ge(S_("kT"), 4)
                p_turn_mixed(pe, 0)
                pe.wait_ge(S_("v_ready"), 4)
                p_output(pe, 0)
                p_turn_h(pe, 0)
                p_queries(pe, 0)
                p_turn_q(pe, 0)
                pe.wait_ge(S_("consts"), 16 * 6)
                with pe.Fori(0, NT) as i:
                    p_turn_mixed(pe, i + 1)
                    p_scores(pe, i)
                    p_output(pe, i + 1)
                    p_values(pe, i)
                    p_turn_h(pe, i + 1)
                    p_memory_output(pe, i)
                    p_queries(pe, i + 1)
                    p_turn_hn(pe, i)
                    p_turn_q(pe, i + 1)
                    p_router(pe, i)
                pe.wait_ge(S_("qT"), TILES)
                pe.wait_ge(S_("lg_ready"), TILES)
                p_attention_sample(pe)
                p_memory_output(pe, NT)
                p_turn_hn(pe, NT)
                p_router(pe, NT)


EXPERT_WEIGHTS = ("w_e_gate", "w_e_up", "w_e_down")


def expert_weights(d, name, n):
    return d[name][0][bass.ds(n, 1)].rearrange("a (c p) m -> p (a c) m", p=P)


def phase_route(core, PS, dest, comb, slot_tok, over_info, ew):
    nc, d, sem = core.nc, core.dram, core.sem
    S_ = lambda n: sem("rt_" + n)
    NR = NG + NE
    NCNT = 2 * NE + NOVER + EPG + 8
    with ExitStack() as ctx:
        sb = lambda n, s, t=F32: ctx.enter_context(nc.sbuf_tensor("rt_" + n, s, t))
        L, masks, ones, cnt_c = sb("L", [P, TILES, NR]), sb("strict", [P, P]), sb("ones", [P, P]), sb("cnt", [P, NCNT])
        valid, token, zero = sb("valid", [P, TILES]), sb("token", [P, TILES], I32), sb("zero", [P, NBLK], I32)
        s = sb("s", [P, 12, TILES])
        og, tg = sb("og", [P, TILES, NG]), sb("tg", [P, TILES, NG])
        sel, el, te = sb("sel", [P, TILES, EPG, NG]), sb("el", [P, TILES, EPG]), sb("te", [P, TILES, EPG])
        o1, o2 = sb("o1", [P, TILES, EPG]), sb("o2", [P, TILES, EPG])
        O = sb("O", [P, 2, TILES, NG, EPG])
        M, before = sb("M", [P, TILES, NE]), sb("before", [P, TILES + 1, NE])
        a, b = sb("a", [P, TILES, NE]), sb("b", [P, TILES, NE])
        e32 = sb("e32", [P, 8, NE])
        nbt = sb("nbt", [P, NE, 8])
        own, own2 = sb("own", [P, NOVER, NE]), sb("own2", [P, NOVER, NE])
        df, of = sb("df", [P, 2, TILES]), sb("of", [P, NOVER + 1])
        ebase, eid, ovn, desc, full = (cnt_c[:, 0:NE], cnt_c[:, NE:2 * NE], cnt_c[:, 2 * NE:2 * NE + NOVER],
                                       cnt_c[:, 2 * NE + NOVER:2 * NE + NOVER + EPG], cnt_c[:, 2 * NE + NOVER + EPG:])
        bc = lambda ap, *shape: ap.to_broadcast([P, *shape])
        with nc.Block() as block:
            @block.sync
            def _(sp):
                with nc.allow_non_contiguous_dma(reason="small"):
                    sp.dma_start(L[:], d["logits"].rearrange("(t p) n -> p t n", p=P)).then_inc(S_("in"), 16)
                for dst, src in ((masks[:], d["mask_p"][:, 3, :]), (cnt_c[:], d["count"]), (valid[:], d["valid"]), (token[:], d["token"])):
                    sp.dma_start(dst, src).then_inc(S_("in"), 16)
                for bf in range(2):
                    for dst, name in zip(ew, EXPERT_WEIGHTS):
                        sp.dma_start(dst[:, bf], expert_weights(d, name, bf)).then_inc(S_("weights"), 16)
                sp.wait_ge(S_("weights"), 96)

            @block.vector
            def _(v):
                lk = Steps(v, S_("dve"))
                tt, red = v.tensor_tensor, v.tensor_reduce
                v.memset(ones[:], 1.0).then_inc(S_("ones"), 1)
                v.wait_ge(S_("in"), 80)

                def pick(dst, src, best, t, n):
                    lk(red(best, src, AX.X, ALU.max))
                    lk(tt(t, src, bc(best.unsqueeze(2), TILES, n), ALU.is_equal))
                    lk(tt(t, t, bc(desc[:, 0:n].unsqueeze(1), TILES, n), ALU.mult))
                    lk(red(s[:, 11], t, AX.X, ALU.max))
                    lk(tt(dst, t, bc(s[:, 11].unsqueeze(2), TILES, n), ALU.is_equal))

                gl = L[:, :, 0:NG]
                pick(og[:], gl, s[:, 0], tg[:], NG)
                tt(tg[:], gl, bc(s[:, 0].unsqueeze(2), TILES, NG), ALU.subtract).then_inc(S_("g_shift"), 1)
                lk(tt(sel[:], L[:, :, NG:NR].rearrange("p t (g e) -> p t e g", g=NG), bc(og[:].unsqueeze(2), TILES, EPG, NG), ALU.mult))
                lk(red(el[:], sel[:], AX.X, ALU.add))
                pick(o1[:], el[:], s[:, 1], te[:], EPG)
                lk(v.scalar_tensor_tensor(el[:], o1[:], -1e30, el[:], ALU.mult, ALU.add))
                pick(o2[:], el[:], s[:, 2], te[:], EPG)
                tt(s[:, 3], s[:, 2], s[:, 1], ALU.subtract).then_inc(S_("e_shift"), 1)
                for k, o in enumerate((o1, o2)):
                    ins = tt(O[:, k], bc(og[:].unsqueeze(3), TILES, NG, EPG), bc(o[:].unsqueeze(2), TILES, NG, EPG), ALU.mult)
                lk(ins)
                O_ = lambda k: O[:, k].rearrange("p t g e -> p t (g e)")
                lk(tt(M[:], O_(0), O_(1), ALU.add))
                tt(M[:], M[:], bc(valid[:].unsqueeze(2), TILES, NE), ALU.mult).then_inc(S_("M_ready"), 1)
                v.memset(before[:, 0], 0.0)
                v.wait_ge(S_("M_ready"), 1)
                lk(v.tensor_copy(before[:, 1], M[:, 0]))
                for t in range(1, TILES):
                    lk(tt(before[:, t + 1], before[:, t], M[:, t], ALU.add))
                v.sem_inc(S_("before_ready"), 1)
                v.wait_ge(S_("exps"), 1)
                lk(red(s[:, 5], tg[:], AX.X, ALU.add))
                lk(v.tensor_scalar(s[:, 6], s[:, 4], 1.0, None, ALU.add))
                lk(tt(s[:, 6], s[:, 6], s[:, 5], ALU.mult))
                lk(v.reciprocal(comb[:, 0], s[:, 6]))
                lk(tt(comb[:, 1], comb[:, 0], s[:, 4], ALU.mult))
                v.wait_ge(S_("ranks"), 1)
                cnt, nb, c0, c1, start, corr = (e32[:, j] for j in range(6))
                lk(v.tensor_copy(cnt, PS[:, 1, 0:NE]))
                lk(v.tensor_copy(b[:].rearrange("p t e -> p (t e)"), PS[:, 0, 0:TILES * NE]))
                lk(tt(nbt[:], bc(cnt.unsqueeze(2), NE, 8), bc(full.unsqueeze(1), NE, 8), ALU.is_gt))
                lk(red(nb, nbt[:], AX.X, ALU.add))
                lk(v.tensor_copy(c0, nb))
                step = 1
                while step < NE:
                    v.tensor_copy(c1[:, 0:step], c0[:, 0:step])
                    lk(tt(c1[:, step:NE], c0[:, step:NE], c0[:, 0:NE - step], ALU.add))
                    c0, c1, step = c1, c0, 2 * step
                lk(tt(start, c0, nb, ALU.subtract))
                lk(v.tensor_scalar(corr, start, float(CAP), float(NE * CAP - CAP), ALU.mult, ALU.add))
                lk(tt(corr, corr, ebase, ALU.subtract))
                lk(v.tensor_scalar(a[:], b[:], float(CAP), None, ALU.is_ge))
                lk(tt(a[:], a[:], bc(corr.unsqueeze(1), TILES, NE), ALU.mult))
                lk(tt(a[:], a[:], b[:], ALU.add))
                lk(tt(a[:], a[:], bc(ebase.unsqueeze(1), TILES, NE), ALU.add))
                for k in range(2):
                    lk(tt(b[:], a[:], O_(k), ALU.mult))
                    lk(red(df[:, k], b[:], AX.X, ALU.add))
                v.tensor_copy(dest[:], df[:]).then_inc(S_("dest"), 1)
                lk(tt(own[:], bc(start.unsqueeze(1), NOVER, NE), bc(ovn.unsqueeze(2), NOVER, NE), ALU.is_le))
                lk(tt(own2[:], bc(c0.unsqueeze(1), NOVER, NE), bc(ovn.unsqueeze(2), NOVER, NE), ALU.is_gt))
                lk(tt(own[:], own[:], own2[:], ALU.mult))
                lk(tt(own[:], own[:], bc(eid.unsqueeze(1), NOVER, NE), ALU.mult))
                lk(red(of[:, 0:NOVER], own[:], AX.X, ALU.add))
                lk(v.tensor_copy(of[:, NOVER:NOVER + 1], c0[:, NE - 1:NE]))
                lk(v.tensor_copy(over_info[:], of[:]))

            @block.scalar
            def _(act):
                act.wait_ge(S_("g_shift"), 1)
                act.activation(tg[:], tg[:], ACT.Exp)
                act.wait_ge(S_("e_shift"), 1)
                act.activation(s[:, 4], s[:, 3], ACT.Exp).then_inc(S_("exps"), 1)

            @block.tensor
            def _(pe):
                pe.wait_ge(S_("ones"), 1)
                pe.wait_ge(S_("M_ready"), 1)
                pe.matmul(PS[:, 0, 0:TILES * NE], masks[:], M[:].rearrange("p t e -> p (t e)"), start=True, stop=False)
                pe.wait_ge(S_("before_ready"), 1)
                pe.matmul(PS[:, 0, 0:TILES * NE], ones[:], before[:, 0:TILES].rearrange("p t e -> p (t e)"), start=False, stop=True)
                pe.matmul(PS[:, 1, 0:NE], ones[:], before[:, TILES], start=True, stop=True).then_inc(S_("ranks"), 1)

            @block.gpsimd
            def _(po):
                po.memset(zero[:], 0).then_inc(S_("zero"), 1)
                po.wait_ge(S_("zero"), 1)
                po.dma_start(d["slots"].rearrange("(p n) o -> p (n o)", p=P), zero[:]).then_inc(S_("slots_zero"), 16)
                po.wait_ge(S_("slots_zero"), 16)
                po.wait_ge(S_("in"), 80)
                po.wait_ge(S_("dest"), 1)
                n = 0
                for k in range(2):
                    for t in range(TILES):
                        rows = P if t < NT else NS
                        po.indirect_dma_start(d["slots"], bass.IndirectOffsetOnAxis(ap=dest[0:rows, k, t:t + 1], axis=0),
                                              token[0:rows, t:t + 1], None).then_inc(S_("scattered"), 16)
                        n += 16
                po.wait_ge(S_("scattered"), n)
                with nc.allow_non_contiguous_dma(reason="a table turned"):
                    po.dma_start(slot_tok[:], d["slots"].rearrange("(b p) o -> p (b o)", p=P)).then_inc(S_("slots_in"), 16)
                po.wait_ge(S_("slots_in"), 16)


def phase_experts(core, PS, slot_tok, over_info, ew, h2):
    nc, d, sem = core.nc, core.dram, core.sem
    S_ = lambda n: sem("ex_" + n)
    HC = DE // P
    with ExitStack() as ctx:
        sb = lambda n, s, t=F32: ctx.enter_context(nc.sbuf_tensor("ex_" + n, s, t))
        wg, wu, wd = ew
        xg, xT = sb("xg", [P, 2, D]), sb("xT", [P, 2, KC, P])
        idx = sb("idx", [P, 2], I32)
        e, h, hT, y = sb("e", [P, 2, DE]), sb("h", [P, 2, DE]), sb("hT", [P, HC, P]), sb("y", [P, 2, D])
        ident = sb("ident", [P, P])
        GATE, UP, HT, OUT = 2, 3, 4, 5

        weights = lambda n, name: expert_weights(d, name, n)

        def over_blocks(eng, body):
            n_over = eng.value_load(over_info[0:1, NOVER:NOVER + 1], min_val=0, max_val=NOVER)
            with eng.Fori(0, NOVER) as j:
                with eng.If(j < n_over):
                    body(j)

        def gate_up(pe, bf):
            for bank, w in ((GATE, wg), (UP, wu)):
                for k in range(KC):
                    ins = pe.matmul(PS[:, bank, :], xT[:, bf, k, :], w[:, bf, k, :], start=k == 0, stop=k == KC - 1)
            return ins

        def down(pe, bf):
            for hf in range(2):
                for k in range(HC):
                    ins = pe.matmul(PS[:, OUT + hf, :], hT[:, k, :], wd[:, bf, k, hf * 512:hf * 512 + 512], start=k == 0, stop=k == HC - 1)
            return ins

        def turn_rows(pe, bf):
            for c in range(KC):
                ins = pe.transpose(PS[:, c // 4, c % 4 * P:c % 4 * P + P], xg[:, bf, c * P:(c + 1) * P], ident[:])
            return ins

        def turn_h(pe, bf):
            for c in range(HC):
                ins = pe.transpose(PS[:, HT, c * P:(c + 1) * P], h[:, bf, c * P:(c + 1) * P], ident[:])
            return ins

        def silu_up(v, bf, lk):
            lk(v.tensor_scalar(e[:, bf], e[:, bf], 1.0, None, ALU.add))
            lk(v.reciprocal(e[:, bf], e[:, bf]))
            lk(v.tensor_tensor(e[:, bf], e[:, bf], PS[:, GATE, :], ALU.mult))
            return v.tensor_tensor(h[:, bf], e[:, bf], PS[:, UP, :], ALU.mult)

        rows_out = lambda: PS[:, OUT:OUT + 2, :].rearrange("p a n -> p (a n)")
        rows_in = lambda: PS[:, 0:2, :].rearrange("p a (c t) -> p (a c) t", t=P)

        with nc.Block() as block:
            @block.sync
            def _(sp):
                sp.dma_start(ident[:], d["ident"]).then_inc(S_("ident"), 16)

                for bf in range(2):
                    for n in ("wg", "wu", "wd"):
                        sp.sem_inc(S_(f"{n}{bf}"), 16)

                def load(it, bf, n):
                    sp.wait_ge(S_(f"gu_used{bf}"), it)
                    sp.dma_start(wg[:, bf], weights(n, "w_e_gate")).then_inc(S_(f"wg{bf}"), 16)
                    sp.dma_start(wu[:, bf], weights(n, "w_e_up")).then_inc(S_(f"wu{bf}"), 16)
                    sp.wait_ge(S_(f"d_used{bf}"), it)
                    sp.dma_start(wd[:, bf], weights(n, "w_e_down")).then_inc(S_(f"wd{bf}"), 16)

                with sp.Fori(1, NE // 2) as it:
                    load(it, 0, 2 * it)
                    load(it, 1, 2 * it + 1)
                sp.dma_start(h2[:], d["h2"].rearrange("(t p) n -> p t n", p=P)).then_inc(S_("h2"), 16)
                sp.wait_ge(S_("h2"), 16)
                sp.wait_ge(S_("gu_used0"), NE // 2)
                sp.wait_ge(S_("d_used0"), NE // 2)

                def over(j):
                    n = sp.value_load(over_info[0:1, bass.ds(j, 1)], min_val=0, max_val=NE - 1)
                    sp.wait_ge(S_("ov_d"), j)
                    for dst, name in ((wg[:, 0], "w_e_gate"), (wu[:, 0], "w_e_up"), (wd[:, 0], "w_e_down")):
                        sp.dma_start(dst, weights(n, name)).then_inc(S_("ov_w"), 16)
                over_blocks(sp, over)

            @block.gpsimd
            def _(po):
                def gather(n, bf):
                    po.tensor_copy(idx[:, bf:bf + 1], slot_tok[:, bass.ds(n, 1)]).then_inc(S_("idx"), 1)
                    po.wait_ge(S_("idx"), n + 1)
                    po.sem_inc(S_("passed"), 1)
                    po.indirect_dma_start(xg[:, bf], None, d["hn"], bass.IndirectOffsetOnAxis(ap=idx[:, bf:bf + 1], axis=0)).then_inc(S_(f"rows{bf}"), 16)

                with po.Fori(0, NE // 2) as it:
                    for bf in range(2):
                        po.wait_ge(S_(f"rows_used{bf}"), it)
                        gather(2 * it + bf, bf)
                po.wait_ge(S_("rows_used0"), NE // 2)
                po.wait_ge(S_("rows0"), 16 * (NE // 2))

                def over(j):
                    po.wait_ge(S_("ov_turned"), j)
                    po.tensor_copy(idx[:, 0:1], slot_tok[:, bass.ds(j + NE, 1)]).then_inc(S_("ov_idx"), 1)
                    po.wait_ge(S_("ov_idx"), j + 1)
                    po.sem_inc(S_("passed"), 1)
                    po.indirect_dma_start(xg[:, 0], None, d["hn"], bass.IndirectOffsetOnAxis(ap=idx[:, 0:1], axis=0)).then_inc(S_("ov_rows"), 16)
                over_blocks(po, over)

            @block.tensor
            def _(pe):
                pe.wait_ge(S_("ident"), 16)

                def T(n, it, bf):
                    pe.wait_ge(S_(f"rows{bf}"), 16 * it + 16)
                    turn_rows(pe, bf).then_inc(S_(f"rows_used{bf}"), 1)

                def GU(n, it, bf):
                    pe.wait_ge(S_("xT"), n + 1)
                    pe.wait_ge(S_(f"wg{bf}"), 16 * it + 16)
                    pe.wait_ge(S_(f"wu{bf}"), 16 * it + 16)
                    pe.wait_ge(S_("h"), n)
                    gate_up(pe, bf).then_inc(S_(f"gu_used{bf}"), 1)

                def HT_(n, bf):
                    pe.wait_ge(S_("h"), n + 1)
                    turn_h(pe, bf).then_inc(S_("h_turned"), 1)

                def DN(n, it, bf):
                    pe.wait_ge(S_("hT"), n + 1)
                    pe.wait_ge(S_(f"wd{bf}"), 16 * it + 16)
                    pe.wait_ge(S_("y"), n)
                    down(pe, bf).then_inc(S_(f"d_used{bf}"), 1)

                T(0, 0, 0)
                GU(0, 0, 0)
                T(1, 0, 1)
                with pe.Fori(0, NE // 2 - 1) as it:
                    n = 2 * it + 1
                    GU(n, it, 1)
                    HT_(n - 1, 0)
                    T(n + 1, it + 1, 0)
                    DN(n - 1, it, 0)
                    GU(n + 1, it + 1, 0)
                    HT_(n, 1)
                    T(n + 2, it + 1, 1)
                    DN(n, it, 1)
                L = NE - 1
                GU(L, NE // 2 - 1, 1)
                HT_(L - 1, 0)
                DN(L - 1, NE // 2 - 1, 0)
                HT_(L, 1)
                DN(L, NE // 2 - 1, 1)

                def over(j):
                    pe.wait_ge(S_("ov_rows"), 16 * j + 16)
                    pe.wait_ge(S_("ov_h"), j)
                    turn_rows(pe, 0).then_inc(S_("ov_turned"), 1)
                    pe.wait_ge(S_("ov_xT"), j + 1)
                    pe.wait_ge(S_("ov_w"), 48 * j + 48)
                    gate_up(pe, 0).then_inc(S_("ov_gu"), 1)
                    pe.wait_ge(S_("ov_h"), j + 1)
                    turn_h(pe, 0).then_inc(S_("ov_ht"), 1)
                    pe.wait_ge(S_("ov_hT"), j + 1)
                    pe.wait_ge(S_("ov_y"), j)
                    down(pe, 0).then_inc(S_("ov_d"), 1)
                pe.wait_ge(S_("y"), NE)
                over_blocks(pe, over)

            @block.vector
            def _(v):
                def block_h(n, it, bf, lk):
                    v.wait_ge(S_("exp"), n + 1)
                    silu_up(v, bf, lk).then_inc(S_("h"), 1)

                def block_hT(n):
                    v.wait_ge(S_("h_turned"), n + 1)
                    v.tensor_copy(hT[:].rearrange("p c t -> p (c t)"), PS[:, HT, :]).then_inc(S_("hT"), 1)

                block_h(0, 0, 0, Steps(v, S_("dve"), 0))
                with v.Fori(0, NE // 2 - 1) as it:
                    n = 2 * it + 1
                    lk = Steps(v, S_("dve"), 6 * it + 3)
                    block_hT(n - 1)
                    block_h(n, it, 1, lk)
                    v.wait_ge(S_("d_used0"), it + 1)
                    block_hT(n)
                    block_h(n + 1, it + 1, 0, lk)
                    v.wait_ge(S_("d_used1"), it + 1)
                lk = Steps(v, S_("dve"), 6 * (NE // 2 - 1) + 3)
                block_hT(NE - 2)
                block_h(NE - 1, 0, 1, lk)
                v.wait_ge(S_("d_used0"), NE // 2)
                block_hT(NE - 1)

                def over(j):
                    lk = Steps(v, S_("ov_dve"), 3 * j)
                    v.wait_ge(S_("ov_exp"), j + 1)
                    silu_up(v, 0, lk).then_inc(S_("ov_h"), 1)
                    v.wait_ge(S_("ov_ht"), j + 1)
                    v.wait_ge(S_("ov_d"), j)
                    v.tensor_copy(hT[:].rearrange("p c t -> p (c t)"), PS[:, HT, :]).then_inc(S_("ov_hT"), 1)
                over_blocks(v, over)

            @block.scalar
            def _(act):
                def X(n, it, bf):
                    act.wait_ge(S_(f"rows_used{bf}"), it + 1)
                    act.copy(xT[:, bf], rows_in()).then_inc(S_("xT"), 1)

                def E(it, bf):
                    act.wait_ge(S_(f"gu_used{bf}"), it + 1)
                    act.activation(e[:, bf], PS[:, GATE, :], ACT.Exp, scale=-1.0).then_inc(S_("exp"), 1)

                def Y(n, it, bf):
                    act.wait_ge(S_(f"d_used{bf}"), it + 1)
                    act.wait_ge(S_(f"y_stored{bf}"), 16 * it)
                    act.copy(y[:, bf], rows_out()).then_inc(S_("y"), 1)
                    act.wait_ge(S_("y"), n + 1)
                    act.dma_start(d["blocks"][bass.ds(n * P, P), :], y[:, bf]).then_inc(S_(f"y_stored{bf}"), 16)

                X(0, 0, 0)
                E(0, 0)
                X(1, 0, 1)
                with act.Fori(0, NE // 2 - 1) as it:
                    n = 2 * it + 1
                    E(it, 1)
                    X(n + 1, it + 1, 0)
                    Y(n - 1, it, 0)
                    E(it + 1, 0)
                    X(n + 2, it + 1, 1)
                    Y(n, it, 1)
                E(NE // 2 - 1, 1)
                Y(NE - 2, NE // 2 - 1, 0)
                Y(NE - 1, NE // 2 - 1, 1)
                act.wait_ge(S_("y_stored0"), 16 * (NE // 2))
                act.wait_ge(S_("y_stored1"), 16 * (NE // 2))

                def over(j):
                    act.wait_ge(S_("ov_turned"), j + 1)
                    act.copy(xT[:, 0], rows_in()).then_inc(S_("ov_xT"), 1)
                    act.wait_ge(S_("ov_gu"), j + 1)
                    act.activation(e[:, 0], PS[:, GATE, :], ACT.Exp, scale=-1.0).then_inc(S_("ov_exp"), 1)
                    act.wait_ge(S_("ov_d"), j + 1)
                    act.copy(y[:, 0], rows_out()).then_inc(S_("ov_y"), 1)
                    act.wait_ge(S_("ov_y"), j + 1)
                    act.dma_start(d["blocks"][bass.ds(j * P + NE * P, P), :], y[:, 0]).then_inc(S_("ov_stored"), 16)
                    act.wait_ge(S_("ov_stored"), 16 * j + 16)
                    act.sem_inc(S_("ov_finished"), 1)
                over_blocks(act, over)


def phase_combine(core, PS, dest, comb, h):
    nc, d, sem = core.nc, core.dram, core.sem
    S_ = lambda n: sem("cb_" + n)
    with ExitStack() as ctx:
        sb = lambda n, s, t=F32: ctx.enter_context(nc.sbuf_tensor("cb_" + n, s, t))
        y1, y2, o = sb("y1", [P, TILES, D]), sb("y2", [P, TILES, D]), sb("o", [P, 2, D])
        gf, expo, st = sb("gf", [P, D]), sb("expo", [P, 1]), sb("st", [P, TILES, 4])
        rows = [P if t < NT else NS for t in range(TILES)]
        with nc.Block() as block:
            @block.sync
            def _(sp):
                sp.dma_start(gf[:], wide_row(d["g_final"], D)).then_inc(S_("g"), 16)
                for t in range(TILES):
                    sp.wait_ge(S_("out"), t + 1)
                    dst = d["y_p"][t * P:(t + 1) * P, :] if t < NT else d["y_s"]
                    sp.dma_start(dst, o[0:rows[t], t % 2]).then_inc(S_(f"stored{t % 2}"), 16)
                sp.wait_ge(S_("stored0"), 16 * 5)
                sp.wait_ge(S_("stored1"), 16 * 4)

            @block.gpsimd
            def _(po):
                po.memset(expo[:], -0.5).then_inc(S_("expo"), 1)
                po.wait_ge(S_("expo"), 1)
                for t in range(TILES):
                    for k, y in enumerate((y1, y2)):
                        po.indirect_dma_start(y[0:rows[t], t], None, d["blocks"],
                                              bass.IndirectOffsetOnAxis(ap=dest[0:rows[t], k, t:t + 1], axis=0)).then_inc(S_(f"y{t}"), 16)
                for t in range(TILES):
                    po.wait_ge(S_("ms"), t + 1)
                    po.tensor_tensor(st[:, t, 2:3], st[:, t, 1:2], expo[:], ALU.pow).then_inc(S_("rstd"), 1)

            @block.vector
            def _(v):
                lk = Steps(v, S_("dve"))
                v.wait_ge(S_("g"), 16)

                def add(t):
                    r = slice(0, rows[t])
                    v.wait_ge(S_(f"y{t}"), 32)
                    lk(v.scalar_tensor_tensor(h[r, t], y1[r, t], comb[r, 0, t:t + 1], h[r, t], ALU.mult, ALU.add))
                    v.scalar_tensor_tensor(h[r, t], y2[r, t], comb[r, 1, t:t + 1], h[r, t], ALU.mult, ALU.add).then_inc(S_("added"), 1)

                def mean_square(t):
                    v.wait_ge(S_("squares"), t + 1)
                    v.tensor_scalar(st[:, t, 1:2], st[:, t, 0:1], 1.0 / D, EPS, ALU.mult, ALU.add).then_inc(S_("ms"), 1)

                def gain(t):
                    r = slice(0, rows[t])
                    v.wait_ge(S_("normed"), t + 1)
                    v.tensor_tensor(o[r, t % 2], o[r, t % 2], gf[r], ALU.mult).then_inc(S_("out"), 1)

                for t in range(TILES):
                    add(t)
                    if t >= 1:
                        mean_square(t - 1)
                    if t >= 2:
                        gain(t - 2)
                mean_square(TILES - 1)
                gain(TILES - 2)
                gain(TILES - 1)

            @block.scalar
            def _(act):
                def normed(t):
                    r = slice(0, rows[t])
                    act.wait_ge(S_("rstd"), t + 1)
                    if t >= 2:
                        act.wait_ge(S_(f"stored{t % 2}"), 16 * (t // 2))
                    act.activation(o[r, t % 2], h[r, t], ACT.Copy, scale=st[r, t, 2:3]).then_inc(S_("normed"), 1)

                for t in range(TILES):
                    act.wait_ge(S_("added"), t + 1)
                    act.activation(y1[:, t], h[:, t], ACT.Square, accum_out=st[:, t, 0:1]).then_inc(S_("squares"), 1)
                    if t >= 1:
                        normed(t - 1)
                normed(TILES - 1)


def build(nc, dram):
    with ExitStack() as ctx:
        core = Core(nc, ctx, dram)
        PS = ctx.enter_context(nc.psum_tensor("banks", [P, 8, 512], F32))
        phase_project(core, PS)
        core.end_phase()
        phase_mixers(core, PS)
        core.end_phase()
        phase_attention(core, PS)
        core.end_phase()
        sb = lambda n, s, t: ctx.enter_context(nc.sbuf_tensor("moe_" + n, s, t))
        dest, comb = sb("dest", [P, 2, TILES], I32), sb("comb", [P, 2, TILES], F32)
        slot_tok, over_info = sb("slot_tok", [P, NBLK], I32), sb("over_info", [P, NOVER + 1], I32)
        h2 = sb("h2", [P, TILES, D], F32)
        with ExitStack() as experts:
            ew = [experts.enter_context(nc.sbuf_tensor("moe_" + n, [P, 2, rows // P, cols], F32))
                  for n, rows, cols in (("gate", D, DE), ("up", D, DE), ("down", DE, D))]
            phase_route(core, PS, dest, comb, slot_tok, over_info, ew)
            core.end_phase()
            phase_experts(core, PS, slot_tok, over_info, ew, h2)
            core.end_phase()
        phase_combine(core, PS, dest, comb, h2)


SCRATCH = {"proj": ((ROWS + 8, NIN), F32), "mixed": ((ROWS, D), F32), "h2": ((ROWS, D), F32),
           "hn": ((ROWS, D), F32), "logits": ((ROWS, NG + NE), F32),
           "slots": ((NBLK * P, 1), I32), "blocks": ((NBLK * P, D), F32)}

INPUTS = ["w_in", "g_mix"]
OUTPUTS = [
    ("y_p", (SEQ, D)), ("y_s", (NS, D)),
    ("out_ret_p", (RH, RDK, RDV)), ("out_rwkv_p", (WH, WN, WN)), ("out_shift_p", (1, NRW)),
    ("out_ret_s", (DB, RH, RDK, RDV)), ("out_rwkv_s", (DB, WH, WN, WN)), ("out_shift_s", (DB, NRW)),
    ("out_mk", (NMEM, D)), ("out_mv", (NMEM, D)),
]


def program(nc, shapes):
    dram = {n: nc.dram_tensor(n, s, t, kind="ExternalInput").ap() for n, (s, t) in shapes.items()}
    for n, (s, t) in SCRATCH.items():
        dram[n] = nc.dram_tensor(n, s, t).ap()
    for n, s in OUTPUTS:
        dram[n] = nc.dram_tensor(n, s, F32, kind="ExternalOutput").ap()
    build(nc, dram)


def arrays_of(inputs):
    a = {k: np.ascontiguousarray(v) for k, v in inputs.items() if k not in ("x_prompt", "x_sample")}
    x = np.zeros((ROWS + P, D), np.float32)
    x[:SEQ] = inputs["x_prompt"][0]
    x[SEQ:SEQ + NS] = np.asarray(inputs["x_sample"]).reshape(NS, D)
    a["x"] = x
    a["zero_row"] = np.zeros((1, NRW), np.float32)
    a.update(shape_constants())
    return a


def kernel(**inputs):
    import concourse.bacc as bacc
    from concourse.bass_utils import run_bass_kernel_spmd

    arrays = arrays_of(inputs)
    nc = bacc.Bacc("TRN2", target_bir_lowering=False, num_devices=1)
    program(nc, {n: (a.shape, mybir.dt.from_np(a.dtype)) for n, a in arrays.items()})
    r = run_bass_kernel_spmd(nc, [arrays], core_ids=[0])
    got = r.results[0]
    order = [("y_p", (1, SEQ, D)), ("y_s", (DB, DS, D)), ("out_ret_p", (1, 1, RH, RDK, RDV)), ("out_rwkv_p", (1, 1, WH, WN, WN)),
             ("out_shift_p", (1, 1, NRW)), ("out_mk", (1, 1, NMEM, MH, MDH)), ("out_mv", (1, 1, NMEM, MH, MDH)),
             ("out_ret_s", (1, DB, RH, RDK, RDV)), ("out_rwkv_s", (1, DB, WH, WN, WN)), ("out_shift_s", (1, DB, NRW))]
    return tuple(got[n].reshape(s) for n, s in order)
```
